# Optimizing a Trainium2 kernel written in Bass

```python
import math
import jax, jax.numpy as jnp
from jax import lax
import numpy as np

D_MODEL = 1024
BATCH = 1
SEQ = 512
DEPTH = 2
DEC_BATCH = 8
DEC_SEQ = 4
PAST_LEN = 4096
PAGE_SIZE = 128

N_EVEN = (DEPTH + 1) // 2
N_ODD = DEPTH // 2
N_VMIX = max(N_ODD - 1, 0)
MIX_A = D_MODEL // 2
H_A = 4
DV_A = MIX_A // H_A
DK_A = DV_A // 2
KA_DIM = H_A * DK_A
GK_RANK = 16
GK_NORM = 16.0
MIX_B = D_MODEL - MIX_A
H_B = 4
DV_B = MIX_B // H_B
N_B = 128
KB_DIM = H_B * N_B
SPLIT_SIZES = (KA_DIM, KA_DIM, MIX_A, MIX_A, GK_RANK, KB_DIM, KB_DIM, MIX_B, MIX_B)
IN_EVEN = sum(SPLIT_SIZES)
CHUNK = 64
LB_FLOOR = 1e-20
N_C = 64
H_C = D_MODEL // N_C
D_DECAY_LORA = 64
D_AAA_LORA = 64
D_MV_LORA = 32
D_GATE_LORA = 128
FFN_DIM = -(-8 * D_MODEL // (3 * 256)) * 256
PLE_DIM = 256
RMS_EPS = 1e-6
GN_EPS = 64e-5

kernel_name = 'gla_hgrn2_rwkv7_hybrid_step'

def rmsnorm(x, g, eps=RMS_EPS):
    xf = x.astype(jnp.float32)
    y = xf * lax.rsqrt(jnp.mean(xf * xf, axis=-1, keepdims=True) + eps)
    return (y * g.astype(jnp.float32)).astype(x.dtype)

def chunk_gated_linear(q, k, v, log_g, s0):
    f32 = jnp.float32
    bsz, t_len, n_h, _ = q.shape
    d_v = v.shape[-1]
    c = math.gcd(t_len, CHUNK)
    n_chunks = t_len // c

    def to_chunks(z):
        return z.astype(f32).reshape(bsz, n_chunks, c, n_h, z.shape[-1]).transpose(1, 0, 3, 2, 4)

    causal = jnp.tril(jnp.ones((c, c), dtype=bool))[:, :, None]

    def step(s, inp):
        qi, ki, vi, gi = inp
        b = jnp.cumsum(gi, axis=2)
        diff = b[:, :, :, None, :] - b[:, :, None, :, :]
        decay = jnp.where(causal, jnp.exp(jnp.minimum(diff, 0.0)), 0.0)
        scores = jnp.einsum('bhtc,bhsc,bhtsc->bhts', qi, ki, decay)
        o = (jnp.einsum('bhts,bhsv->bhtv', scores, vi)
             + jnp.einsum('bhtc,bhcv->bhtv', qi * jnp.exp(b), s))
        b_last = b[:, :, -1:, :]
        s_new = (jnp.exp(b_last[:, :, 0, :])[..., None] * s
                 + jnp.einsum('bhsc,bhsv->bhcv', ki * jnp.exp(b_last - b), vi))
        return s_new, o

    s_fin, o = lax.scan(step, s0.astype(f32),
                        (to_chunks(q), to_chunks(k), to_chunks(v), to_chunks(log_g)))
    o = o.transpose(1, 0, 3, 2, 4).reshape(bsz, t_len, n_h, d_v)
    return o, s_fin

def rwkv7_recurrence(r, log_w, k, v, kk, a, s0):
    f32 = jnp.float32

    def to_time(z):
        return jnp.moveaxis(z.astype(f32), 1, 0)

    def step(s, inp):
        r_t, lw_t, k_t, v_t, kk_t, a_t = inp
        s_kk = jnp.einsum('bhik,bhk->bhi', s, kk_t)
        s = (s * jnp.exp(lw_t)[:, :, None, :]
             - s_kk[..., :, None] * (kk_t * a_t)[..., None, :]
             + v_t[..., :, None] * k_t[..., None, :])
        return s, jnp.einsum('bhij,bhj->bhi', s, r_t)

    s_fin, o = lax.scan(step, s0.astype(f32),
                        (to_time(r), to_time(log_w), to_time(k), to_time(v), to_time(kk), to_time(a)))
    return jnp.moveaxis(o, 0, 1), s_fin

def gla_hgrn_mixer(xn, s_gla, s_hgrn, lb, w_in, w_gk2, b_gk, gla_norm, hgrn_norm, w_out):
    f32 = jnp.float32
    bsz, t_len, _ = xn.shape
    u = xn @ w_in
    cuts = [int(c) for c in np.cumsum(SPLIT_SIZES)[:-1]]
    q_a, k_a, v_a, g_a, gk_lr, q_b, f_b, i_b, g_b = jnp.split(u, cuts, axis=-1)

    def heads(z, n_h):
        return z.reshape(bsz, t_len, n_h, -1)

    log_alpha = jax.nn.log_sigmoid((gk_lr @ w_gk2 + b_gk).astype(f32)) / GK_NORM
    o_a, s_gla_new = chunk_gated_linear(heads(q_a, H_A) * DK_A ** -0.5, heads(k_a, H_A),
                                        heads(v_a, H_A), heads(log_alpha, H_A), s_gla)
    o_a = rmsnorm(o_a, gla_norm).reshape(bsz, t_len, MIX_A).astype(xn.dtype) * jax.nn.silu(g_a)
    z = f_b.astype(f32)
    log_f = jnp.logaddexp(jnp.log(jnp.maximum(lb, LB_FLOOR)), jnp.log1p(-lb) + jax.nn.log_sigmoid(z))
    k_b = (1.0 - lb) * jax.nn.sigmoid(-z)
    o_b, s_hgrn_new = chunk_gated_linear(heads(jax.nn.silu(q_b), H_B) * N_B ** -0.5, heads(k_b, H_B),
                                         heads(i_b, H_B), heads(log_f, H_B), s_hgrn)
    o_b = rmsnorm(o_b, hgrn_norm).reshape(bsz, t_len, MIX_B).astype(xn.dtype) * jax.nn.silu(g_b)
    return jnp.concatenate([o_a, o_b], axis=-1) @ w_out, s_gla_new, s_hgrn_new

def rwkv7_mixer(xn, s_wkv, x_last, v_first, mu, w_r, w_k, w_v, w_o, w0, w1, w2,
                a0, a1, a2, vmix, g1, g2, k_k, k_a, r_k, ln_w, ln_b):
    f32 = jnp.float32
    bsz, t_len, _ = xn.shape
    x_prev = jnp.concatenate([x_last[:, None, :].astype(xn.dtype), xn[:, :-1]], axis=1)
    xmix = xn[:, :, None, :] + (x_prev - xn)[:, :, None, :] * mu
    xr, xw, xk, xv, xa, xg = [xmix[:, :, m] for m in range(6)]
    r = xr @ w_r
    k = xk @ w_k
    v = xv @ w_v
    log_w = -jnp.exp(-jax.nn.softplus(-(w0 + jnp.tanh(xw @ w1) @ w2).astype(f32)) - 0.5)
    a = jax.nn.sigmoid((a0 + (xa @ a1) @ a2).astype(f32))
    g = jax.nn.sigmoid(xg @ g1) @ g2
    kk = (k * k_k).astype(f32).reshape(bsz, t_len, H_C, N_C)
    kk = kk * lax.rsqrt(jnp.maximum(jnp.sum(kk * kk, axis=-1, keepdims=True), 1e-24))
    k = k.astype(f32) * (1.0 + (a - 1.0) * k_a)
    if vmix is None:
        v_first = v
    else:
        v0, v1, v2 = vmix
        v = v + (v_first - v) * jax.nn.sigmoid(v0 + (xv @ v1) @ v2)

    def heads(z):
        return z.astype(f32).reshape(bsz, t_len, H_C, N_C)

    o, s_new = rwkv7_recurrence(heads(r), heads(log_w), heads(k), heads(v), kk, heads(a), s_wkv)
    mean = jnp.mean(o, axis=-1, keepdims=True)
    var = jnp.mean(jnp.square(o - mean), axis=-1, keepdims=True)
    on = ((o - mean) * lax.rsqrt(var + GN_EPS)).reshape(bsz, t_len, D_MODEL) * ln_w + ln_b
    bonus = jnp.sum(heads(r) * heads(k) * r_k, axis=-1, keepdims=True) * heads(v)
    on = on + bonus.reshape(bsz, t_len, D_MODEL)
    return (on.astype(xn.dtype) * g) @ w_o, s_new, xn[:, -1], v_first

def swiglu(x, w_gate, w_up, w_down):
    return (jax.nn.silu(x @ w_gate) * (x @ w_up)) @ w_down

def setup_inputs(seed: int = 0) -> dict:
    key = jax.random.key(seed)
    ks = iter(jax.random.split(key, 64))

    def nrm(shape, scale):
        return scale * jax.random.normal(next(ks), shape, jnp.float32)

    def uni(shape, lo, hi):
        return jax.random.uniform(next(ks), shape, jnp.float32, lo, hi)

    sd = D_MODEL ** -0.5
    return {
        'x_prompt': nrm((BATCH, SEQ, D_MODEL), 1.0),
        'x_sample': nrm((DEC_BATCH, DEC_SEQ, D_MODEL), 1.0),
        'p_prompt': nrm((DEPTH, BATCH, SEQ, PLE_DIM), 1.0),
        'p_sample': nrm((DEPTH, DEC_BATCH, DEC_SEQ, PLE_DIM), 1.0),
        'state_gla': nrm((N_EVEN, DEC_BATCH, H_A, DK_A, DV_A), 0.2),
        'state_hgrn': nrm((N_EVEN, DEC_BATCH, H_B, N_B, DV_B), 0.2),
        'state_rwkv': nrm((N_ODD, DEC_BATCH, H_C, N_C, N_C), 0.1),
        'state_shift': nrm((N_ODD, DEC_BATCH, D_MODEL), 1.0),
        'norm_mix': 1.0 + nrm((DEPTH, D_MODEL), 0.05),
        'norm_ffn': 1.0 + nrm((DEPTH, D_MODEL), 0.05),
        'norm_ple': 1.0 + nrm((DEPTH, D_MODEL), 0.05),
        'norm_final': 1.0 + nrm((D_MODEL,), 0.05),
        'w_in_even': nrm((N_EVEN, D_MODEL, IN_EVEN), sd),
        'w_gk2': nrm((N_EVEN, GK_RANK, KA_DIM), GK_RANK ** -0.5),
        'b_gk': nrm((N_EVEN, KA_DIM), 0.1),
        'gla_norm': 1.0 + nrm((N_EVEN, DV_A), 0.05),
        'hgrn_gamma': nrm((N_EVEN, KB_DIM), 1.0),
        'hgrn_norm': 1.0 + nrm((N_EVEN, DV_B), 0.05),
        'w_out_even': nrm((N_EVEN, MIX_A + MIX_B, D_MODEL), sd),
        'rw_mu': uni((N_ODD, 6, D_MODEL), 0.0, 1.0),
        'rw_wr': nrm((N_ODD, D_MODEL, D_MODEL), sd),
        'rw_wk': nrm((N_ODD, D_MODEL, D_MODEL), sd),
        'rw_wv': nrm((N_ODD, D_MODEL, D_MODEL), sd),
        'rw_wo': nrm((N_ODD, D_MODEL, D_MODEL), sd),
        'rw_w0': uni((N_ODD, D_MODEL), -3.0, -0.5),
        'rw_w1': nrm((N_ODD, D_MODEL, D_DECAY_LORA), sd),
        'rw_w2': nrm((N_ODD, D_DECAY_LORA, D_MODEL), 0.1 * D_DECAY_LORA ** -0.5),
        'rw_a0': nrm((N_ODD, D_MODEL), 0.1),
        'rw_a1': nrm((N_ODD, D_MODEL, D_AAA_LORA), sd),
        'rw_a2': nrm((N_ODD, D_AAA_LORA, D_MODEL), 0.1 * D_AAA_LORA ** -0.5),
        'rw_v0': 0.5 + nrm((N_VMIX, D_MODEL), 0.1),
        'rw_v1': nrm((N_VMIX, D_MODEL, D_MV_LORA), sd),
        'rw_v2': nrm((N_VMIX, D_MV_LORA, D_MODEL), 0.1 * D_MV_LORA ** -0.5),
        'rw_g1': nrm((N_ODD, D_MODEL, D_GATE_LORA), sd),
        'rw_g2': nrm((N_ODD, D_GATE_LORA, D_MODEL), D_GATE_LORA ** -0.5),
        'rw_kk': 0.85 + nrm((N_ODD, D_MODEL), 0.05),
        'rw_ka': 1.0 + nrm((N_ODD, D_MODEL), 0.05),
        'rw_rk': nrm((N_ODD, H_C, N_C), 0.1),
        'rw_lnw': 1.0 + nrm((N_ODD, D_MODEL), 0.05),
        'rw_lnb': nrm((N_ODD, D_MODEL), 0.01),
        'w_ffn_gate': nrm((DEPTH, D_MODEL, FFN_DIM), sd),
        'w_ffn_up': nrm((DEPTH, D_MODEL, FFN_DIM), sd),
        'w_ffn_down': nrm((DEPTH, FFN_DIM, D_MODEL), FFN_DIM ** -0.5),
        'w_ple': nrm((DEPTH, PLE_DIM, D_MODEL), PLE_DIM ** -0.5),
        'w_ple_gate': nrm((DEPTH, D_MODEL, D_MODEL), sd),
    }

def reference(x_prompt, x_sample, p_prompt, p_sample, state_gla, state_hgrn, state_rwkv, state_shift,
              norm_mix, norm_ffn, norm_ple, norm_final,
              w_in_even, w_gk2, b_gk, gla_norm, hgrn_gamma, hgrn_norm, w_out_even,
              rw_mu, rw_wr, rw_wk, rw_wv, rw_wo, rw_w0, rw_w1, rw_w2, rw_a0, rw_a1, rw_a2,
              rw_v0, rw_v1, rw_v2, rw_g1, rw_g2, rw_kk, rw_ka, rw_rk, rw_lnw, rw_lnb,
              w_ffn_gate, w_ffn_up, w_ffn_down, w_ple, w_ple_gate):
    f32 = jnp.float32
    sm = jax.nn.softmax(hgrn_gamma.astype(f32), axis=0)
    lower_bounds = jnp.cumsum(sm, axis=0) - sm[0:1]

    def run(x, p, s_gla, s_hgrn, s_rwkv, s_shift):
        h = x
        out_gla, out_hgrn, out_rwkv, out_shift = [], [], [], []
        v_first = None
        for i in range(DEPTH):
            j = i // 2
            xn = rmsnorm(h, norm_mix[i])
            if i % 2 == 0:
                mix, sg, sh = gla_hgrn_mixer(xn, s_gla[j], s_hgrn[j], lower_bounds[j], w_in_even[j],
                                             w_gk2[j], b_gk[j], gla_norm[j], hgrn_norm[j], w_out_even[j])
                out_gla.append(sg)
                out_hgrn.append(sh)
            else:
                vmix = None if j == 0 else (rw_v0[j - 1], rw_v1[j - 1], rw_v2[j - 1])
                mix, sr, ss, v_first = rwkv7_mixer(xn, s_rwkv[j], s_shift[j], v_first, rw_mu[j], rw_wr[j],
                                                   rw_wk[j], rw_wv[j], rw_wo[j], rw_w0[j], rw_w1[j], rw_w2[j],
                                                   rw_a0[j], rw_a1[j], rw_a2[j], vmix, rw_g1[j], rw_g2[j],
                                                   rw_kk[j], rw_ka[j], rw_rk[j], rw_lnw[j], rw_lnb[j])
                out_rwkv.append(sr)
                out_shift.append(ss)
            h = h + mix
            h = h + swiglu(rmsnorm(h, norm_ffn[i]), w_ffn_gate[i], w_ffn_up[i], w_ffn_down[i])
            gate = jax.nn.sigmoid(rmsnorm(h, norm_ple[i]) @ w_ple_gate[i])
            h = h + gate * (p[i] @ w_ple[i])
        return (rmsnorm(h, norm_final), jnp.stack(out_gla), jnp.stack(out_hgrn),
                jnp.stack(out_rwkv), jnp.stack(out_shift))

    bp = x_prompt.shape[0]
    y_prompt, gla_p, hgrn_p, rwkv_p, shift_p = run(
        x_prompt, p_prompt,
        jnp.zeros((N_EVEN, bp, H_A, DK_A, DV_A), f32),
        jnp.zeros((N_EVEN, bp, H_B, N_B, DV_B), f32),
        jnp.zeros((N_ODD, bp, H_C, N_C, N_C), f32),
        jnp.zeros((N_ODD, bp, D_MODEL), x_prompt.dtype))
    y_sample, gla_s, hgrn_s, rwkv_s, shift_s = run(
        x_sample, p_sample, state_gla, state_hgrn, state_rwkv, state_shift)
    return (y_prompt, y_sample, gla_p, hgrn_p, rwkv_p, shift_p, gla_s, hgrn_s, rwkv_s, shift_s)


_drawn_inputs = setup_inputs


def setup_inputs(seed=0):
    import zlib

    import numpy as np

    out = dict(_drawn_inputs(seed))
    spreads = {}
    factors = {'norm_ple': 5.256,
     'rw_w1': 5.351,
     'rw_w2': 5.365,
     'rw_kk': 10.73,
     'rw_lnw': 3.399,
     'rw_lnb': 23.024}
    for name, (base, spread) in spreads.items():
        noise = np.random.default_rng([zlib.crc32(name.encode()), seed]).standard_normal(out[name].shape)
        drawn = base * np.exp(spread * noise) if base else spread * noise
        out[name] = __import__('jax').numpy.asarray(drawn.astype(out[name].dtype))
    for name, factor in factors.items():
        out[name] = (out[name] * factor).astype(out[name].dtype)
    return out
```

```python
from contextlib import ExitStack

import numpy as np

import concourse.bass as bass
from concourse import mybir

F32 = mybir.dt.float32
F32R = mybir.dt.float32r
ACT = mybir.ActivationFunctionType
ALU = mybir.AluOpType
ds = bass.ds

P = 128
D = 1024
KT = D // P
TP = 512
NB, ST = 8, 4
TS = NB * ST
T = TP + TS
TH = T // 2
FFN = 2816
FT = FFN // P // 2
PLE = 256
RMS_EPS = 1e-6

HA, DKA, HB, NBK, DV = 4, 64, 4, 128, 128
KTILES = HA * DKA // P + HB
CE = 64
NCE = TP // CE
LEVELS = 6
EVEN_IN = {"q_a": 0, "k_a": 256, "v_a": 512, "g_a": 1024, "gk": 1536, "q_b": 1552, "f_b": 2064, "i_b": 2576,
           "g_b": 3088}
HC, NC = 16, 64
CO = 32
NCO = T // CO
GN_EPS = 64e-5


class Signal:

    def __init__(self, sem, name, seen, known):
        self.sem, self.name, self.seen, self.known, self.n = sem, name, seen, known, 0

    def done(self, step):
        self.n += 1
        assert (self.name, step) not in self.seen, (self.name, step)
        self.seen[self.name, step] = self.n
        return self.sem, 1

    def loaded(self, step):
        self.n += 16
        self.seen[self.name, step] = self.n
        return self.sem, 16

    def at(self, step):
        if self.known is not None:
            return self.sem, self.known[self.name, step]
        return self.sem, 1


VEC0 = [("norm_mix", 16), ("norm_ffn", 16), ("norm_ple", 16), ("norm_final", 8), ("b_gk", 2), ("gla_norm", 1),
        ("hgrn_gamma", 4), ("hgrn_norm", 1), ("rw_mu", 48), ("rw_w0", 8), ("rw_a0", 8)]
VEC1 = [("rw_kk", 8), ("rw_ka", 8), ("rw_rk", 8), ("rw_lnw", 8), ("rw_lnb", 8), ("state_shift", 64)]
VCOL = {}
for _half, _table in enumerate((VEC0, VEC1)):
    _at = 0
    for _name, _rows in _table:
        VCOL[_name] = (_half, _at, _rows)
        _at += _rows



def even_tables():
    p, t = np.arange(P)[:, None], np.arange(CE)[None, :]
    s = p % CE
    masks = [s == t]
    for level in range(1, LEVELS + 1):
        m = 1 << (level - 1)
        masks.append((s // (2 * m) == t // (2 * m)) & (s % (2 * m) < m) & (t % (2 * m) >= m))
    return np.concatenate(masks + [scan_resets(CE), p // ST == np.arange(NB)[None, :]], 1).astype(np.float32)


def scan_resets(chunk):
    t = np.arange(T)
    keep = np.where(t < TP, t % chunk != 0, t % ST != 0)
    return np.broadcast_to(keep, (P, T))


def odd_tables():
    p, t = np.arange(P)[:, None], np.arange(CO)[None, :]
    s = p % CO
    same_head = p // NC == np.arange(P)[None, :] // NC
    halves = []
    for level in range(1, 6):
        m = 1 << (level - 1)
        halves.append((s // (2 * m) == t // (2 * m)) & (s % (2 * m) < m) & (t % (2 * m) >= m))
    prompt = [s < t, s <= t]
    sample = [(s < t) & (s // ST == t // ST), (s <= t) & (s // ST == t // ST)]
    head = [(2 * k + p // NC) == np.arange(HC)[None, :] for k in range(KT)]
    batch = [s // ST == np.arange(NB)[None, :]]
    return np.concatenate([scan_resets(CO), same_head] + halves + prompt + sample + head + batch, 1).astype(np.float32)


def head_spread():
    return (np.arange(HC)[:, None] == np.arange(D)[None, :] // NC).astype(np.float32)


TABC = 1104


def trunk(nc, a, o, known, seen, stop=99):
    ctx = ExitStack()
    with ctx:
        def sb(name, shape, dt=F32):
            return ctx.enter_context(nc.sbuf_tensor(name, shape, dt))

        def sem(name):
            return ctx.enter_context(nc.semaphore(name))

        class Section:
            def __init__(self, name):
                def signal(by):
                    return Signal(sem(f"{name}_{by}"), f"{name}_{by}", seen, known)

                self.pe, self.act, self.dve = signal("pe"), signal("act"), signal("dve")
                self.pool, self.dma = signal("pool"), signal("dma")

        hT = sb("hT", [P, KT, T])
        xs_byte = (nc.sbuf_base + 31) // 32 * 32
        xs = sb("x_split", [P, 2 * KT * T], F32R)
        xh = xs[:, 0:KT * T].rearrange("p (k t) -> p k t", k=KT)
        xl = xs[:, KT * T:2 * KT * T].rearrange("p (k t) -> p k t", k=KT)
        raw = sb("w_raw", [P, 2, FT * P])
        wh = sb("w_head", [P, 2, FT * P], F32R)
        wl = sb("w_rest", [P, 2, FT * P], F32R)
        ident = sb("ident", [P, P])
        ones = sb("ones", [P, P])
        vec = sb("vectors", [P, 2, P])
        eps = sb("epsilons", [P, 3])
        eps_rms, eps_gn, bias17 = eps[:, 0:1], eps[:, 1:2], eps[:, 2:3]
        tab = sb("tables", [P, TABC])
        MIXC = 30016
        mix_byte = (nc.sbuf_base + 31) // 32 * 32
        mix = sb("mix", [P, MIXC])
        ps = ctx.enter_context(nc.psum_tensor("ps", [P, 8, 512], F32))

        def col(name, i=0):
            half, at, _ = VCOL[name]
            return vec[:, half, at + i:at + i + 1]

        raw_in = [sem("slabA_loaded"), sem("slabB_loaded")]
        head_ok = [sem("slabA_head"), sem("slabB_head")]
        rest_ok = [sem("slabA_rest"), sem("slabB_rest")]
        mm_ok = [sem("productA"), sem("productB")]
        bank_free = [sem("banksA_read"), sem("banksB_read")]

        def W(name, layer):
            return a[name][layer]

        w_in = W("w_in_even", 0)
        stages = {}
        order = []

        def stage(name, n, units):
            stages[name] = (n, units)
            order.append(name)

        X = (xh, xl)
        stage("v_a", 2, [(w_in, EVEN_IN["v_a"], 256, 0, KT, X), (w_in, EVEN_IN["v_a"] + 128, 256, 0, KT, X)])
        stage("i_b", 2, [(w_in, EVEN_IN["i_b"], 256, 0, KT, X), (w_in, EVEN_IN["i_b"] + 128, 256, 0, KT, X)])
        stage("gk", 1, [(w_in, EVEN_IN["gk"], 0, 0, KT, X)])
        for name, n in (("f_b", 2), ("k_a", 1), ("q_a", 1), ("q_b", 2), ("g_a", 2), ("g_b", 2)):
            stage(name, n, [(w_in, EVEN_IN[name], 256, 0, KT, X), (w_in, EVEN_IN[name] + 128, 256, 0, KT, X)])
        stage("w_out", 4, [(W("w_out_even", 0), 0, 256, 0, KT, X), (W("w_out_even", 0), 128, 256, 0, KT, X)])

        base = mix_byte
        hid = nc.alloc_sbuf_tensor_at("hidden_split", [P, 2, FT, T], F32R, offset=base)
        ple = nc.alloc_sbuf_tensor_at("ple_split", [P, 2, PLE // P, T], F32R, offset=base + 4 * 2 * FT * T)
        MIXF = 2 * FT * T + 2 * (PLE // P) * T

        def tail_stages(i):
            for half in range(2):
                c = half * FT * P
                stage(f"up{i}{half}", FT, [(W("w_ffn_gate", i), c, 128, 0, KT, X), (W("w_ffn_up", i), c, 128, 0, KT, X)])
                stage(f"down{i}{half}", 4, [(W("w_ffn_down", i), 0, 256, c, FT, (hid[:, 0], hid[:, 1])),
                                            (W("w_ffn_down", i), 128, 256, c, FT, (hid[:, 0], hid[:, 1]))])
            stage(f"ple{i}", 8, [(W("w_ple_gate", i), 0, 128, 0, KT, X),
                                 (W("w_ple", i), 0, 128, 0, PLE // P, (ple[:, 0], ple[:, 1]))])

        tail_stages(0)
        for name in ("r", "k", "g1", "v"):
            if name == "g1":
                stage("rw_g1", 1, [(W("rw_g1", 0), 0, 0, 0, KT, X)])
                continue
            w = W(f"rw_w{name}", 0)
            stage(f"rw_{name}", 4, [(w, 0, 256, 0, KT, X), (w, 128, 256, 0, KT, X)])
        stage("rw_o", 4, [(W("rw_wo", 0), 0, 256, 0, KT, X), (W("rw_wo", 0), 128, 256, 0, KT, X)])
        tail_stages(1)
        used = {}
        ab = [0, 0]
        for name in order:
            used[name] = tuple(ab)
            n, units = stages[name]
            for s in range(len(units)):
                ab[s] += n

        def each(eng, n, first, body):
            if n > 2:
                with eng.Fori(0, n - 1) as i:
                    body(i, False)
            else:
                for i in range(n - 1):
                    body(i, False)
            body(n - 1, True)

        def sp_stage(sp, name):
            n, units = stages[name]

            def load(i):
                for s, (w, c, step, row, kt, _) in enumerate(units):
                    use = used[name][s] + i
                    if not (isinstance(use, int) and use == 0):
                        sp.wait_ge(rest_ok[s], use)
                    src = w[row:row + kt * P, :].rearrange("(k p) n -> p k n", p=P)
                    sp.dma_start(raw[:, s, 0:kt * P].rearrange("p (k n) -> p k n", k=kt),
                                 src[:, :, ds(i * step + c, P)]).then_inc(raw_in[s], 16)

            if n > 2:
                with sp.Fori(0, n) as i:
                    load(i)
            else:
                for i in range(n):
                    load(i)

        def act_head(act, name, s, i):
            use, kt = used[name][s] + i, stages[name][1][s][4]
            act.wait_ge(raw_in[s], 16 * use + 16)
            act.wait_ge(mm_ok[s], use)
            act.activation(wh[:, s, 0:kt * P], raw[:, s, 0:kt * P], ACT.Copy).then_inc(head_ok[s], 1)

        def dve_rest(dve, name, s, i):
            use, kt = used[name][s] + i, stages[name][1][s][4]
            dve.wait_ge(head_ok[s], use + 1)
            dve.tensor_tensor(wl[:, s, 0:kt * P], raw[:, s, 0:kt * P], wh[:, s, 0:kt * P].bitcast(F32),
                              ALU.subtract).then_inc(rest_ok[s], 1)

        def ahead(split, eng, name, s, i, last):
            if not last:
                split(eng, name, s, i + 1)
                return
            at = order.index(name) + 1
            while at < len(order) and len(stages[order[at]][1]) <= s:
                at += 1
            if at < len(order):
                split(eng, order[at], s, 0)

        def unit_products(pe, name, i, s):
            _, _, _, _, kt, (uh, ul) = stages[name][1][s]
            use = used[name][s] + i
            pe.wait_ge(head_ok[s], use + 1)
            pe.wait_ge(rest_ok[s], use + 1)
            pe.wait_ge(bank_free[s], use)
            for k in range(kt):
                for w, x, first in ((wh, uh, True), (wh, ul, False), (wl, uh, False)):
                    for h in range(2):
                        mm = pe.matmul(ps[:, 2 * s + h, 0:TH], w[:, s, k * P:(k + 1) * P],
                                       x[:, k, h * TH:(h + 1) * TH], start=first and k == 0,
                                       stop=k == kt - 1 and w is wl)
            mm.then_inc(mm_ok[s], 1)

        def pe_stage(pe, name):
            n, units = stages[name]

            def products(i, last):
                for s in range(len(units)):
                    unit_products(pe, name, i, s)

            each(pe, n, name, products)

        def out2(s):
            return ps[:, 2 * s:2 * s + 2, 0:TH]

        def two(ap):
            return ap.rearrange("p (h t) -> p h t", h=2)

        def cols(at, *shape):
            n = int(np.prod(shape))
            ap = mix[:, at:at + n]
            if len(shape) == 2:
                return ap.rearrange("p (a b) -> p a b", a=shape[0])
            if len(shape) == 3:
                return ap.rearrange("p (a b c) -> p a b c", a=shape[0], b=shape[1])
            return ap

        xtok = cols(0, 5, D)
        vrow = cols(5 * D, 2, P)
        vT = cols(0, KT, T)
        gate = cols(8 * T, KT, T)
        qq = cols(16 * T, KTILES, T)
        kk = cols(22 * T, KTILES, T)
        lg = cols(28 * T, KTILES, T)
        vtok = cols(34 * T, 5, D)
        ktok = cols(34 * T + 5 * D, 5, KTILES * P)
        soft = cols(34 * T + 5 * D, KTILES, T)
        pT = cols(34 * T + 5 * D + 5 * KTILES * P, 8, 5, CE)
        qk = cols(0, LEVELS, T)
        ee = cols(LEVELS * T, 2, T)
        oT = cols(22 * T, KT, T)
        sq = cols(0, 2, T)
        rstd = cols(2 * T, 2, T)
        nrm = cols(4 * T, 2, T)
        lrT = cols(34 * T + 5 * D, T)
        wgk2 = cols(34 * T + 5 * D + 3300, HA * DKA)
        lbs = cols(34 * T + 5 * D + 5 * KTILES * P + 2500, 40)
        alias = nc.alloc_sbuf_tensor_at("even_scratch", [P, 8704], F32, offset=xs_byte)
        state = alias[:, 0:768].rearrange("p (k v) -> p k v", k=KTILES)
        sst = alias[:, 768:2816].rearrange("p (a b v) -> p a b v", a=2, b=NB)
        vx = alias[:, 2816:4864].rearrange("p (a b v) -> p a b v", a=2, b=NB)
        mt = alias[:, 4864:6912].rearrange("p (a c) -> p a c", a=2)
        ebl = alias[:, 6912:7008].rearrange("p (k c) -> p k c", k=KTILES)
        snew = alias[:, 7168:8192].rearrange("p (b v) -> p b v", b=NB)
        lvmask = tab[:, 0:7 * CE].rearrange("p (l t) -> p l t", l=7)
        resetE = tab[:, 7 * CE:7 * CE + T]
        batE = tab[:, 7 * CE + T:7 * CE + T + NB]

        def rows(h):
            if h < HA:
                return h // 2, 64 * (h % 2), DKA
            return h - HA + 2, 0, NBK

        heads_of = [[0, 1], [2, 3], [4], [5], [6], [7]]
        jobs = [(kt, h) for kt in range(KTILES) for h in heads_of[kt]]

        E0 = Section("embed")

        def act_embed(act):
            act.dma_start(ident[:, :], a["ident"][:, 0:P]).then_inc(*E0.dma.loaded("i"))
            act.dma_start(ones[:, :], a["ident"][:, P:2 * P]).then_inc(*E0.dma.loaded("o"))
            act.dma_start(tab[:, 0:7 * CE + T + NB], a["even_tables"]).then_inc(*E0.dma.loaded("t"))
            for half, table in enumerate((VEC0, VEC1)):
                at = 0
                for name, n in table:
                    shape = a[name].shape
                    flat = a[name]
                    if len(shape) == 1:
                        flat = flat.rearrange("(r c) -> r c", c=P)
                    elif len(shape) == 2:
                        flat = flat.rearrange("i (r c) -> (i r) c", c=P)
                    elif name == "rw_rk":
                        flat = flat.rearrange("i (r e) c -> (i r) (e c)", e=2)
                    elif len(shape) == 3:
                        flat = flat.rearrange("i j (r c) -> (i j r) c", c=P)
                    act.dma_start(vrow[at:at + n, half, :], flat).then_inc(*E0.dma.loaded(name))
                    at += n
            act.dma_start(xtok[:, 0:4, :], a["x_prompt"][0].rearrange("(a p) d -> p a d", p=P)).then_inc(
                *E0.dma.loaded("xp"))
            act.dma_start(xtok[0:TS, 4, :], a["x_sample"].rearrange("b t d -> (b t) d")).then_inc(
                *E0.dma.loaded("all"))

        def pe_embed(pe):
            pe.wait_ge(*E0.dma.at("all"))
            for half, n in ((0, P), (1, 104)):
                mm = pe.transpose(ps[:, 4 + half, 0:n], vrow[0:n, half, :], ident[0:n, 0:n])
            mm.then_inc(*E0.pe.done("vec"))
            for j, (tt, k4) in enumerate((t, k) for t in range(5) for k in range(2)):
                n = P if tt < 4 else TS
                if j < 2:
                    bank = 6 + j
                else:
                    bank = 4 + (j - 2) % 4
                if j >= 6:
                    pe.wait_ge(*E0.dve.at(f"x{j - 4}"))
                elif j >= 2 and j < 4:
                    pe.wait_ge(*E0.dve.at("vec"))
                elif j >= 4:
                    pe.wait_ge(*E0.dve.at(f"x{j - 4}"))
                for k in range(4):
                    mm = pe.transpose(ps[:, bank, k * n:(k + 1) * n], xtok[0:n, tt, (4 * k4 + k) * P:(4 * k4 + k + 1) * P],
                                      ident[0:n, 0:n])
                mm.then_inc(*E0.pe.done(f"x{j}"))

        def dve_embed(dve):
            dve.memset(eps_rms, RMS_EPS)
            dve.memset(eps_gn, GN_EPS)
            dve.memset(bias17, 8.5 * float(np.log(2.0)))
            dve.wait_ge(*E0.pe.at("vec"))
            dve.tensor_copy(vec[:, 0, :], ps[:, 4, 0:P])
            dve.tensor_copy(vec[:, 1, 0:104], ps[:, 5, 0:104]).then_inc(*E0.dve.done("vec"))
            for j, (tt, k4) in enumerate((t, k) for t in range(5) for k in range(2)):
                n = P if tt < 4 else TS
                bank = 6 + j if j < 2 else 4 + (j - 2) % 4
                dve.wait_ge(*E0.pe.at(f"x{j}"))
                dve.tensor_copy(hT[:, 4 * k4:4 * k4 + 4, tt * P:tt * P + n],
                                ps[:, bank, 0:4 * n].rearrange("p (k t) -> p k t", k=4)).then_inc(*E0.dve.done(f"x{j}"))
            dve.wait_ge(*E0.dve.at("x9"))

        nsq = cols(MIXC - 4 * T, 3, T)
        nrs = cols(MIXC - T, T)

        class Norm:
            def __init__(self, name, gain, ready, before):
                self.s, self.gain, self.ready, self.before = Section(f"norm_{name}"), gain, ready, used[before]

        def act_norm(act, n, split=True):
            s = n.s
            for r in n.ready:
                act.wait_ge(*r)
            for k in range(KT):
                if k >= 2:
                    act.wait_ge(*s.dve.at(f"sum{k - 2}"))
                act.activation(nsq[:, k % 2, :], hT[:, k, :], ACT.Square).then_inc(*s.act.done(f"sq{k}"))
            act.wait_ge(*s.pe.at("mean"))
            act.activation(two(nsq[:, 0, :]), ps[:, 4:6, 0:TH], ACT.Sqrt, bias=eps_rms,
                           scale=1.0 / D).then_inc(*s.act.done("mean"))
            for k in range(KT if split else 0):
                act.wait_ge(*s.dve.at(f"y{k}"))
                act.activation(xh[:, k, :], nsq[:, 1 + k % 2, :], ACT.Copy).then_inc(*s.act.done(f"h{k}"))

        def dve_norm(dve, n, split=True):
            s = n.s
            for r in n.ready:
                dve.wait_ge(*r)
            for k in range(KT):
                dve.wait_ge(*s.act.at(f"sq{k}"))
                if k == 0:
                    dve.tensor_copy(nsq[:, 2, :], nsq[:, 0, :]).then_inc(*s.dve.done("sum0"))
                else:
                    dve.wait_ge(*s.dve.at(f"sum{k - 1}"))
                    dve.tensor_tensor(nsq[:, 2, :], nsq[:, 2, :], nsq[:, k % 2, :], ALU.add).then_inc(
                        *s.dve.done(f"sum{k}"))
            dve.wait_ge(*s.act.at("mean"))
            dve.reciprocal(nrs[:, :], nsq[:, 0, :]).then_inc(*s.dve.done("rstd"))
            dve.wait_ge(*s.dve.at("rstd"))
            dve.wait_ge(mm_ok[0], n.before[0])
            dve.wait_ge(mm_ok[1], n.before[1])
            for k in range(KT):
                y = nsq[:, 1 + k % 2, :] if split else xn[:, k, :]
                if k >= 2 and split:
                    dve.wait_ge(*s.dve.at(f"l{k - 2}"))
                dve.scalar_tensor_tensor(out=y, in0=hT[:, k, :], scalar=n.gain(k), in1=nrs[:, :], op0=ALU.mult,
                                         op1=ALU.mult).then_inc(*s.dve.done(f"y{k}"))
                if not split:
                    continue
                dve.wait_ge(*s.act.at(f"h{k}"))
                dve.tensor_tensor(xl[:, k, :], y, xh[:, k, :].bitcast(F32), ALU.subtract).then_inc(
                    *s.dve.done(f"l{k}"))

        def pe_norm(pe, n):
            s = n.s
            pe.wait_ge(*s.dve.at(f"sum{KT - 1}"))
            for h in range(2):
                mm = pe.matmul(ps[:, 4 + h, 0:TH], ones[:, :], nsq[:, 2, h * TH:(h + 1) * TH], start=True, stop=True)
            mm.then_inc(*s.pe.done("mean"))

        def pe_norm_wait(pe, n):
            pe.wait_ge(*n.s.dve.at(f"l{KT - 1}"))
            pe.wait_ge(*n.s.act.at(f"h{KT - 1}"))


        E1 = Section("even_in")
        E2 = Section("even_decay")
        E3 = Section("even_scores")
        E4 = Section("even_chunks")
        E5 = Section("even_gate")
        K40 = float(2.0 ** 40)

        def pe_even_in(pe):
            pe_norm_wait(pe, norm0)
            for name in ("v_a", "i_b", "gk"):
                pe_stage(pe, name)
            for s in range(2):
                pe.wait_ge(bank_free[s], used["gk"][s])
            for j, (tt, half) in enumerate((t, k) for t in range(5) for k in range(2)):
                n = P if tt < 4 else TS
                if j >= 4:
                    pe.wait_ge(*E1.dve.at(f"vt{j - 4}"))
                for k in range(4):
                    mm = pe.transpose(ps[0:n, 4 + j % 4, k * P:(k + 1) * P], vT[:, 4 * half + k, tt * P:tt * P + n],
                                      ident[:, :])
                mm.then_inc(*E1.pe.done(f"vt{j}"))
            pe.wait_ge(bank_free[0], used["f_b"][0])
            pe.wait_ge(*E1.dma.at("wgk2"))
            pe.wait_ge(*E1.dve.at("vt9"))
            for k in range(2):
                for h in range(2):
                    mm = pe.matmul(ps[:, 4 + 2 * k + h, 0:TH], wgk2[0:16, k * P:(k + 1) * P],
                                   lrT[0:16, h * TH:(h + 1) * TH], start=True, stop=True)
            mm.then_inc(*E1.pe.done("gk2"))
            for name in ("f_b", "k_a", "q_a", "q_b", "g_a", "g_b"):
                pe_stage(pe, name)

        def act_even_in(act):
            act.dma_start(wgk2[0:16, :], a["w_gk2"][0]).then_inc(*E1.dma.loaded("wgk2"))

            for name, fn in (("v_a", None), ("i_b", None), ("gk", "gk"), ("f_b", None), ("k_a", None), ("q_a", None),
                             ("q_b", "q"), ("g_a", "g"), ("g_b", "g")):
                n, units = stages[name]
                for i in range(n):
                    for s in range(len(units)):
                        use = used[name][s] + i
                        act.wait_ge(mm_ok[s], use + 1)
                        ahead(act_head, act, name, s, i, i == n - 1)
                        if fn == "gk":
                            act.activation(two(lrT)[0:16], out2(s)[0:16], ACT.Copy).then_inc(bank_free[s], 1)
                        if fn == "q":
                            act.activation(two(qq[:, 2 + 2 * i + s, :]), out2(s), ACT.Silu).then_inc(bank_free[s], 1)
                        if fn == "g":
                            t = 2 * i + s + (4 if name == "g_b" else 0)
                            act.activation(two(gate[:, t, :]), out2(s), ACT.Silu).then_inc(bank_free[s], 1)

        def dve_even_in(dve):
            for name, fn in (("v_a", 0), ("i_b", 4), ("gk", None), ("f_b", "f"), ("k_a", "k"), ("q_a", "qa"),
                             ("q_b", None), ("g_a", None), ("g_b", None)):
                n, units = stages[name]
                for i in range(n):
                    for s in range(len(units)):
                        use = used[name][s] + i
                        if fn is not None:
                            dve.wait_ge(mm_ok[s], use + 1)
                        if fn in (0, 4):
                            t = fn + 2 * i + s
                            dve.tensor_copy(two(vT[:, t, :]), out2(s)).then_inc(bank_free[s], 1)
                        if fn == "f":
                            dve.tensor_copy(two(lg[:, 2 + 2 * i + s, :]), out2(s)).then_inc(bank_free[s], 1)
                        if fn == "k":
                            dve.tensor_copy(two(kk[:, s, :]), out2(s)).then_inc(bank_free[s], 1)
                        if fn == "qa":
                            dve.tensor_scalar(two(qq[:, s, :]), out2(s), DKA ** -0.5, None, ALU.mult).then_inc(
                                bank_free[s], 1)
                        ahead(dve_rest, dve, name, s, i, i == n - 1)
                if name == "gk":
                    for j, (tt, half) in enumerate((t, k) for t in range(5) for k in range(2)):
                        nt = P if tt < 4 else TS
                        dve.wait_ge(*E1.pe.at(f"vt{j}"))
                        dve.tensor_copy(vtok[0:nt, tt, half * 512:half * 512 + 512], ps[0:nt, 4 + j % 4, :]).then_inc(
                            *E1.dve.done(f"vt{j}"))
                    dve.wait_ge(*E1.pe.at("gk2"))
                    for k in range(2):
                        dve.tensor_scalar(two(lg[:, k, :]), ps[:, 4 + 2 * k:6 + 2 * k, 0:TH], col("b_gk", k), None,
                                          ALU.add).then_inc(*E1.dve.done(f"z{k}"))

        gam = vec[:, 0, VCOL["hgrn_gamma"][1]:VCOL["hgrn_gamma"][1] + 4]
        lb_e, lb_r, lb_sm, lb, lb_c, lb_1m, lb_om, lb_t = (lbs[:, 4 * i:4 * i + 4] for i in range(8))
        zz = lg[:, :, :]
        hz = lg[:, 2:6, :]

        def dve_decay(dve):
            def step(ins, name):
                ins.then_inc(*E2.dve.done(name))
                dve.wait_ge(*E2.dve.at(name))

            step(dve.tensor_tensor(lb_t, gam, gam, ALU.subtract), "g0")
            dve.wait_ge(*E2.act.at("ge"))
            step(dve.reciprocal(lb_r, lb_e), "gr")
            step(dve.tensor_tensor(lb_sm, lb_e, lb_r, ALU.mult), "gsm")
            step(dve.tensor_tensor(lb, lb_sm, lb_sm, ALU.subtract), "lb")
            step(dve.tensor_scalar(lb_t, lb, 1e-20, K40, ALU.max, ALU.mult), "lbt")
            step(dve.tensor_scalar(lb_om, lb, -1.0, 1.0, ALU.mult, ALU.add), "lbo")
            dve.wait_ge(bank_free[0], used["k_a"][0])
            dve.wait_ge(bank_free[1], used["k_a"][1])
            dve.wait_ge(*E1.dve.at("z1"))
            dve.wait_ge(*E1.pe.at("gk2"))
            step(dve.scalar_tensor_tensor(out=soft, in0=zz, scalar=-1.0, in1=zz, op0=ALU.mult, op1=ALU.max), "abs")
            dve.wait_ge(*E2.act.at("ln"))
            step(dve.scalar_tensor_tensor(out=soft, in0=zz, scalar=0.0, in1=soft, op0=ALU.min, op1=ALU.subtract), "lsig")
            step(dve.tensor_tensor(kk[:, 2:6, :], soft[:, 2:6, :], hz, ALU.subtract), "kz")
            step(dve.tensor_scalar(lg[:, 0:2, :], soft[:, 0:2, :], 1.0 / 16.0, None, ALU.mult), "gla")
            dve.wait_ge(*E2.act.at("l1m"))
            for t in range(4):
                dve.tensor_scalar(lg[:, 2 + t, :], soft[:, 2 + t, :], lb_1m[:, t:t + 1], None, ALU.add).then_inc(
                    *E2.dve.done(f"l1{t}"))
            dve.wait_ge(*E2.dve.at("l13"))
            step(dve.tensor_scalar(lb_c, lb_c, -40.0 * float(np.log(2.0)), None, ALU.add), "c")
            for t in range(4):
                dve.tensor_scalar(soft[:, 2 + t, :], lg[:, 2 + t, :], lb_c[:, t:t + 1], None, ALU.subtract).then_inc(
                    *E2.dve.done(f"d{t}"))
            dve.wait_ge(*E2.dve.at("d3"))
            step(dve.scalar_tensor_tensor(out=soft[:, 2:6, :], in0=soft[:, 2:6, :], scalar=-1.0,
                                          in1=soft[:, 2:6, :], op0=ALU.mult, op1=ALU.max), "abs2")
            dve.wait_ge(*E2.act.at("ln2"))
            for t in range(4):
                dve.scalar_tensor_tensor(out=lg[:, 2 + t, :], in0=lg[:, 2 + t, :], scalar=lb_c[:, t:t + 1],
                                         in1=soft[:, 2 + t, :], op0=ALU.max, op1=ALU.add).then_inc(
                    *E2.dve.done(f"lf{t}"))
            dve.wait_ge(*E2.act.at("kb"))
            for t in range(4):
                dve.tensor_scalar(kk[:, 2 + t, :], kk[:, 2 + t, :], lb_om[:, t:t + 1], None, ALU.mult).then_inc(
                    *E2.dve.done(f"kb{t}"))
            dve.wait_ge(bank_free[0], used["g_a"][0])
            dve.wait_ge(bank_free[1], used["g_a"][1])
            dve.tensor_scalar(qq[:, 2:6, :], qq[:, 2:6, :], NBK ** -0.5, None, ALU.mult).then_inc(*E2.dve.done("qb"))
            dve.wait_ge(*E2.dve.at("lf3"))
            for kt in range(KTILES):
                dve.tensor_tensor_scan(lg[:, kt, :], resetE, lg[:, kt, :], 0.0, ALU.mult, ALU.add).then_inc(
                    *E2.dve.done(f"b{kt}"))

        def act_decay(act):
            act.wait_ge(*E2.dve.at("g0"))
            act.activation(lb_e, lb_t, ACT.Exp).then_inc(*E2.act.done("ge"))
            act.wait_ge(*E2.dve.at("lbo"))
            act.activation(lb_c, lb_t, ACT.Ln)
            act.activation(lb_1m, lb_om, ACT.Ln).then_inc(*E2.act.done("l1m"))
            act.wait_ge(*E2.dve.at("abs"))
            act.activation(soft, soft, ACT.Exp, scale=-1.0).then_inc(*E2.act.done("e"))
            act.wait_ge(*E2.act.at("e"))
            act.activation(soft, soft, ACT.Ln, bias=1.0).then_inc(*E2.act.done("ln"))
            act.wait_ge(*E2.dve.at("kz"))
            act.activation(kk[:, 2:6, :], kk[:, 2:6, :], ACT.Exp).then_inc(*E2.act.done("kb"))
            act.wait_ge(*E2.dve.at("abs2"))
            act.activation(soft[:, 2:6, :], soft[:, 2:6, :], ACT.Exp, scale=-1.0).then_inc(*E2.act.done("e2"))
            act.wait_ge(*E2.act.at("e2"))
            act.activation(soft[:, 2:6, :], soft[:, 2:6, :], ACT.Ln, bias=1.0).then_inc(*E2.act.done("ln2"))

        def span(level):
            return T if level <= 2 else TP

        def halves_of(ap, level):
            m = 1 << (level - 1)
            return ap[:, 0:span(level)].rearrange("p (n h m) -> p n h m", h=2, m=m)

        steps = [(kt, level) for kt in range(KTILES) for level in range(1, LEVELS + 1)]

        def dve_scores(dve):
            dve.wait_ge(mm_ok[0], used["w_out"][0])
            dve.wait_ge(mm_ok[1], used["w_out"][1])
            dve.wait_ge(*E2.dve.at(f"b{KTILES - 1}"))

            def distances(n):
                kt, level = steps[n]
                m = 1 << (level - 1)
                b, e = halves_of(lg[:, kt, :], level), halves_of(ee[:, n % 2, :], level)
                mid = b[:, :, 0, m - 1:m].to_broadcast([P, span(level) // (2 * m), m])
                if n >= 2:
                    dve.wait_ge(*E3.dve.at(f"qk{n - 2}"))
                dve.tensor_tensor(e[:, :, 0, :], mid, b[:, :, 0, :], ALU.subtract)
                dve.tensor_tensor(e[:, :, 1, :], b[:, :, 1, :], mid, ALU.subtract).then_inc(*E3.dve.done(f"e{n}"))

            def factors(n):
                kt, level = steps[n]
                e, z = halves_of(ee[:, n % 2, :], level), halves_of(qk[:, level - 1, :], level)
                dve.wait_ge(*E3.act.at(f"e{n}"))
                if kt > 0:
                    dve.wait_ge(*E3.pe.at(f"g{heads_of[kt - 1][-1]}"))
                dve.tensor_tensor(z[:, :, 0, :], e[:, :, 0, :], halves_of(kk[:, kt, :], level)[:, :, 0, :], ALU.mult)
                dve.tensor_tensor(z[:, :, 1, :], e[:, :, 1, :], halves_of(qq[:, kt, :], level)[:, :, 1, :],
                                  ALU.mult).then_inc(*E3.dve.done(f"qk{n}"))

            def masked(j):
                h = jobs[j][1]
                b0 = 4 * (j % 2)
                dve.wait_ge(*E3.pe.at(f"g{h}"))
                if j > 0:
                    dve.wait_ge(*E3.dve.at(f"ps{jobs[j - 1][1]}"))
                for q in range(4):
                    nl = 2 if q < 3 else 1
                    at = 0 if q % 2 else 512
                    out = mt[:, 1, at:at + nl * 256] if q else mt[:, 0, 0:512]
                    m = lvmask[:, 2 * q:2 * q + nl, :].unsqueeze(2).to_broadcast([P, nl, 4, CE])
                    if q == 3:
                        dve.wait_ge(*E3.dve.at(f"a{h}_1"))
                    dve.tensor_tensor(out.rearrange("p (l c t) -> p l c t", l=nl, c=4),
                                      ps[:, b0 + q, 0:nl * 256].rearrange("p (l c t) -> p l c t", l=nl, c=4), m,
                                      ALU.mult).then_inc(*E3.dve.done(f"m{h}_{q}"))
                    if q > 0:
                        dve.wait_ge(*E3.dve.at(f"m{h}_{q}"))
                        if q > 1:
                            dve.wait_ge(*E3.dve.at(f"a{h}_{q - 1}"))
                        dve.tensor_tensor(mt[:, 0, 0:nl * 256], mt[:, 0, 0:nl * 256], out, ALU.add).then_inc(
                            *E3.dve.done(f"a{h}_{q}"))
                dve.wait_ge(*E3.dve.at(f"a{h}_3"))
                dve.tensor_tensor(pT[:, h, 0:4, :], mt[:, 0, 0:256].rearrange("p (c t) -> p c t", c=4),
                                  mt[:, 0, 256:512].rearrange("p (c t) -> p c t", c=4), ALU.add).then_inc(
                    *E3.dve.done(f"p{h}"))
                dve.tensor_tensor(mt[0:TS, 1, 0:96].rearrange("p (l t) -> p l t", l=3),
                                  ps[0:TS, b0 + 3, 256:352].rearrange("p (l t) -> p l t", l=3),
                                  lvmask[0:TS, 0:3, 0:TS], ALU.mult).then_inc(*E3.dve.done(f"s{h}"))
                dve.wait_ge(*E3.dve.at(f"s{h}"))
                dve.tensor_tensor(mt[0:TS, 1, 0:32], mt[0:TS, 1, 0:32], mt[0:TS, 1, 32:64], ALU.add).then_inc(
                    *E3.dve.done(f"s2{h}"))
                dve.wait_ge(*E3.dve.at(f"s2{h}"))
                dve.tensor_tensor(pT[0:TS, h, 4, 0:TS], mt[0:TS, 1, 0:32], mt[0:TS, 1, 64:96], ALU.add).then_inc(
                    *E3.dve.done(f"ps{h}"))

            done = 0
            for n in range(len(steps)):
                distances(n)
                if n >= 1:
                    factors(n - 1)
                kt, level = steps[n]
                if kt > 0 and level == 3:
                    for h in heads_of[kt - 1]:
                        masked(done)
                        done += 1
            factors(len(steps) - 1)
            for h in heads_of[KTILES - 1]:
                masked(done)
                done += 1
            for kt in range(KTILES):
                b, e = lg[:, kt, :], ee[:, kt % 2, :]
                if kt >= 2:
                    dve.wait_ge(*E3.dve.at(f"kh{kt - 2}"))
                else:
                    dve.wait_ge(*E3.dve.at(f"qk{len(steps) - 1}"))
                for lo, n, c in ((0, NCE, CE), (TP, NB, ST)):
                    bb = b[:, lo:lo + n * c].rearrange("p (n c) -> p n c", c=c)
                    ins = dve.tensor_tensor(e[:, lo:lo + n * c].rearrange("p (n c) -> p n c", c=c),
                                            bb[:, :, c - 1:c].to_broadcast([P, n, c]), bb, ALU.subtract)
                ins.then_inc(*E3.dve.done(f"eh{kt}"))
                dve.wait_ge(*E3.act.at(f"eq{kt}"))
                dve.tensor_tensor(kk[:, kt, :], kk[:, kt, :], e, ALU.mult).then_inc(*E3.dve.done(f"kh{kt}"))
                dve.tensor_tensor(qq[:, kt, :], qq[:, kt, :], b, ALU.mult)
                dve.tensor_copy(ebl[:, kt, 0:NCE], b[:, 0:TP].rearrange("p (n c) -> p n c", c=CE)[:, :, CE - 1])
                dve.tensor_copy(ebl[:, kt, NCE:NCE + NB], b[:, TP:T].rearrange("p (n c) -> p n c", c=ST)[:, :, ST - 1]
                                ).then_inc(*E3.dve.done(f"qh{kt}"))

        def act_scores(act):
            for n in range(len(steps)):
                act.wait_ge(*E3.dve.at(f"e{n}"))
                w = span(steps[n][1])
                act.activation(ee[:, n % 2, 0:w], ee[:, n % 2, 0:w], ACT.Exp).then_inc(*E3.act.done(f"e{n}"))
            for kt in range(KTILES):
                act.wait_ge(*E3.dve.at(f"eh{kt}"))
                act.activation(ee[:, kt % 2, :], ee[:, kt % 2, :], ACT.Exp)
                act.activation(lg[:, kt, :], lg[:, kt, :], ACT.Exp).then_inc(*E3.act.done(f"eq{kt}"))

        def pe_scores(pe):
            for s in range(2):
                pe.wait_ge(bank_free[s], used["w_out"][s])
            pe.wait_ge(*E2.dve.at("qb"))
            pe.wait_ge(*E2.dve.at("kb3"))
            for j, (kt, h) in enumerate(jobs):
                _, r0, dk = rows(h)
                b0 = 4 * (j % 2)
                if j >= 2:
                    pe.wait_ge(*E3.dve.at(f"ps{jobs[j - 2][1]}"))
                for level in range(LEVELS + 1):
                    left = kk[r0:r0 + dk, kt, :] if level == 0 else qk[r0:r0 + dk, level - 1, :]
                    right = qq[r0:r0 + dk, kt, :] if level == 0 else left
                    if level:
                        pe.wait_ge(*E3.dve.at(f"qk{steps.index((kt, level))}"))
                    for c in range(NCE):
                        at = (level % 2) * 256 + (c // 2) * CE
                        mm = pe.matmul(ps[64 * (c % 2):64 * (c % 2) + CE, b0 + level // 2, at:at + CE],
                                       left[:, c * CE:(c + 1) * CE], right[:, c * CE:(c + 1) * CE],
                                       start=True, stop=True)
                    if level <= 2:
                        at = 256 + 32 * level
                        pe.matmul(ps[0:TS, b0 + 3, at:at + TS], left[:, TP:T], right[:, TP:T], start=True, stop=True)
                mm.then_inc(*E3.pe.done(f"g{h}"))

        loads4 = [Signal(sem(f"even_states{i}"), f"even_states{i}", seen, known) for i in range(2)]

        def pe_chunks(pe):
            for j in range(KTILES):
                b0 = 2 * (j % 4)
                pe.wait_ge(*E3.dve.at(f"kh{j}"))
                if j < 4:
                    pe.wait_ge(*E3.dve.at(f"ps{HA + HB - 1}"))
                else:
                    pe.wait_ge(*E4.act.at(f"kt{j - 4}"))
                for c in range(4):
                    pe.transpose(ps[:, b0, c * P:(c + 1) * P], kk[:, j, c * P:(c + 1) * P], ident[:, :])
                pe.transpose(ps[0:TS, b0 + 1, 0:P], kk[:, j, TP:T], ident[:, :]).then_inc(*E4.pe.done(f"kt{j}"))
            pe.wait_ge(*E4.act.at(f"kt{KTILES - 1}"))
            pe.wait_ge(*E3.dve.at(f"qh{KTILES - 1}"))
            for c in range(NCE):
                b0 = 4 * (c % 2)
                r, tt = 64 * (c % 2), c // 2
                if c >= 2:
                    pe.wait_ge(*E4.act.at(f"o{c - 2}"))
                    pe.wait_ge(*E4.dve.at(f"s{c - 2}_{KTILES - 1}"))
                for h in range(8):
                    kt, r0, dk = rows(h)
                    mm = pe.matmul(ps[r0:r0 + dk, b0 + 1 + kt // 4, (kt % 4) * DV:(kt % 4 + 1) * DV],
                              ktok[r:r + CE, tt, kt * P + r0:kt * P + r0 + dk],
                              vtok[r:r + CE, tt, h * DV:(h + 1) * DV], start=True, stop=True)
                mm.then_inc(*E4.pe.done(f"s{c}"))
                for h in range(8):
                    mm = pe.matmul(ps[:, b0, h * CE:(h + 1) * CE], vtok[r:r + CE, tt, h * DV:(h + 1) * DV],
                                   pT[r:r + CE, h, tt, :], start=h == 0, stop=c == 0, skip_group_check=True)
                if c > 0:
                    even, odd = [0, 2], [1, 3]
                    for i, h in enumerate((even if r == 0 else odd) + [4, 5, 6, 7] + (odd if r == 0 else even)):
                        kt, r0, dk = rows(h)
                        pe.wait_ge(*E4.dve.at(f"s{c - 1}_{kt}"))
                        if i == 6:
                            pe.wait_ge(*E4.pe.at(f"rows{c}"))
                        mm = pe.matmul(ps[:, b0, h * CE:(h + 1) * CE], state[r0:r0 + dk, kt, :],
                                       qq[r0:r0 + dk, kt, c * CE:(c + 1) * CE], start=False, stop=True,
                                       skip_group_check=True)
                        if i == 5:
                            mm.then_inc(*E4.pe.done(f"rows{c}"))
                mm.then_inc(*E4.pe.done(f"o{c}"))
            pe.wait_ge(*E4.act.at(f"o{NCE - 1}"))
            pe.wait_ge(*E4.dve.at(f"s{NCE - 1}_{KTILES - 1}"))
            for kt in range(KTILES):
                b0 = 4 * (kt % 2)
                pe.wait_ge(*loads4[kt % 2].at(f"ss{kt}"))
                if kt >= 2:
                    pe.wait_ge(*E4.dve.at(f"ss{kt - 2}"))
                for h in heads_of[kt]:
                    _, r0, dk = rows(h)
                    pe.wait_ge(*E4.pool.at(f"vx{h}"))
                    for g in range(2):
                        mm = pe.matmul(ps[r0:r0 + dk, b0 + g, :], ktok[0:TS, 4, kt * P + r0:kt * P + r0 + dk],
                                       vx[0:TS, h % 2, 4 * g:4 * g + 4, :].rearrange("p b v -> p (b v)"), start=True,
                                       stop=True)
                    mm.then_inc(*E4.pe.done(f"vx{h}"))
                for h in heads_of[kt]:
                    _, r0, dk = rows(h)
                    if h > 0:
                        pe.wait_ge(*E4.pe.at(f"so{h - 1}"))
                    pe.matmul(ps[:, 3, h * TS:(h + 1) * TS], vtok[0:TS, 4, h * DV:(h + 1) * DV], pT[0:TS, h, 4, 0:TS],
                              start=True, stop=False, skip_group_check=True)
                    for b in range(NB):
                        mm = pe.matmul(ps[:, 3, h * TS + b * ST:h * TS + (b + 1) * ST], sst[r0:r0 + dk, kt % 2, b, :],
                                       qq[r0:r0 + dk, kt, TP + b * ST:TP + (b + 1) * ST], start=False, stop=True,
                                       skip_group_check=True)
                    mm.then_inc(*E4.pe.done(f"so{h}"))

        def act_chunks(act):
            for j in range(KTILES):
                b0 = 2 * (j % 4)
                act.wait_ge(*E4.pe.at(f"kt{j}"))
                if j == 0:
                    act.wait_ge(*E2.dve.at("lf3"))
                act.activation(ktok[:, 0:4, j * P:(j + 1) * P], ps[:, b0, :].rearrange("p (c k) -> p c k", c=4),
                               ACT.Copy)
                act.activation(ktok[0:TS, 4, j * P:(j + 1) * P], ps[0:TS, b0 + 1, 0:P], ACT.Copy).then_inc(
                    *E4.act.done(f"kt{j}"))
            for c in range(NCE):
                act.wait_ge(*E4.pe.at(f"o{c}"))
                act.activation(oT[:, :, c * CE:(c + 1) * CE], ps[:, 4 * (c % 2), :].rearrange("p (h t) -> p h t", h=8),
                               ACT.Copy).then_inc(*E4.act.done(f"o{c}"))
            act.wait_ge(*E4.pe.at("so7"))
            act.activation(oT[:, :, TP:T], ps[:, 3, 0:8 * TS].rearrange("p (h t) -> p h t", h=8), ACT.Copy).then_inc(
                *E4.act.done("os"))

        def dve_chunks(dve):
            for c in range(NCE):
                b0 = 4 * (c % 2)
                for kt in range(KTILES):
                    src = ps[:, b0 + 1 + kt // 4, (kt % 4) * DV:(kt % 4 + 1) * DV]
                    dve.wait_ge(*E4.pe.at(f"s{c}"))
                    if c == 0:
                        dve.tensor_copy(state[:, kt, :], src).then_inc(*E4.dve.done(f"s{c}_{kt}"))
                        continue
                    dve.wait_ge(*E4.dve.at(f"s{c - 1}_{kt}"))
                    dve.wait_ge(*E4.pe.at(f"o{c}"))
                    dve.scalar_tensor_tensor(out=state[:, kt, :], in0=state[:, kt, :], scalar=ebl[:, kt, c:c + 1],
                                             in1=src, op0=ALU.mult, op1=ALU.add).then_inc(*E4.dve.done(f"s{c}_{kt}"))
            for kt in range(KTILES):
                b0 = 4 * (kt % 2)
                dve.wait_ge(*E4.pe.at(f"so{heads_of[kt][-1]}"))
                dve.wait_ge(*loads4[kt % 2].at(f"ss{kt}"))
                if kt >= 1:
                    dve.wait_ge(*E4.pool.at(f"out{kt - 1}"))
                dve.tensor_tensor(snew, sst[:, kt % 2, :, :],
                                  ebl[:, kt, NCE:NCE + NB].unsqueeze(2).to_broadcast([P, NB, DV]), ALU.mult).then_inc(
                    *E4.dve.done(f"sm{kt}"))
                dve.wait_ge(*E4.dve.at(f"sm{kt}"))
                dve.tensor_tensor(snew.rearrange("p (g b) v -> p g (b v)", g=2), snew.rearrange(
                    "p (g b) v -> p g (b v)", g=2), ps[:, b0:b0 + 2, :], ALU.add).then_inc(*E4.dve.done(f"ss{kt}"))

        def pool_chunks(pool):
            pool.wait_ge(mm_ok[0], used["w_out"][0])
            pool.wait_ge(mm_ok[1], used["w_out"][1])

            def sample_state(name, kt):
                if kt < 2:
                    return [(64 * i, 64, a[name[0]][0][:, 2 * kt + i].rearrange("b k v -> k b v")) for i in range(2)]
                return [(0, P, a[name[1]][0][:, kt - 2].rearrange("b k v -> k b v"))]

            def load(kt):
                parts = sample_state(("state_gla", "state_hgrn"), kt)
                for n, (r0, nr, src) in enumerate(parts):
                    d = pool.dma_start(sst[r0:r0 + nr, kt % 2, :, :], src)
                    d.then_inc(*loads4[kt % 2].loaded(f"ss{kt}"))

            load(0)
            load(1)
            pool.wait_ge(*E4.dve.at(f"s{NCE - 1}_{KTILES - 1}"))
            for kt in range(KTILES):
                if kt < 2:
                    dst = o["gla_prompt"][0, 0][2 * kt:2 * kt + 2].rearrange("h k v -> (h k) v")
                else:
                    dst = o["hgrn_prompt"][0, 0][kt - 2]
                pool.dma_start(dst, state[:, kt, :]).then_inc(out_sem, 16)
            for kt in range(KTILES):
                for h in heads_of[kt]:
                    if h >= 2:
                        pool.wait_ge(*E4.pe.at(f"vx{h - 2}"))
                    pool.tensor_tensor(vx[0:TS, h % 2, :, :],
                                       vtok[0:TS, 4, h * DV:(h + 1) * DV].unsqueeze(1).to_broadcast([TS, NB, DV]),
                                       batE[0:TS, :].unsqueeze(2).to_broadcast([TS, NB, DV]), ALU.mult).then_inc(
                        *E4.pool.done(f"vx{h}"))
                pool.wait_ge(*E4.dve.at(f"ss{kt}"))
                for r0, nr, dst in sample_state_out(kt):
                    pool.dma_start(dst, snew[r0:r0 + nr, :, :]).then_inc(state_out, 16)
                pool.wait_ge(state_out, 16 * state_outs[kt])
                pool.nop().then_inc(*E4.pool.done(f"out{kt}"))
                if kt + 2 < KTILES:
                    load(kt + 2)

        state_out, out_sem = sem("sample_states_out"), sem("outputs_out")
        state_outs = [2, 4, 5, 6, 7, 8]

        def sample_state_out(kt):
            if kt < 2:
                return [(64 * i, 64, o["gla_sample"][0][:, 2 * kt + i].rearrange("b k v -> k b v")) for i in range(2)]
            return [(0, P, o["hgrn_sample"][0][:, kt - 2].rearrange("b k v -> k b v"))]

        def act_gate(act):
            act.wait_ge(*E4.act.at("os"))
            for h in range(8):
                if h >= 2:
                    act.wait_ge(*E5.pe.at(f"m{h - 2}"))
                act.activation(sq[:, h % 2, :], oT[:, h, :], ACT.Square).then_inc(*E5.act.done(f"sq{h}"))
                act.wait_ge(*E5.pe.at(f"m{h}"))
                if h >= 2:
                    act.wait_ge(*E5.dve.at(f"n{h - 2}"))
                act.activation(two(rstd[:, h % 2, :]), ps[:, 4 + 2 * (h % 2):6 + 2 * (h % 2), 0:TH], ACT.Sqrt,
                               bias=eps_rms, scale=1.0 / DV).then_inc(*E5.act.done(f"m{h}"))
                if h >= 1:
                    head(act, h - 1)
            head(act, 7)

        def head(act, h):
            act.wait_ge(*E5.dve.at(f"y{h}"))
            act.activation(xh[:, h, :], nrm[:, h % 2, :], ACT.Copy).then_inc(*E5.act.done(f"h{h}"))

        def pe_gate(pe):
            for h in range(8):
                pe.wait_ge(*E5.act.at(f"sq{h}"))
                if h == 0:
                    pe.wait_ge(*E4.dve.at(f"ss{KTILES - 1}"))
                if h >= 2:
                    pe.wait_ge(*E5.act.at(f"m{h - 2}"))
                for g in range(2):
                    mm = pe.matmul(ps[:, 4 + 2 * (h % 2) + g, 0:TH], ones[:, :], sq[:, h % 2, g * TH:(g + 1) * TH],
                                   start=True, stop=True)
                mm.then_inc(*E5.pe.done(f"m{h}"))

        def dve_gate(dve):
            dve.wait_ge(*E4.pool.at(f"out{KTILES - 1}"))
            dve.wait_ge(out_sem, 16 * KTILES)
            dve.wait_ge(*E4.act.at("os"))
            for h in range(8):
                gain = col("gla_norm") if h < HA else col("hgrn_norm")
                y = nrm[:, h % 2, :]
                dve.wait_ge(*E5.act.at(f"m{h}"))
                dve.reciprocal(rstd[:, h % 2, :], rstd[:, h % 2, :]).then_inc(*E5.dve.done(f"r{h}"))
                dve.wait_ge(*E5.dve.at(f"r{h}"))
                if h >= 2:
                    dve.wait_ge(*E5.dve.at(f"l{h - 2}"))
                dve.scalar_tensor_tensor(out=y, in0=oT[:, h, :], scalar=gain, in1=rstd[:, h % 2, :], op0=ALU.mult,
                                         op1=ALU.mult).then_inc(*E5.dve.done(f"n{h}"))
                dve.wait_ge(*E5.dve.at(f"n{h}"))
                dve.tensor_tensor(y, y, gate[:, h, :], ALU.mult).then_inc(*E5.dve.done(f"y{h}"))
                dve.wait_ge(*E5.act.at(f"h{h}"))
                dve.tensor_tensor(xl[:, h, :], y, xh[:, h, :].bitcast(F32), ALU.subtract).then_inc(
                    *E5.dve.done(f"l{h}"))

        def add_stage(name, wait_pe):
            n, units = stages[name]

            def pe_part(pe):
                wait_pe(pe)
                pe_stage(pe, name)

            def act_part(act):
                def body(i, last):
                    for s in range(2):
                        act.wait_ge(mm_ok[s], used[name][s] + i + 1)
                        ahead(act_head, act, name, s, i, last)
                each(act, n, name, body)

            def dve_part(dve):
                def body(i, last):
                    for s in range(2):
                        dve.wait_ge(mm_ok[s], used[name][s] + i + 1)
                        h = hT[:, ds(2 * i + s, 1), :].rearrange("p one (h t) -> p (one h) t", h=2)
                        dve.tensor_tensor(h, h, out2(s), ALU.add).then_inc(bank_free[s], 1)
                        ahead(dve_rest, dve, name, s, i, last)
                each(dve, n, name, body)

            return pe_part, act_part, dve_part

        def gate_ready(pe):
            pe.wait_ge(*E5.dve.at("l7"))
            pe.wait_ge(*E5.act.at("h7"))

        out_even = add_stage("w_out", gate_ready)

        silu_ok, prod_ok = sem("ffn_silu"), sem("ffn_product")
        hhead_ok, hrest_ok = sem("hidden_head"), sem("hidden_rest")
        sig_ok, gated_ok, added_ok = sem("ple_sigmoid"), sem("ple_gated"), sem("ple_added")
        ptok = cols(MIXF, 5, PLE)
        pf = cols(MIXF + 5 * PLE, PLE // P, T)
        act_out = cols(MIXF + 5 * PLE + 2 * T, T)
        prod = cols(MIXF + 5 * PLE + 3 * T, T)

        def first_counts(dve):
            for s in (prod_ok, hrest_ok, hhead_ok, gated_ok, added_ok):
                dve.sem_inc(s, 1)

        def tail_of(i):
            S = Section(f"ple_in{i}")
            last = [(bank_free[s], used[f"up{i}0"][s]) for s in range(2)]
            norm_f = Norm(f"ffn{i}", lambda k: col("norm_ffn", 8 * i + k), last, f"up{i}0")
            norm_p = Norm(f"ple{i}", lambda k: col("norm_ple", 8 * i + k),
                          [(bank_free[s], used[f"ple{i}"][s]) for s in range(2)], f"ple{i}")

            def act_in(act):
                for r in last:
                    act.wait_ge(*r)
                act.dma_start(ptok[:, 0:4, :], a["p_prompt"][i, 0].rearrange("(a p) d -> p a d", p=P)).then_inc(
                    *S.dma.loaded("pp"))
                act.dma_start(ptok[0:TS, 4, :], a["p_sample"][i].rearrange("b t d -> (b t) d")).then_inc(
                    *S.dma.loaded("p"))

            def pe_in(pe):
                pe.wait_ge(*S.dma.at("p"))
                for tt in range(5):
                    n = P if tt < 4 else TS
                    bank = 4 + tt if tt < 2 else 6 + tt % 2
                    if tt == 0:
                        pe.wait_ge(*norm_f.s.act.at("mean"))
                    if tt == 4:
                        pe.wait_ge(*S.dve.at("t2"))
                    for k in range(2):
                        mm = pe.transpose(ps[:, bank, k * n:(k + 1) * n], ptok[0:n, tt, k * P:(k + 1) * P],
                                          ident[0:n, 0:n])
                    mm.then_inc(*S.pe.done(f"t{tt}"))

            def dve_in(dve):
                for tt in range(5):
                    n = P if tt < 4 else TS
                    bank = 4 + tt if tt < 2 else 6 + tt % 2
                    dve.wait_ge(*S.pe.at(f"t{tt}"))
                    dve.tensor_copy(pf[:, :, tt * P:tt * P + n],
                                    ps[:, bank, 0:2 * n].rearrange("p (k t) -> p k t", k=2)).then_inc(
                        *S.dve.done(f"t{tt}"))
                dve.wait_ge(*S.act.at("head"))
                dve.tensor_tensor(ple[:, 1, :, :], pf, ple[:, 0, :, :].bitcast(F32), ALU.subtract).then_inc(
                    *S.dve.done("rest"))

            def act_split(act):
                act.wait_ge(*S.dve.at("t4"))
                act.activation(ple[:, 0, :, :], pf, ACT.Copy).then_inc(*S.act.done("head"))

            def up(half):
                name = f"up{i}{half}"
                base = FT * (2 * i + half) + 1

                def pe_part(pe):
                    if half == 0:
                        pe_norm_wait(pe, norm_f)
                    pe_stage(pe, name)

                def act_part(act):
                    def body(j, last):
                        act.wait_ge(mm_ok[0], used[name][0] + j + 1)
                        ahead(act_head, act, name, 0, j, last)
                        act.wait_ge(prod_ok, base + j)
                        act.activation(two(act_out), out2(0), ACT.Silu).then_inc(bank_free[0], 1)
                        act.wait_ge(bank_free[0], used[name][0] + j + 1)
                        act.sem_inc(silu_ok, 1)
                        act.wait_ge(mm_ok[1], used[name][1] + j + 1)
                        ahead(act_head, act, name, 1, j, last)
                        act.wait_ge(prod_ok, base + j + 1)
                        act.activation(hid[:, 0, ds(j, 1), :], prod.unsqueeze(1), ACT.Copy).then_inc(hhead_ok, 1)
                    each(act, FT, name, body)

                def dve_part(dve):
                    def body(j, last):
                        ahead(dve_rest, dve, name, 0, j, last)
                        dve.wait_ge(bank_free[0], used[name][0] + j + 1)
                        dve.wait_ge(mm_ok[1], used[name][1] + j + 1)
                        dve.wait_ge(hrest_ok, base + j)
                        dve.tensor_tensor(two(prod), two(act_out), out2(1), ALU.mult).then_inc(prod_ok, 1)
                        dve.wait_ge(prod_ok, base + j + 1)
                        dve.sem_inc(bank_free[1], 1)
                        ahead(dve_rest, dve, name, 1, j, last)
                        dve.wait_ge(hhead_ok, base + j + 1)
                        dve.tensor_tensor(hid[:, 1, ds(j, 1), :], prod.unsqueeze(1),
                                          hid[:, 0, ds(j, 1), :].bitcast(F32), ALU.subtract).then_inc(hrest_ok, 1)
                    each(dve, FT, name, body)

                return dict(tensor=pe_part, scalar=act_part, vector=dve_part)

            def down(half):
                def hidden(pe):
                    pe.wait_ge(hrest_ok, FT * (2 * i + half + 1) + 1)
                pe_part, act_part, dve_part = add_stage(f"down{i}{half}", hidden)
                return dict(tensor=pe_part, scalar=act_part, vector=dve_part)

            name = f"ple{i}"

            def pe_ple(pe):
                pe_norm_wait(pe, norm_p)
                pe.wait_ge(*S.dve.at("rest"))
                pe_stage(pe, name)

            def act_ple(act):
                def body(j, last):
                    act.wait_ge(mm_ok[0], used[name][0] + j + 1)
                    ahead(act_head, act, name, 0, j, last)
                    act.wait_ge(gated_ok, 8 * i + 1 + j)
                    act.activation(two(act_out), out2(0), ACT.Sigmoid).then_inc(bank_free[0], 1)
                    act.wait_ge(mm_ok[1], used[name][1] + j + 1)
                    ahead(act_head, act, name, 1, j, last)
                each(act, 8, name, body)

            def dve_ple(dve):
                def body(j, last):
                    ahead(dve_rest, dve, name, 0, j, last)
                    dve.wait_ge(bank_free[0], used[name][0] + j + 1)
                    dve.wait_ge(mm_ok[1], used[name][1] + j + 1)
                    dve.wait_ge(added_ok, 8 * i + 1 + j)
                    dve.tensor_tensor(two(prod), two(act_out), out2(1), ALU.mult).then_inc(gated_ok, 1)
                    dve.wait_ge(gated_ok, 8 * i + j + 2)
                    dve.sem_inc(bank_free[1], 1)
                    h = hT[:, ds(j, 1), :]
                    dve.tensor_tensor(h, h, prod.unsqueeze(1), ALU.add).then_inc(added_ok, 1)
                    ahead(dve_rest, dve, name, 1, j, last)
                each(dve, 8, name, body)

            return [dict(scalar=act_in),
                    dict(tensor=lambda e: pe_norm(e, norm_f), scalar=lambda e: act_norm(e, norm_f),
                         vector=lambda e: dve_norm(e, norm_f)),
                    dict(tensor=pe_in, scalar=act_split, vector=dve_in),
                    up(0), down(0), up(1), down(1),
                    dict(tensor=lambda e: pe_norm(e, norm_p), scalar=lambda e: act_norm(e, norm_p),
                         vector=lambda e: dve_norm(e, norm_p)),
                    dict(tensor=pe_ple, scalar=act_ple, vector=dve_ple)]

        tail_parts = [tail_of(0), tail_of(1)]

        F = Section("final")
        ysum = cols(0, 3, T)
        yr = cols(3 * T, T)
        yT = cols(4 * T, KT, T)
        ytok = cols(12 * T, 5, D)

        def act_final(act):
            act.wait_ge(added_ok, 17)
            for k in range(KT):
                if k >= 2:
                    act.wait_ge(*F.dve.at(f"sum{k - 2}"))
                act.activation(ysum[:, k % 2, :], hT[:, k, :], ACT.Square).then_inc(*F.act.done(f"sq{k}"))
            act.wait_ge(*F.pe.at("mean"))
            act.activation(two(ysum[:, 0, :]), ps[:, 4:6, 0:TH], ACT.Sqrt, bias=eps_rms, scale=1.0 / D).then_inc(
                *F.act.done("mean"))
            for j, (tt, half) in enumerate((t, k) for t in range(5) for k in range(2)):
                n = P if tt < 4 else TS
                act.wait_ge(*F.pe.at(f"t{j}"))
                act.activation(ytok[0:n, tt, half * 512:half * 512 + 512], ps[0:n, 4 + j % 4, :], ACT.Copy).then_inc(
                    *F.act.done(f"t{j}"))

        def dve_final(dve):
            dve.wait_ge(added_ok, 17)
            for k in range(KT):
                dve.wait_ge(*F.act.at(f"sq{k}"))
                if k == 0:
                    dve.tensor_copy(ysum[:, 2, :], ysum[:, 0, :]).then_inc(*F.dve.done("sum0"))
                else:
                    dve.wait_ge(*F.dve.at(f"sum{k - 1}"))
                    dve.tensor_tensor(ysum[:, 2, :], ysum[:, 2, :], ysum[:, k % 2, :], ALU.add).then_inc(
                        *F.dve.done(f"sum{k}"))
            dve.wait_ge(*F.act.at("mean"))
            dve.reciprocal(yr, ysum[:, 0, :]).then_inc(*F.dve.done("rstd"))
            dve.wait_ge(*F.dve.at("rstd"))
            for k in range(KT):
                dve.scalar_tensor_tensor(out=yT[:, k, :], in0=hT[:, k, :], scalar=col("norm_final", k), in1=yr,
                                         op0=ALU.mult, op1=ALU.mult).then_inc(*F.dve.done(f"y{k}"))

        def pe_final(pe):
            pe.wait_ge(*F.dve.at(f"sum{KT - 1}"))
            for h in range(2):
                mm = pe.matmul(ps[:, 4 + h, 0:TH], ones[:, :], ysum[:, 2, h * TH:(h + 1) * TH], start=True, stop=True)
            mm.then_inc(*F.pe.done("mean"))
            pe.wait_ge(*F.act.at("mean"))
            pe.wait_ge(*F.dve.at(f"y{KT - 1}"))
            for j, (tt, half) in enumerate((t, k) for t in range(5) for k in range(2)):
                n = P if tt < 4 else TS
                if j >= 4:
                    pe.wait_ge(*F.act.at(f"t{j - 4}"))
                for k in range(4):
                    mm = pe.transpose(ps[0:n, 4 + j % 4, k * P:(k + 1) * P], yT[:, 4 * half + k, tt * P:tt * P + n],
                                      ident[:, :])
                mm.then_inc(*F.pe.done(f"t{j}"))

        def pool_final(pool):
            for tt in range(4):
                pool.wait_ge(*F.act.at(f"t{2 * tt + 1}"))
                pool.dma_start(o["y_prompt"][0, tt * P:(tt + 1) * P, :], ytok[:, tt, :]).then_inc(out_sem, 16)
            pool.wait_ge(*F.act.at("t9"))
            pool.dma_start(o["y_sample"].rearrange("b t d -> (b t) d"), ytok[0:TS, 4, :]).then_inc(out_sem, 16)
            pool.wait_ge(out_sem, 16 * OUTS)
            pool.wait_ge(state_out, 16 * 8)

        O0 = Section("odd_mix")
        O1 = Section("odd_proj")
        O2 = Section("odd_quads")
        O3 = Section("odd_gate")
        kb = mix[:, 0:8704].rearrange("p (i n s t) -> p i n s t", i=KT, n=NCO, s=2)
        qr = mix[:, 8704:17408].rearrange("p (i n s t) -> p i n s t", i=KT, n=NCO, s=2)
        vF = cols(17408, KT, T)
        dx = vF
        xn = cols(21760, KT, T)
        hs = mix[:, 21760:21760 + NB * 512].rearrange("p (b i v) -> p b i v", b=NB, i=KT)
        SC0 = 26112
        ymix = cols(SC0, 2, T)
        t1, t2, e1, e2 = (cols(SC0 + (2 + i) * T, T) for i in range(4))
        gs = cols(SC0 + 6 * T, T)
        omka = mix[:, SC0 + 7 * T:SC0 + 7 * T + KT]
        shT = mix[:, SC0 + 7 * T + 8:SC0 + 7 * T + 88]
        hst = mix[:, SC0:SC0 + 512].rearrange("p (i v) -> p i v", i=KT)
        rb_ = mix[:, SC0 + 512:SC0 + 1536].rearrange("p (g i v) -> p g i v", g=2, i=KT)
        lio = mix[:, SC0 + 1536:SC0 + 1536 + 1024]
        rts = mix[:, SC0 + 2560:SC0 + 3072].rearrange("p (i s t) -> p i s t", i=KT, s=2)
        wc = raw[:, 0, 1024:1024 + KT * 24].rearrange("p (i n) -> p i n", i=KT)
        small = nc.alloc_sbuf_tensor_at("odd_small", [P, 8704], F32, offset=xs_byte)
        w1 = small[:, 0:512].rearrange("p (k n) -> p k n", k=KT)
        a1 = small[:, 512:1024].rearrange("p (k n) -> p k n", k=KT)
        w2, a2 = small[0:64, 1024:2048], small[0:64, 2048:3072]
        lw_, la_ = small[0:64, 3072:3072 + T], small[0:64, 3072 + T:3072 + 2 * T]
        quad = nc.alloc_sbuf_tensor_at("odd_quad", [P, 8704], F32, offset=xs_byte)
        vu = quad[:, 0:2048].rearrange("p (c g i v) -> p c g i v", c=2, g=2, i=KT)
        kbt = quad[:, 2048:4096].rearrange("p (c i k) -> p c i k", c=2, i=KT)
        sc = quad[:, 4096:6144].rearrange("p (c g i t) -> p c g i t", c=2, g=2, i=KT)
        aT, xT, xx, bT, pp = (quad[:, 6144 + 512 * i:6144 + 512 * (i + 1)] for i in range(5))
        vux = quad[0:64, 4096 + 1024:4096 + 2048]
        g2s = nc.alloc_sbuf_tensor_at("odd_gate_w", [P, 8704], F32, offset=xs_byte)
        resetO = tab[:, 0:T]
        s16 = tab[0:HC, 0:T]
        same = tab[:, 544:672]
        lvO = tab[:, 672:832].rearrange("p (l t) -> p l t", l=5)
        scm = tab[:, 832:960].rearrange("p (m t) -> p m t", m=2)
        hsel = tab[:, 960:1088].rearrange("p (k h) -> p k h", k=KT)
        batO = tab[:, 1088:1096]
        chunked = lambda ap: ap.rearrange("p (n t) -> p n t", t=CO)

        norm_o = Norm("mix1", lambda k: col("norm_mix", 8 + k), [(added_ok, 9)], "rw_r")

        def act_mix(act):
            act.wait_ge(added_ok, 9)
            for i in range(2):
                act.wait_ge(mm_ok[i], used["rw_r"][i])
            act.dma_start(tab[:, 0:1096], a["odd_tables"]).then_inc(*O0.dma.loaded("tab"))
            act.dma_start(w1, a["rw_w1"][0].rearrange("(k p) n -> p k n", p=P)).then_inc(*O0.dma.loaded("w1"))
            act.dma_start(a1, a["rw_a1"][0].rearrange("(k p) n -> p k n", p=P)).then_inc(*O0.dma.loaded("a1"))
            act.dma_start(w2, a["rw_w2"][0]).then_inc(*O0.dma.loaded("w2"))
            act.dma_start(a2, a["rw_a2"][0]).then_inc(*O0.dma.loaded("all"))

        def act_mix2(act):
            act.wait_ge(*O0.pe.at(f"mix{KT - 1}"))
            act.activation(lw_.rearrange("p (h t) -> p h t", h=2), ps[0:64, 4:6, 0:TH], ACT.Tanh).then_inc(
                *O0.act.done("lw"))
            act.wait_ge(*O0.pe.at(f"mix{2 * KT - 1}"))
            act.activation(la_.rearrange("p (h t) -> p h t", h=2), ps[0:64, 6:8, 0:TH], ACT.Copy).then_inc(
                *O0.act.done("la"))
            for i in range(KT):
                act.wait_ge(*O0.pe.at(f"w2{i}"))
                b0 = 2 * (i % 2)
                if i >= 2:
                    act.wait_ge(*O0.dve.at(f"a{i - 2}"))
                act.activation(two((t1, t2)[i % 2]), ps[:, b0:b0 + 2, 0:TH], ACT.Sigmoid, bias=col("rw_w0", i)).then_inc(
                    *O0.act.done(f"w{i}"))
                act.wait_ge(*O0.pe.at(f"a2{i}"))
                act.activation(two((e1, e2)[i % 2]), ps[:, 4 + b0:6 + b0, 0:TH], ACT.Sigmoid, bias=col("rw_a0", i)).then_inc(
                    *O0.act.done(f"a{i}"))

        def dve_mix(dve):
            dve.wait_ge(*norm_o.s.dve.at(f"y{KT - 1}"))
            pr = TP - 1
            dve.tensor_tensor(dx[:, :, 1:TP], xn[:, :, 0:pr], xn[:, :, 1:TP], ALU.subtract)
            dve.tensor_scalar(dx[:, :, 0:1], xn[:, :, 0:1], -1.0, None, ALU.mult)
            ends = xn[:, :, TP - 1:TP]
            dve.tensor_copy(shT[:, 0:KT].unsqueeze(2), ends)
            last = vec[:, 1, VCOL["state_shift"][1]:VCOL["state_shift"][1] + 64].rearrange("p (b k) -> p k b", k=KT)
            for k in range(KT):
                x4 = xn[:, k, TP:T].rearrange("p (b t) -> p b t", t=ST)
                d4 = dx[:, k, TP:T].rearrange("p (b t) -> p b t", t=ST)
                dve.tensor_tensor(d4[:, :, 1:ST], x4[:, :, 0:ST - 1], x4[:, :, 1:ST], ALU.subtract)
                dve.tensor_tensor(d4[:, :, 0], last[:, k, :], x4[:, :, 0], ALU.subtract)
                mm = dve.tensor_copy(shT[:, KT:KT + 64].rearrange("p (b k) -> p k b", k=KT)[:, k, :],
                                     x4[:, :, ST - 1])
            mm.then_inc(*O0.dve.done("dx"))
            dve.wait_ge(*O0.dve.at("dx"))
            dve.tensor_scalar(omka, vec[:, 1, VCOL["rw_ka"][1]:VCOL["rw_ka"][1] + KT], -1.0, 1.0, ALU.mult,
                              ALU.add).then_inc(*O0.dve.done("omka"))
            for m, name in ((1, "lw"), (4, "la")):
                for k in range(KT):
                    j = (0 if m == 1 else KT) + k
                    if j >= 2:
                        dve.wait_ge(*O0.pe.at(f"mix{j - 2}"))
                    dve.scalar_tensor_tensor(out=ymix[:, k % 2, :], in0=dx[:, k, :], scalar=col("rw_mu", 8 * m + k),
                                             in1=xn[:, k, :], op0=ALU.mult, op1=ALU.add).then_inc(
                        *O0.dve.done(f"mix{j}"))
            dve.wait_ge(*O0.pe.at("shift"))
            dve.tensor_copy(lioS, ps[0:72, 3, 0:P]).then_inc(*O0.dve.done("shift"))
            for i in range(KT):
                t, u = (t1, t2)[i % 2], (e1, e2)[i % 2]
                dve.wait_ge(*O0.act.at(f"w{i}"))
                dve.tensor_scalar(qr[:, i, :, 0, :], chunked(t), -float(np.exp(-0.5)), None, ALU.mult).then_inc(
                    *O0.dve.done(f"lw{i}"))
                dve.tensor_scalar(t, t, -float(np.exp(-0.5)), None, ALU.mult).then_inc(*O0.dve.done(f"lt{i}"))
                dve.wait_ge(*O0.dve.at(f"lt{i}"))
                dve.tensor_tensor_scan(t, resetO, t, 0.0, ALU.mult, ALU.add).then_inc(*O0.dve.done(f"b{i}"))
                dve.wait_ge(*O0.dve.at(f"b{i}"))
                dve.tensor_copy(qr[:, i, :, 1, :], chunked(t))
                dve.wait_ge(*O0.act.at(f"a{i}"))
                dve.tensor_copy(kb[:, i, :, 0, :], chunked(u)).then_inc(*O0.dve.done(f"a{i}"))

        def pe_mix(pe):
            pe.wait_ge(*O0.dma.at("all"))
            pe.wait_ge(*norm_o.s.act.at("mean"))
            for m, w in enumerate((w1, a1)):
                for k in range(KT):
                    j = m * KT + k
                    pe.wait_ge(*O0.dve.at(f"mix{j}"))
                    for h in range(2):
                        mm = pe.matmul(ps[0:64, 4 + 2 * m + h, 0:TH], w[:, k, :], ymix[:, k % 2, h * TH:(h + 1) * TH],
                                       start=k == 0, stop=k == KT - 1)
                    mm.then_inc(*O0.pe.done(f"mix{j}"))
            for s in range(2):
                pe.wait_ge(bank_free[s], used["rw_r"][s])
            pe.transpose(ps[0:72, 3, 0:P], shT[:, 0:72], ident[:, :]).then_inc(*O0.pe.done("shift"))
            pe.wait_ge(*O0.dve.at("shift"))
            pe.wait_ge(*O0.act.at("la"))
            for i in range(KT):
                b0 = 2 * (i % 2)
                if i >= 2:
                    pe.wait_ge(*O0.act.at(f"a{i - 2}"))
                for w, x, b, name in ((w2, lw_, b0, "w2"), (a2, la_, 4 + b0, "a2")):
                    for h in range(2):
                        mm = pe.matmul(ps[:, b + h, 0:TH], w[:, i * P:(i + 1) * P], x[:, h * TH:(h + 1) * TH],
                                       start=True, stop=True)
                    mm.then_inc(*O0.pe.done(f"{name}{i}"))

        lioS = small[0:72, 4224:4352]

        def pool_shift(pool):
            pool.wait_ge(*O0.dve.at("shift"))
            pool.dma_start(o["shift_prompt"].rearrange("i b (k c) -> (i b k) c", c=P), lioS[0:KT, :]).then_inc(out_sem, 16)
            pool.dma_start(o["shift_sample"].rearrange("i b (k c) -> (i b k) c", c=P), lioS[KT:72, :]).then_inc(
                out_sem, 16)

        mixes = {"rw_r": 0, "rw_k": 2, "rw_g1": 5, "rw_v": 3}
        seq = ["rw_r", "rw_k", "rw_g1", "rw_v"]

        def dve_x(dve, name):
            if name == seq[0]:
                dve.wait_ge(*O0.act.at(f"a{KT - 1}"))
                dve.wait_ge(out_sem, 16 * (KTILES + 2))
                dve.wait_ge(*O0.pe.at(f"mix{2 * KT - 1}"))
            for s in range(2):
                dve.wait_ge(mm_ok[s], used[name][s])
            for k in range(KT):
                y = ymix[:, k % 2, :]
                if k >= 2:
                    dve.wait_ge(*O1.dve.at(f"{name}l{k - 2}"))
                elif name != seq[0]:
                    dve.wait_ge(*O1.dve.at(f"{seq[seq.index(name) - 1]}l{KT - 2 + k}"))
                dve.scalar_tensor_tensor(out=y, in0=dx[:, k, :], scalar=col("rw_mu", 8 * mixes[name] + k),
                                         in1=xn[:, k, :], op0=ALU.mult, op1=ALU.add).then_inc(
                    *O1.dve.done(f"{name}y{k}"))
                dve.wait_ge(*O1.act.at(f"{name}h{k}"))
                dve.tensor_tensor(xl[:, k, :], y, xh[:, k, :].bitcast(F32), ALU.subtract).then_inc(
                    *O1.dve.done(f"{name}l{k}"))

        def act_x(act, name):
            for k in range(KT):
                act.wait_ge(*O1.dve.at(f"{name}y{k}"))
                act.activation(xh[:, k, :], ymix[:, k % 2, :], ACT.Copy).then_inc(*O1.act.done(f"{name}h{k}"))

        def pe_x(pe, name):
            pe.wait_ge(*O1.dve.at(f"{name}l{KT - 1}"))
            pe_stage(pe, name)

        def units_of(name):
            n, units = stages[name]
            return [(i, s, len(units) * i + s, i == n - 1) for i in range(n) for s in range(len(units))]

        def plain(eng_split, name):
            def run(eng):
                for i, s, t, last in units_of(name):
                    eng.wait_ge(mm_ok[s], used[name][s] + i + 1)
                    ahead(eng_split, eng, name, s, i, last)
            return run

        def dve_r(dve):
            for i, s, t, last in units_of("rw_r"):
                dve.wait_ge(mm_ok[s], used["rw_r"][s] + i + 1)
                ahead(dve_rest, dve, "rw_r", s, i, last)

        def act_r(act):
            for i, s, t, last in units_of("rw_r"):
                act.wait_ge(mm_ok[s], used["rw_r"][s] + i + 1)
                ahead(act_head, act, "rw_r", s, i, last)
                act.activation(kb[:, t, 0:8, 1, :], chunked(ps[:, 2 * s, 0:256]), ACT.Copy)
                act.activation(kb[:, t, 8, 1, 0:16], ps[:, 2 * s, 256:272], ACT.Copy)
                act.activation(kb[:, t, 8, 1, 16:32], ps[:, 2 * s + 1, 0:16], ACT.Copy)
                act.activation(kb[:, t, 9:17, 1, :], chunked(ps[:, 2 * s + 1, 16:272]), ACT.Copy).then_inc(
                    bank_free[s], 1)

        def act_k(act):
            for i, s, t, last in units_of("rw_k"):
                act.wait_ge(mm_ok[s], used["rw_k"][s] + i + 1)
                ahead(act_head, act, "rw_k", s, i, last)
                if t > 0:
                    act.wait_ge(*O1.dve.at(f"end{t - 1}"))
                act.activation(two(t1), out2(s), ACT.Copy, scale=col("rw_kk", t))
                act.activation(two(e1), out2(s), ACT.Square, scale=col("rw_kk", t)).then_inc(*O1.act.done(f"sq{t}"))
                act.wait_ge(*O1.dve.at(f"nn{t}"))
                act.activation(e2, e2, ACT.Ln, scale=float(2.0 ** 17)).then_inc(*O1.act.done(f"ln{t}"))
                act.wait_ge(*O1.act.at(f"ln{t}"))
                act.activation(e2, e2, ACT.Exp, scale=-0.5, bias=bias17).then_inc(*O1.act.done(f"rs{t}"))
                act.wait_ge(*O1.dve.at(f"d{t}"))
                act.activation(e1, e1, ACT.Exp).then_inc(*O1.act.done(f"e1{t}"))
                act.wait_ge(*O1.dve.at(f"kn{t}"))
                act.activation(chunked(e2), qr[:, t, :, 1, :], ACT.Exp, scale=-1.0).then_inc(*O1.act.done(f"e2{t}"))
                act.wait_ge(*O1.dve.at(f"kk{t}"))
                act.activation(chunked(e1), qr[:, t, :, 1, :], ACT.Exp).then_inc(*O1.act.done(f"e3{t}"))

        def pe_k(pe):
            pe.wait_ge(*O1.dve.at(f"rw_kl{KT - 1}"))
            n, units = stages["rw_k"]
            pe.wait_ge(*O0.act.at(f"a{KT - 1}"))
            for i, s, t, last in units_of("rw_k"):
                unit_products(pe, "rw_k", i, s)
                if t > 0:
                    k_sums(pe, t - 1)
            k_sums(pe, KT - 1)

        def k_sums(pe, t):
            pe.wait_ge(*O1.act.at(f"sq{t}"))
            for h in range(2):
                mm = pe.matmul(ps[:, 4 + h, 0:TH], same, e1[:, h * TH:(h + 1) * TH], start=True, stop=True)
            mm.then_inc(*O1.pe.done(f"nn{t}"))
            pe.wait_ge(*O1.dve.at(f"s{t}"))
            for h in range(2):
                mm = pe.matmul(ps[0:HC, 6 + h, 0:TH], hsel[:, t, :], t2s[:, h * TH:(h + 1) * TH], start=t == 0,
                               stop=t == KT - 1)
            mm.then_inc(*O1.pe.done(f"s{t}"))

        t2s = ymix[:, 0, :]

        def dve_k(dve):
            for i, s, t, last in units_of("rw_k"):
                dve.wait_ge(mm_ok[s], used["rw_k"][s] + i + 1)
                ahead(dve_rest, dve, "rw_k", s, i, last)
                dve.wait_ge(*O1.pe.at(f"nn{t}"))
                dve.tensor_scalar(two(e2), ps[:, 4:6, 0:TH], 1e-24, None, ALU.max).then_inc(*O1.dve.done(f"nn{t}"))
                dve.tensor_tensor(chunked(e1), qr[:, t, :, 1, :], qr[:, t, :, 0, :], ALU.subtract).then_inc(
                    *O1.dve.done(f"d{t}"))
                dve.tensor_scalar(chunked(t2), kb[:, t, :, 0, :], col("rw_ka", t), omka[:, t:t + 1], ALU.mult,
                                  ALU.add).then_inc(*O1.dve.done(f"f{t}"))
                dve.wait_ge(*O1.dve.at(f"f{t}"))
                dve.tensor_tensor(two(t2), two(t2), out2(s), ALU.mult).then_inc(*O1.dve.done(f"kp{t}"))
                dve.wait_ge(*O1.dve.at(f"kp{t}"))
                dve.wait_ge(*O1.act.at(f"sq{t}"))
                dve.sem_inc(bank_free[s], 1)
                if t > 0:
                    dve.wait_ge(*O1.pe.at(f"s{t - 1}"))
                dve.scalar_tensor_tensor(out=chunked(t2s), in0=chunked(t2), scalar=col("rw_rk", t),
                                         in1=kb[:, t, :, 1, :], op0=ALU.mult, op1=ALU.mult).then_inc(
                    *O1.dve.done(f"s{t}"))
                dve.wait_ge(*O1.act.at(f"rs{t}"))
                dve.tensor_tensor(t1, t1, e2, ALU.mult).then_inc(*O1.dve.done(f"kn{t}"))
                dve.wait_ge(*O1.act.at(f"e1{t}"))
                dve.wait_ge(*O1.dve.at(f"kn{t}"))
                dve.tensor_tensor(qr[:, t, :, 0, :], chunked(t1), chunked(e1), ALU.mult).then_inc(
                    *O1.dve.done(f"kk{t}"))
                dve.tensor_tensor(chunked(t1), chunked(t1), kb[:, t, :, 0, :], ALU.mult).then_inc(
                    *O1.dve.done(f"be{t}"))
                dve.wait_ge(*O1.act.at(f"e3{t}"))
                dve.wait_ge(*O1.dve.at(f"be{t}"))
                dve.tensor_tensor(qr[:, t, :, 1, :], kb[:, t, :, 1, :], chunked(e1), ALU.mult).then_inc(
                    *O1.dve.done(f"r{t}"))
                dve.tensor_copy(wc[:, t, 0:16], chunked(e1)[:, 0:16, CO - 1])
                dve.tensor_copy(wc[:, t, 16:24], e1[:, TP:T].rearrange("p (b t) -> p b t", t=ST)[:, :, ST - 1])
                dve.tensor_tensor(kb[:, t, :, 0, :], chunked(t2), chunked(e2), ALU.mult)
                dve.wait_ge(*O1.dve.at(f"r{t}"))
                dve.tensor_tensor(kb[:, t, :, 1, :], chunked(t1), chunked(e2), ALU.mult).then_inc(
                    *O1.dve.done(f"end{t}"))
            dve.wait_ge(*O1.pe.at(f"s{KT - 1}"))
            dve.tensor_copy(two(s16), ps[0:HC, 6:8, 0:TH]).then_inc(*O1.dve.done("s16"))

        def act_g1(act):
            for i, s, t, last in units_of("rw_g1"):
                act.wait_ge(mm_ok[s], used["rw_g1"][s] + i + 1)
                ahead(act_head, act, "rw_g1", s, i, last)
                act.activation(two(gs), out2(s), ACT.Sigmoid).then_inc(bank_free[s], 1)

        def dve_v(dve):
            for i, s, t, last in units_of("rw_v"):
                dve.wait_ge(mm_ok[s], used["rw_v"][s] + i + 1)
                ahead(dve_rest, dve, "rw_v", s, i, last)
                if t == 0:
                    dve.wait_ge(*O1.dve.at(f"rw_vl{KT - 1}"))
                dve.tensor_copy(two(vF[:, t, :]), out2(s)).then_inc(bank_free[s], 1)

        odd_parts = [
            dict(scalar=act_mix),
            dict(tensor=lambda e: pe_norm(e, norm_o), scalar=lambda e: act_norm(e, norm_o, False),
                 vector=lambda e: dve_norm(e, norm_o, False)),
            dict(tensor=pe_mix, scalar=act_mix2, vector=dve_mix, gpsimd=pool_shift),
            dict(tensor=lambda e: pe_x(e, "rw_r"), scalar=lambda e: (act_x(e, "rw_r"), act_r(e)),
                 vector=lambda e: (dve_x(e, "rw_r"), dve_r(e))),
            dict(tensor=pe_k, scalar=lambda e: (act_x(e, "rw_k"), act_k(e)),
                 vector=lambda e: (dve_x(e, "rw_k"), dve_k(e))),
            dict(tensor=lambda e: pe_x(e, "rw_g1"), scalar=lambda e: (act_x(e, "rw_g1"), act_g1(e)),
                 vector=lambda e: (dve_x(e, "rw_g1"), plain(dve_rest, "rw_g1")(e))),
            dict(tensor=lambda e: pe_x(e, "rw_v"), scalar=lambda e: (act_x(e, "rw_v"), plain(act_head, "rw_v")(e)),
                 vector=lambda e: (dve_x(e, "rw_v"), dve_v(e))),
        ]

        QUADS = TP // P
        slot_in = [sem("state_in_even"), sem("state_in_odd")]
        slot_out = [sem("state_out_even"), sem("state_out_odd")]
        id32 = mix[:, SC0 + 3072:SC0 + 3072 + CO]
        spread = mix[0:HC, D:2 * D]
        g2 = mix[:, 0:D]
        heads2 = [(g, i) for i in range(KT) for g in range(2)]

        def quad_shape(q):
            return (list(range(4)), P, 2, P) if q < QUADS else ([0], 64, 1, TS)

        def spots(q):
            js, _, ncp, _ = quad_shape(q)
            return [(2 * par + g, cp, g, i) for cp in range(ncp) for i in range(KT) for par in range(min(2, len(js)))
                    for g in range(2)]

        def level_count(q):
            return 5 if q < QUADS else 2

        def blocks(ap, q):
            js, pr, ncp, _ = quad_shape(q)
            return ap[0:pr, 0:256 * ncp].rearrange("p (c t) -> p c t", t=CO)

        def at_block(ap, tile, cp, i):
            c = (cp * KT + i) * CO
            return ap[32 * tile:32 * tile + 32, c:c + CO]

        def pe_quad(pe, q):
            js, pr, ncp, nt = quad_shape(q)
            first = q == 0
            if first:
                for s in range(2):
                    pe.wait_ge(bank_free[s], used["rw_o"][s])
                pe.wait_ge(*O1.dve.at("s16"))
            else:
                pe.wait_ge(*O2.dve.at(f"H{4 * q - 1}"))
                pe.wait_ge(*O2.act.at(f"o{4 * q - 1}"))
            for cp in range(ncp):
                for g in range(2):
                    for par in range(min(2, len(js))):
                        n = 4 * q + 2 * cp + par
                        for i in range(KT):
                            mm = pe.matmul(ps[64 * par:64 * par + 64, 2 * cp + g, i * 64:(i + 1) * 64],
                                           kb[64 * g:64 * g + 64, i, n, :, :], qr[64 * g:64 * g + 64, i, n, :, :],
                                           start=True, stop=True)
                    mm.then_inc(*O2.pe.done(f"sc{q}{cp}{g}"))
            for b in range(2):
                for i in range(4):
                    mm = pe.transpose(ps[0:nt, 4 + b, i * P:(i + 1) * P], vF[:, 4 * b + i, q * P:q * P + nt], ident[:, :])
                mm.then_inc(*O2.pe.done(f"vt{q}{b}"))
            for j, (cp, half) in enumerate((c, h) for c in range(ncp) for h in range(2)):
                bank = (6, 7, 4, 5)[j]
                if j == 2:
                    pe.wait_ge(*O2.act.at(f"vt{q}"))
                    pe.wait_ge(*O2.dve.at(f"vt{q}"))
                n = 4 * q + 2 * cp
                for i in range(4):
                    mm = pe.transpose(ps[0:pr, bank, i * P:(i + 1) * P], kb[:, 4 * half + i, n:n + (pr // 64), :, :],
                                      ident[:, :])
                mm.then_inc(*O2.pe.done(f"kt{q}{j}"))
            if q == QUADS:
                pe_rts(pe)
            for level in range(2, level_count(q) + 1):
                pe.wait_ge(*O2.dve.at(f"b{q}{level}"))
                for k, (tile, cp, g, i) in enumerate(spots(q)):
                    mm = pe.matmul(at_block(ps[:, 0, :], tile, cp, i), at_block(bT, tile, cp, i),
                                   at_block(xx, tile, cp, i), start=True, stop=True)
                mm.then_inc(*O2.pe.done(f"P{q}{level}"))
                pe.wait_ge(*O2.act.at(f"P{q}{level}"))
                for k, (tile, cp, g, i) in enumerate(spots(q)):
                    mm = pe.matmul(at_block(ps[:, 1, :], tile, cp, i), at_block(pp, tile, cp, i),
                                   at_block(xT, tile, cp, i), start=True, stop=True)
                mm.then_inc(*O2.pe.done(f"X{q}{level}"))
            pe.wait_ge(*O2.act.at(f"kt{q}"))
            pe.wait_ge(*O2.dve.at(f"x{q}{level_count(q)}"))
            for j in js:
                pe_chunk(pe, q, j)

        def pe_chunk(pe, q, j):
            n, cp, par = 4 * q + j, j // 2, j % 2
            rb, sample = 64 * par, q == QUADS
            for g in range(2):
                for i in range(KT):
                    mm = pe.matmul(ps[rb + 32 * g:rb + 32 * g + 32, 2 + g, i * NC:(i + 1) * NC],
                                   sc[rb:rb + 32, cp, g, i, 0:CO], vu[rb:rb + 32, cp, g, i, :],
                                   start=i == 0, stop=False, skip_group_check=True)
            mm.then_inc(*O2.pe.done(f"av{n}" if n else "R0"))
            if sample:
                pe.wait_ge(*O2.dve.at("rts"))
            elif n > 0:
                pe.wait_ge(*O2.dve.at(f"H{n - 1}"))
                pe.wait_ge(*O2.act.at(f"o{n - 1}"))
            if n > 0:
                pe.wait_ge(*O2.pe.at(f"av{n}"))
                for g in range(2):
                    r = slice(64 * g, 64 * g + 64)
                    for i in range(KT):
                        w = rts[r, i, 0, :] if sample else qr[r, i, n, 0, :]
                        x = ident[r, r] if sample else hst[r, i, :]
                        mm = pe.matmul(ps[rb + 32 * g:rb + 32 * g + 32, 2 + g, i * NC:(i + 1) * NC], w, x, start=False,
                                       stop=True, skip_group_check=True)
                mm.then_inc(*O2.pe.done(f"R{n}"))
                for g in range(2):
                    r = slice(64 * g, 64 * g + 64)
                    for i in range(KT):
                        w = ident[r, r] if sample else hst[r, i, :]
                        x = rts[r, i, 1, :] if sample else qr[r, i, n, 1, :]
                        pe.matmul(ps[r, 6, i * CO:(i + 1) * CO], w, x, start=i == 0, stop=False, skip_group_check=True)
            pe.wait_ge(*O2.act.at(f"R{n}"))
            pe.wait_ge(*O2.dve.at(f"R{n}"))
            for i in range(KT):
                for g in range(2):
                    rows_g = slice(rb + 32 * g, rb + 32 * g + 32)
                    mm = pe.matmul(ps[rb + 32:rb + 64, 4 + g, i * NC:(i + 1) * NC], at_block(xT, 2 * par + g, cp, i),
                                   rb_[rows_g, g, i, :], start=True, stop=True)
            mm.then_inc(*O2.pe.done(f"U{n}"))
            pe.wait_ge(*O2.act.at(f"U{n}"))
            pe.wait_ge(*O2.dve.at(f"U{n}"))
            r = slice(rb, rb + 64)
            if not sample:
                for i in range(KT):
                    for g in range(2):
                        mm = pe.matmul(ps[64 * g:64 * g + 64, 7, i * NC:(i + 1) * NC],
                                       kbt[r, cp, i, g * NC:(g + 1) * NC], vu[r, cp, g, i, :], start=True, stop=True)
                mm.then_inc(*O2.pe.done(f"H{n}"))
            for i in range(KT):
                for g in range(2):
                    mm = pe.matmul(ps[64 * g:64 * g + 64, 6, i * CO:(i + 1) * CO], vu[r, cp, g, i, :],
                                   sc[r, cp, g, i, CO:2 * CO], start=n == 0 and i == 0, stop=True,
                                   skip_group_check=True)
            mm.then_inc(*O2.pe.done(f"o{n}"))

        def act_quad(act, q):
            js, pr, ncp, nt = quad_shape(q)
            act.wait_ge(*O2.pe.at(f"vt{q}0"))
            for j in js:
                act.activation(vu[64 * (j % 2):64 * (j % 2) + 32, j // 2, :, 0:4, :].rearrange("p g i v -> p i g v"),
                               ps[32 * j:32 * j + 32, 4, :].rearrange("p (i g v) -> p i g v", i=4, g=2),
                               ACT.Copy).then_inc(*O2.act.done(f"vt{q}" if j == js[-1] else f"vt{q}_{j}"))
            for j in range(2 * ncp):
                act.wait_ge(*O2.pe.at(f"kt{q}{j}"))
                act.activation(kbt[0:pr, j // 2, 4 * (j % 2):4 * (j % 2) + 4, :],
                               ps[0:pr, (6, 7, 4, 5)[j], :].rearrange("p (i k) -> p i k", i=4),
                               ACT.Copy).then_inc(*O2.act.done(f"kt{q}" if j == 2 * ncp - 1 else f"kt{q}_{j}"))
            for level in range(2, level_count(q) + 1):
                act.wait_ge(*O2.pe.at(f"P{q}{level}"))
                act.activation(pp[0:pr, 0:256 * ncp], ps[0:pr, 0, 0:256 * ncp], ACT.Copy).then_inc(
                    *O2.act.done(f"P{q}{level}"))
            for j in js:
                n, rb, cp = 4 * q + j, 64 * (j % 2), j // 2
                act.wait_ge(*O2.pe.at(f"R{n}"))
                act.activation(rb_[rb:rb + 32, 0, :, :], ps[rb:rb + 32, 2, :].rearrange("p (i v) -> p i v", i=KT),
                               ACT.Copy).then_inc(*O2.act.done(f"R{n}"))
                act.wait_ge(*O2.pe.at(f"U{n}"))
                act.activation(vu[rb + 32:rb + 64, cp, 0, :, :],
                               ps[rb + 32:rb + 64, 4, :].rearrange("p (i v) -> p i v", i=KT), ACT.Copy,
                               scale=-1.0).then_inc(*O2.act.done(f"U{n}"))
                act.wait_ge(*O2.pe.at(f"o{n}"))
                act.activation(qr[:, :, n, 0, :], ps[:, 6, 0:256].rearrange("p (i t) -> p i t", i=KT),
                               ACT.Copy).then_inc(*O2.act.done(f"o{n}"))

        def dve_quad(dve, q):
            js, pr, ncp, nt = quad_shape(q)
            if q == 0:
                for k in range(4):
                    r = slice(32 * k, 32 * k + 32)
                    mm = dve.tensor_copy(id32[r, :], ident[r, r])
                mm.then_inc(*O2.dve.done("id32"))
                dve.wait_ge(*O2.dve.at("id32"))
            for cp in range(ncp):
                for g in range(2):
                    dve.wait_ge(*O2.pe.at(f"sc{q}{cp}{g}"))
                    dve.tensor_tensor(sc[0:pr, cp, g, :, :], ps[0:pr, 2 * cp + g, :].rearrange("p (i t) -> p i t", i=KT),
                                      scm[0:pr, q // QUADS, :].unsqueeze(1).to_broadcast([pr, KT, 64]),
                                      ALU.mult).then_inc(*O2.dve.done(f"sc{q}{cp}{g}"))
            dve.wait_ge(*O2.pe.at(f"vt{q}1"))
            for j in js:
                dve.tensor_copy(vu[64 * (j % 2):64 * (j % 2) + 32, j // 2, :, 4:8, :].rearrange("p g i v -> p i g v"),
                                ps[32 * j:32 * j + 32, 5, :].rearrange("p (i g v) -> p i g v", i=4, g=2)).then_inc(
                    *O2.dve.done(f"vt{q}" if j == js[-1] else f"vt{q}_{j}"))
            dve.wait_ge(*O2.dve.at(f"vt{q}"))
            for par in range(min(2, len(js))):
                for g in range(2):
                    k = 2 * par + g
                    dve.tensor_copy(aT[32 * k:32 * k + 32, 0:256 * ncp].rearrange("p (c i t) -> p c i t", c=ncp, i=KT),
                                    sc[64 * par + 32:64 * par + 64, 0:ncp, g, :, 0:CO]).then_inc(
                        *O2.dve.done(f"aT{q}{k}"))
            dve.wait_ge(*O2.dve.at(f"aT{q}{k}"))
            nb = 8 * ncp

            def halving(level):
                return lvO[0:pr, level - 1, :].unsqueeze(1).to_broadcast([pr, nb, CO])

            dve.tensor_tensor(blocks(bT, q), blocks(aT, q), halving(1), ALU.mult).then_inc(*O2.dve.done(f"b{q}1"))
            dve.wait_ge(*O2.dve.at(f"b{q}1"))
            dve.tensor_tensor(blocks(xT, q), id32[0:pr].unsqueeze(1).to_broadcast([pr, nb, CO]), blocks(bT, q),
                              ALU.subtract).then_inc(*O2.dve.done(f"x{q}1"))
            for level in range(2, level_count(q) + 1):
                dve.wait_ge(*O2.dve.at(f"x{q}{level - 1}"))
                dve.transpose(xx[0:pr, 0:32 * nb], xT[0:pr, 0:32 * nb])
                dve.tensor_tensor(blocks(bT, q), blocks(aT, q), halving(level), ALU.mult).then_inc(
                    *O2.dve.done(f"b{q}{level}"))
                dve.wait_ge(*O2.pe.at(f"X{q}{level}"))
                dve.tensor_tensor(xT[0:pr, 0:32 * nb], xT[0:pr, 0:32 * nb], ps[0:pr, 1, 0:32 * nb],
                                  ALU.subtract).then_inc(*O2.dve.done(f"x{q}{level}"))
            if q == QUADS:
                dve.wait_ge(*O2.pe.at("rts"))
                dve.tensor_copy(rts, ps[:, 7, :].rearrange("p (i s t) -> p i s t", i=KT, s=2)).then_inc(
                    *O2.dve.done("rts"))
            for j in js:
                n, rb, cp = 4 * q + j, 64 * (j % 2), j // 2
                dve.wait_ge(*O2.pe.at(f"R{n}"))
                dve.tensor_copy(rb_[rb + 32:rb + 64, 1, :, :],
                                ps[rb + 32:rb + 64, 3, :].rearrange("p (i v) -> p i v", i=KT)).then_inc(
                    *O2.dve.done(f"R{n}"))
                dve.wait_ge(*O2.pe.at(f"U{n}"))
                dve.tensor_scalar(vu[rb + 32:rb + 64, cp, 1, :, :],
                                  ps[rb + 32:rb + 64, 5, :].rearrange("p (i v) -> p i v", i=KT), -1.0, None,
                                  ALU.mult).then_inc(*O2.dve.done(f"U{n}"))
                if q == QUADS:
                    continue
                dve.wait_ge(*O2.pe.at(f"H{n}"))
                total = ps[:, 7, :].rearrange("p (i v) -> p i v", i=KT)
                if n > 0:
                    dve.tensor_tensor(hst, hst, total, ALU.add).then_inc(*O2.dve.done(f"h{n}"))
                    dve.wait_ge(*O2.dve.at(f"h{n}"))
                    total = hst
                dve.tensor_tensor(hst, total, wc[:, :, n:n + 1].to_broadcast([P, KT, NC]), ALU.mult).then_inc(
                    *O2.dve.done(f"H{n}"))

        def pool_states(pool):
            pool.wait_ge(*O1.dve.at(f"rw_vl{KT - 1}"))
            for b in range(NB):
                if b >= 2:
                    pool.wait_ge(*O2.pe.at(f"st{b - 2}"))
                pool.dma_start(lio[64 * (b % 2):64 * (b % 2) + 64, :].rearrange("p (h k) -> p h k", h=HC),
                               a["state_rwkv"][0, b].rearrange("h v k -> v h k")).then_inc(slot_in[b % 2], 16)

        def pe_states(pe, b0):
            pe.wait_ge(*(O2.act.at(f"o{2 * b0 - 1}") if b0 else O1.dve.at("s16")))
            if b0:
                pe.wait_ge(*O2.dve.at(f"H{2 * b0 - 1}"))
            for b in (b0, b0 + 1):
                r = slice(64 * (b % 2), 64 * (b % 2) + 64)
                pe.wait_ge(slot_in[b % 2], 8 * (b - b % 2) + 16)
                for i in range(KT):
                    mm = pe.transpose(ps[:, 6 + b % 2, i * NC:(i + 1) * NC], lio[r, i * P:(i + 1) * P], ident[r, r])
                mm.then_inc(*O2.pe.done(f"st{b}"))
            pe.wait_ge(*O2.act.at(f"st{b0}"))
            pe.wait_ge(*O2.dve.at(f"st{b0 + 1}"))

        def act_states(act, b):
            act.wait_ge(*O2.pe.at(f"st{b}"))
            act.activation(hs[:, b, :, :], ps[:, 6, :].rearrange("p (i v) -> p i v", i=KT), ACT.Copy).then_inc(
                *O2.act.done(f"st{b}"))

        def dve_states(dve, b):
            dve.wait_ge(*O2.pe.at(f"st{b}"))
            dve.tensor_copy(hs[:, b, :, :], ps[:, 7, :].rearrange("p (i v) -> p i v", i=KT)).then_inc(
                *O2.dve.done(f"st{b}"))

        def pe_rts(pe):
            pe.wait_ge(*O2.act.at(f"kt{QUADS}"))
            for b in range(NB):
                for i in range(KT):
                    for g in range(2):
                        r = slice(64 * g, 64 * g + 64)
                        out = ps[r, 7, i * 64:(i + 1) * 64].rearrange("p (s t) -> p s t", s=2)
                        mm = pe.matmul(out[:, :, b * ST:(b + 1) * ST], hs[r, b, i, :],
                                       qr[r, i, NCO - 1, :, b * ST:(b + 1) * ST], start=True, stop=True)
            mm.then_inc(*O2.pe.done("rts"))

        def pe_new_states(pe):
            for k, (g, i) in enumerate(heads2):
                bank = i % 2
                pe.wait_ge(*O2.dve.at(f"vx{k}"))
                if k >= 4 and g == 0:
                    pe.wait_ge(*O2.dve.at(f"ns{i - 2}"))
                pe.matmul(ps[64 * g:64 * g + 64, bank, :], kbt[0:64, 0, i, g * NC:(g + 1) * NC],
                          vux2[k % 2], start=True, stop=True).then_inc(*O2.pe.done(f"ns{k}"))
            for b in range(NB + 1):
                b0 = 2 + 2 * (b % 2)
                if b == 0:
                    pe.wait_ge(*O2.dve.at(f"ns{KT - 1}"))
                elif b >= 2:
                    pe.wait_ge(*O2.act.at(f"so{b - 2}"))
                    pe.wait_ge(*O2.dve.at(f"so{b - 2}"))
                for i in range(KT):
                    src = hs[:, b, i, :] if b < NB else hst[:, i, :]
                    mm = pe.transpose(ps[0:64, b0 + i // 4, (i % 4) * P:(i % 4 + 1) * P], src, ident[:, :])
                mm.then_inc(*O2.pe.done(f"so{b}"))

        vux2 = [quad[0:64, 5120 + 512 * k:5632 + 512 * k] for k in range(2)]

        def dve_new_states(dve):
            dve.wait_ge(*O2.act.at(f"U{4 * QUADS}"))
            dve.wait_ge(*O2.dve.at(f"U{4 * QUADS}"))
            for k, (g, i) in enumerate(heads2):
                if k >= 2:
                    dve.wait_ge(*O2.pe.at(f"ns{k - 2}"))
                dve.tensor_tensor(vux2[k % 2].rearrange("p (b v) -> p b v", b=NB),
                                  vu[0:64, 0, g, i, :].unsqueeze(1).to_broadcast([64, NB, NC]),
                                  batO[0:64, :].unsqueeze(2).to_broadcast([64, NB, NC]), ALU.mult).then_inc(
                    *O2.dve.done(f"vx{k}"))
                if k % 2 == 0 and i > 0:
                    new_state(dve, i - 1)
            new_state(dve, KT - 1)
            dve.wait_ge(*O2.dve.at(f"ns{KT - 1}"))
            for b in range(NB + 1):
                state_rows(dve, O2.dve, b)

        def new_state(dve, i):
            dve.wait_ge(*O2.pe.at(f"ns{2 * i + 1}"))
            h = hs[:, :, i, :]
            dve.tensor_tensor(h, h, ps[:, i % 2, :].rearrange("p (b v) -> p b v", b=NB), ALU.add).then_inc(
                *O2.dve.done(f"na{i}"))
            dve.wait_ge(*O2.dve.at(f"na{i}"))
            dve.tensor_tensor(h, h, wc[:, i, 16:24].unsqueeze(2).to_broadcast([P, NB, NC]), ALU.mult).then_inc(
                *O2.dve.done(f"ns{i}"))

        def state_rows(eng, signal, b):
            half = 0 if signal is O2.act else 1
            eng.wait_ge(*O2.pe.at(f"so{b}"))
            if b >= 2:
                eng.wait_ge(slot_out[b % 2], 16 * (b // 2))
            elif half == 0:
                eng.wait_ge(*O2.pe.at(f"st{NB - 2 + b}"))
            dst = lio[64 * (b % 2):64 * (b % 2) + 64, half * 512:half * 512 + 512]
            src = ps[0:64, 2 + 2 * (b % 2) + half, :]
            if half == 0:
                eng.activation(dst, src, ACT.Copy).then_inc(*signal.done(f"so{b}"))
            else:
                eng.tensor_copy(dst, src).then_inc(*signal.done(f"so{b}"))

        def pool_out(pool):
            pool.wait_ge(*O2.pe.at(f"kt{QUADS}1"))
            pool.dma_start(g2, a["rw_g2"][0]).then_inc(*O3.dma.loaded("g2"))
            pool.dma_start(spread, a["head_spread"]).then_inc(*O3.dma.loaded("all"))
            for b in range(NB + 1):
                pool.wait_ge(*O2.act.at(f"so{b}"))
                pool.wait_ge(*O2.dve.at(f"so{b}"))
                dst = o["rwkv_sample"][0, b] if b < NB else o["rwkv_prompt"][0, 0]
                pool.dma_start(dst.rearrange("h v k -> v h k"),
                               lio[64 * (b % 2):64 * (b % 2) + 64, :].rearrange("p (h k) -> p h k", h=HC)).then_inc(
                    slot_out[b % 2], 16)

        ot, xc, sqo, rso, bo = (cols(2 * D + 2 * T * i, 2, T) for i in range(5))

        def act_ogate(act):
            act.wait_ge(*O2.pe.at(f"kt{QUADS}1"))
            for i in range(KT + 1):
                if i < KT:
                    if i >= 2:
                        act.wait_ge(*O3.dve.at(f"xc{i - 2}"))
                    else:
                        act.wait_ge(*O2.act.at(f"o{4 * QUADS}"))
                    act.activation(chunked(ot[:, i % 2, :]), qr[:, i, :, 0, :], ACT.Copy).then_inc(
                        *O3.act.done(f"o{i}"))
                if i > 0:
                    k = i - 1
                    act.wait_ge(*O3.dve.at(f"y{k}"))
                    act.activation(xh[:, k, :], bo[:, k % 2, :], ACT.Copy).then_inc(*O3.act.done(f"h{k}"))
                if i == KT:
                    continue
                act.wait_ge(*O3.dve.at(f"xc{i}"))
                act.activation(sqo[:, i % 2, :], xc[:, i % 2, :], ACT.Square).then_inc(*O3.act.done(f"sq{i}"))
                act.wait_ge(*O3.pe.at(f"var{i}"))
                act.activation(two(rso[:, i % 2, :]), ps[:, 6:8, 0:TH], ACT.Ln, bias=eps_gn, scale=1.0 / NC).then_inc(
                    *O3.act.done(f"ln{i}"))
                act.wait_ge(*O3.act.at(f"ln{i}"))
                act.activation(rso[:, i % 2, :], rso[:, i % 2, :], ACT.Exp, scale=-0.5).then_inc(*O3.act.done(f"rs{i}"))

        def pe_ogate(pe):
            pe.wait_ge(*O2.act.at(f"so{NB}"))
            pe.wait_ge(*O2.dve.at(f"so{NB}"))
            pe.wait_ge(*O3.dma.at("all"))
            pe.wait_ge(*O1.dve.at("s16"))
            for i in range(KT):
                pe.wait_ge(*O3.act.at(f"o{i}"))
                if i > 0:
                    pe.wait_ge(*O3.dve.at(f"xc{i - 1}"))
                for h in range(2):
                    mm = pe.matmul(ps[:, 4 + h, 0:TH], same, ot[:, i % 2, h * TH:(h + 1) * TH], start=True, stop=True)
                mm.then_inc(*O3.pe.done(f"mean{i}"))
                if i > 0:
                    pe.wait_ge(*O3.dve.at(f"y{i - 1}"))
                for h in range(2):
                    pe.matmul(ps[:, h, 0:TH], spread[:, i * P:(i + 1) * P], s16[:, h * TH:(h + 1) * TH], start=True,
                              stop=True)
                for h in range(2):
                    mm = pe.matmul(ps[:, 2 + h, 0:TH], g2[:, i * P:(i + 1) * P], gs[:, h * TH:(h + 1) * TH], start=True,
                                   stop=True)
                mm.then_inc(*O3.pe.done(f"g{i}"))
                pe.wait_ge(*O3.act.at(f"sq{i}"))
                for h in range(2):
                    mm = pe.matmul(ps[:, 6 + h, 0:TH], same, sqo[:, i % 2, h * TH:(h + 1) * TH], start=True, stop=True)
                mm.then_inc(*O3.pe.done(f"var{i}"))

        def dve_ogate(dve):
            for i in range(KT):
                y, x = bo[:, i % 2, :], xc[:, i % 2, :]
                dve.wait_ge(*O3.pe.at(f"mean{i}"))
                if i >= 2:
                    dve.wait_ge(*O3.dve.at(f"l{i - 2}"))
                dve.scalar_tensor_tensor(out=two(x), in0=ps[:, 4:6, 0:TH], scalar=-1.0 / NC,
                                         in1=two(ot[:, i % 2, :]), op0=ALU.mult, op1=ALU.add).then_inc(
                    *O3.dve.done(f"xc{i}"))
                dve.wait_ge(*O3.pe.at(f"g{i}"))
                dve.tensor_tensor(two(y), ps[:, 0:2, 0:TH], two(vF[:, i, :]), ALU.mult).then_inc(
                    *O3.dve.done(f"bo{i}"))
                dve.wait_ge(*O3.act.at(f"rs{i}"))
                dve.scalar_tensor_tensor(out=x, in0=x, scalar=col("rw_lnw", i), in1=rso[:, i % 2, :], op0=ALU.mult,
                                         op1=ALU.mult).then_inc(*O3.dve.done(f"n{i}"))
                dve.wait_ge(*O3.dve.at(f"n{i}"))
                dve.scalar_tensor_tensor(out=y, in0=x, scalar=col("rw_lnb", i), in1=y, op0=ALU.add,
                                         op1=ALU.add).then_inc(*O3.dve.done(f"on{i}"))
                dve.wait_ge(*O3.dve.at(f"on{i}"))
                dve.tensor_tensor(two(y), two(y), ps[:, 2:4, 0:TH], ALU.mult).then_inc(*O3.dve.done(f"y{i}"))
                dve.wait_ge(*O3.act.at(f"h{i}"))
                dve.tensor_tensor(xl[:, i, :], y, xh[:, i, :].bitcast(F32), ALU.subtract).then_inc(
                    *O3.dve.done(f"l{i}"))

        def o_ready(pe):
            pe.wait_ge(*O3.dve.at(f"l{KT - 1}"))
            pe.wait_ge(*O3.act.at(f"h{KT - 1}"))

        out_odd = add_stage("rw_o", o_ready)

        def states_out(eng):
            eng.wait_ge(slot_out[0], 16 * (NB // 2 + 1))
            eng.wait_ge(slot_out[1], 16 * (NB // 2))

        odd_late = [dict(gpsimd=pool_states)]
        for _q in range(QUADS + 1):
            def _pe(e, q=_q):
                if q < 4:
                    pe_states(e, 2 * q)
                pe_quad(e, q)

            def _act(e, q=_q):
                if q < 4:
                    act_states(e, 2 * q)
                act_quad(e, q)

            def _dve(e, q=_q):
                if q < 4:
                    dve_states(e, 2 * q + 1)
                dve_quad(e, q)
            odd_late.append(dict(tensor=_pe, scalar=_act, vector=_dve))
        odd_late += [
            dict(tensor=pe_new_states, scalar=lambda e: [state_rows(e, O2.act, b) for b in range(NB + 1)],
                 vector=dve_new_states, gpsimd=pool_out),
            dict(tensor=pe_ogate, scalar=act_ogate, vector=dve_ogate),
            dict(tensor=out_odd[0], scalar=lambda e: (out_odd[1](e), states_out(e)), vector=out_odd[2]),
        ]
        OUTS = KTILES + 2 + 5

        norm0 = Norm("mix0", lambda k: col("norm_mix", k), [E0.dve.at("x9")], "v_a")

        todo = [
            dict(sync=lambda e: [sp_stage(e, n) for n in order[:order.index("rw_r")]]),
            dict(vector=first_counts),
            dict(tensor=pe_embed, scalar=act_embed, vector=dve_embed),
            dict(scalar=lambda e: [act_head(e, "v_a", s, 0) for s in range(2)],
                 vector=lambda e: [dve_rest(e, "v_a", s, 0) for s in range(2)]),
            dict(tensor=lambda e: pe_norm(e, norm0), scalar=lambda e: act_norm(e, norm0),
                 vector=lambda e: dve_norm(e, norm0)),
            dict(tensor=pe_even_in, scalar=act_even_in, vector=dve_even_in),
            dict(scalar=act_decay, vector=dve_decay),
            dict(tensor=pe_scores, scalar=act_scores, vector=dve_scores),
            dict(tensor=pe_chunks, scalar=act_chunks, vector=dve_chunks, gpsimd=pool_chunks),
            dict(tensor=pe_gate, scalar=act_gate, vector=dve_gate),
            dict(tensor=out_even[0], scalar=out_even[1], vector=out_even[2]),
        ] + tail_parts[0] + [
            dict(sync=lambda e: [sp_stage(e, n) for n in order[order.index("rw_r"):order.index("rw_o") + 1]]),
        ] + odd_parts + odd_late + [
            dict(sync=lambda e: [sp_stage(e, n) for n in order[order.index("rw_o") + 1:]]),
        ] + tail_parts[1] + [
            dict(tensor=pe_final, scalar=act_final, vector=dve_final, gpsimd=pool_final),
        ]
        todo = todo[:stop]
        with nc.Block() as block:
            @block.sync
            def _(sp):
                for part in todo:
                    if "sync" in part:
                        part["sync"](sp)

            @block.tensor
            def _(pe):
                for part in todo:
                    if "tensor" in part:
                        part["tensor"](pe)

            @block.scalar
            def _(act):
                for part in todo:
                    if "scalar" in part:
                        part["scalar"](act)

            @block.vector
            def _(dve):
                for part in todo:
                    if "vector" in part:
                        part["vector"](dve)

            @block.gpsimd
            def _(pool):
                for part in todo:
                    if "gpsimd" in part:
                        part["gpsimd"](pool)


_INS = ["x_prompt", "x_sample", "p_prompt", "p_sample", "state_gla", "state_hgrn", "state_rwkv", "state_shift",
        "norm_mix", "norm_ffn", "norm_ple", "norm_final", "w_in_even", "w_gk2", "b_gk", "gla_norm", "hgrn_gamma",
        "hgrn_norm", "w_out_even", "rw_mu", "rw_wr", "rw_wk", "rw_wv", "rw_wo", "rw_w0", "rw_w1", "rw_w2", "rw_a0",
        "rw_a1", "rw_a2", "rw_g1", "rw_g2", "rw_kk", "rw_ka", "rw_rk", "rw_lnw", "rw_lnb", "w_ffn_gate", "w_ffn_up",
        "w_ffn_down", "w_ple", "w_ple_gate"]
_OUTS = [("y_prompt", (1, TP, D)), ("y_sample", (NB, ST, D)), ("gla_prompt", (1, 1, HA, DKA, DV)),
         ("hgrn_prompt", (1, 1, HB, NBK, DV)), ("rwkv_prompt", (1, 1, HC, NC, NC)), ("shift_prompt", (1, 1, D)),
         ("gla_sample", (1, NB, HA, DKA, DV)), ("hgrn_sample", (1, NB, HB, NBK, DV)),
         ("rwkv_sample", (1, NB, HC, NC, NC)), ("shift_sample", (1, NB, D))]


def _constants():
    return {"ident": np.concatenate([np.eye(P), np.ones((P, P))], 1).astype(np.float32),
            "even_tables": even_tables(), "odd_tables": odd_tables(), "head_spread": head_spread()}


def build(new_core, shapes, stop=99):
    known = None
    for _ in range(2):
        nc, seen = new_core(), {}
        a = {n: nc.dram_tensor(f"in_{n}", s, F32, kind="ExternalInput").ap() for n, s in shapes.items()}
        o = {n: nc.dram_tensor(f"out_{n}", s, F32, kind="ExternalOutput").ap() for n, s in _OUTS}
        trunk(nc, a, o, known, seen, stop)
        known = seen
    return nc


def kernel(**inputs):
    import concourse.bacc as bacc
    from concourse.bass_utils import run_bass_kernel_spmd

    arrays = {n: np.ascontiguousarray(inputs[n]) for n in _INS}
    arrays.update(_constants())
    nc = build(lambda: bacc.Bacc("TRN2", target_bir_lowering=False, num_devices=1),
               {n: x.shape for n, x in arrays.items()})
    r = run_bass_kernel_spmd(nc, [{f"in_{n}": x for n, x in arrays.items()}], core_ids=[0])
    return tuple(r.results[0][f"out_{n}"] for n, _ in _OUTS)
```

```python
from contextlib import ExitStack

import numpy as np

import concourse.bass as bass
from concourse import mybir

F32 = mybir.dt.float32
F32R = mybir.dt.float32r
ACT = mybir.ActivationFunctionType
ALU = mybir.AluOpType
ds = bass.ds

P = 128
D = 1024
KT = D // P
TP = 512
NB, ST = 8, 4
TS = NB * ST
T = TP + TS
TH = T // 2
FFN = 2816
FT = FFN // P // 2
PLE = 256
RMS_EPS = 1e-6

HA, DKA, HB, NBK, DV = 4, 64, 4, 128, 128
KTILES = HA * DKA // P + HB
CE = 64
NCE = TP // CE
LEVELS = 6
EVEN_IN = {"q_a": 0, "k_a": 256, "v_a": 512, "g_a": 1024, "gk": 1536, "q_b": 1552, "f_b": 2064, "i_b": 2576,
           "g_b": 3088}
HC, NC = 16, 64
CO = 32
NCO = T // CO
GN_EPS = 64e-5


class Signal:

    def __init__(self, sem, name, seen, known):
        self.sem, self.name, self.seen, self.known, self.n = sem, name, seen, known, 0

    def done(self, step):
        self.n += 1
        assert (self.name, step) not in self.seen, (self.name, step)
        self.seen[self.name, step] = self.n
        return self.sem, 1

    def loaded(self, step):
        self.n += 16
        self.seen[self.name, step] = self.n
        return self.sem, 16

    def at(self, step):
        if self.known is not None:
            return self.sem, self.known[self.name, step]
        return self.sem, 1


VEC0 = [("norm_mix", 16), ("norm_ffn", 16), ("norm_ple", 16), ("norm_final", 8), ("b_gk", 2), ("gla_norm", 1),
        ("hgrn_gamma", 4), ("hgrn_norm", 1), ("rw_mu", 48), ("rw_w0", 8), ("rw_a0", 8)]
VEC1 = [("rw_kk", 8), ("rw_ka", 8), ("rw_rk", 8), ("rw_lnw", 8), ("rw_lnb", 8), ("state_shift", 64)]
VCOL = {}
for _half, _table in enumerate((VEC0, VEC1)):
    _at = 0
    for _name, _rows in _table:
        VCOL[_name] = (_half, _at, _rows)
        _at += _rows



def even_tables():
    p, t = np.arange(P)[:, None], np.arange(CE)[None, :]
    s = p % CE
    masks = [s == t]
    for level in range(1, LEVELS + 1):
        m = 1 << (level - 1)
        masks.append((s // (2 * m) == t // (2 * m)) & (s % (2 * m) < m) & (t % (2 * m) >= m))
    return np.concatenate(masks + [scan_resets(CE), p // ST == np.arange(NB)[None, :]], 1).astype(np.float32)


def scan_resets(chunk):
    t = np.arange(T)
    keep = np.where(t < TP, t % chunk != 0, t % ST != 0)
    return np.broadcast_to(keep, (P, T))


def odd_tables():
    p, t = np.arange(P)[:, None], np.arange(CO)[None, :]
    s = p % CO
    same_head = p // NC == np.arange(P)[None, :] // NC
    halves = []
    for level in range(1, 6):
        m = 1 << (level - 1)
        halves.append((s // (2 * m) == t // (2 * m)) & (s % (2 * m) < m) & (t % (2 * m) >= m))
    prompt = [s < t, s <= t]
    sample = [(s < t) & (s // ST == t // ST), (s <= t) & (s // ST == t // ST)]
    head = [(2 * k + p // NC) == np.arange(HC)[None, :] for k in range(KT)]
    batch = [s // ST == np.arange(NB)[None, :]]
    return np.concatenate([scan_resets(CO), same_head] + halves + prompt + sample + head + batch, 1).astype(np.float32)


def head_spread():
    return (np.arange(HC)[:, None] == np.arange(D)[None, :] // NC).astype(np.float32)


TABC = 1104


def trunk(nc, a, o, known, seen, stop=99):
    ctx = ExitStack()
    with ctx:
        def sb(name, shape, dt=F32):
            return ctx.enter_context(nc.sbuf_tensor(name, shape, dt))

        def sem(name):
            return ctx.enter_context(nc.semaphore(name))

        class Section:
            def __init__(self, name):
                def signal(by):
                    return Signal(sem(f"{name}_{by}"), f"{name}_{by}", seen, known)

                self.pe, self.act, self.dve = signal("pe"), signal("act"), signal("dve")
                self.pool, self.dma = signal("pool"), signal("dma")

        hT = sb("hT", [P, KT, T])
        xs_byte = (nc.sbuf_base + 31) // 32 * 32
        xs = sb("x_split", [P, 2 * KT * T], F32R)
        xh = xs[:, 0:KT * T].rearrange("p (k t) -> p k t", k=KT)
        xl = xs[:, KT * T:2 * KT * T].rearrange("p (k t) -> p k t", k=KT)
        raw = sb("w_raw", [P, 2, FT * P])
        wh = sb("w_head", [P, 2, FT * P], F32R)
        wl = sb("w_rest", [P, 2, FT * P], F32R)
        ident = sb("ident", [P, P])
        ones = sb("ones", [P, P])
        vec = sb("vectors", [P, 2, P])
        eps = sb("epsilons", [P, 3])
        eps_rms, eps_gn, bias17 = eps[:, 0:1], eps[:, 1:2], eps[:, 2:3]
        tab = sb("tables", [P, TABC])
        MIXC = 30016
        mix_byte = (nc.sbuf_base + 31) // 32 * 32
        mix = sb("mix", [P, MIXC])
        ps = ctx.enter_context(nc.psum_tensor("ps", [P, 8, 512], F32))

        def col(name, i=0):
            half, at, _ = VCOL[name]
            return vec[:, half, at + i:at + i + 1]

        raw_in = [sem("slabA_loaded"), sem("slabB_loaded")]
        head_ok = [sem("slabA_head"), sem("slabB_head")]
        rest_ok = [sem("slabA_rest"), sem("slabB_rest")]
        mm_ok = [sem("productA"), sem("productB")]
        bank_free = [sem("banksA_read"), sem("banksB_read")]
        x_free = sem("input_tile_read")

        def W(name, layer):
            return a[name][layer]

        w_in = W("w_in_even", 0)
        stages = {}
        order = []

        def stage(name, n, units):
            stages[name] = (n, units)
            order.append(name)

        X = (xh, xl)
        stage("v_a", 2, [(w_in, EVEN_IN["v_a"], 256, 0, KT, X), (w_in, EVEN_IN["v_a"] + 128, 256, 0, KT, X)])
        stage("i_b", 2, [(w_in, EVEN_IN["i_b"], 256, 0, KT, X), (w_in, EVEN_IN["i_b"] + 128, 256, 0, KT, X)])
        stage("gk", 1, [(w_in, EVEN_IN["gk"], 0, 0, KT, X)])
        for name, n in (("f_b", 2), ("k_a", 1), ("q_a", 1), ("q_b", 2), ("g_a", 2), ("g_b", 2)):
            stage(name, n, [(w_in, EVEN_IN[name], 256, 0, KT, X), (w_in, EVEN_IN[name] + 128, 256, 0, KT, X)])
        stage("w_out", 4, [(W("w_out_even", 0), 0, 256, 0, KT, X), (W("w_out_even", 0), 128, 256, 0, KT, X)])

        base = mix_byte
        hid = nc.alloc_sbuf_tensor_at("hidden_split", [P, 2, FT, T], F32R, offset=base)
        ple = nc.alloc_sbuf_tensor_at("ple_split", [P, 2, PLE // P, T], F32R, offset=base + 4 * 2 * FT * T)
        MIXF = 2 * FT * T + 2 * (PLE // P) * T

        def tail_stages(i):
            for half in range(2):
                c = half * FT * P
                stage(f"up{i}{half}", FT, [(W("w_ffn_gate", i), c, 128, 0, KT, X), (W("w_ffn_up", i), c, 128, 0, KT, X)])
                stage(f"down{i}{half}", 4, [(W("w_ffn_down", i), 0, 256, c, FT, (hid[:, 0], hid[:, 1])),
                                            (W("w_ffn_down", i), 128, 256, c, FT, (hid[:, 0], hid[:, 1]))])
            stage(f"ple{i}", 8, [(W("w_ple_gate", i), 0, 128, 0, KT, X),
                                 (W("w_ple", i), 0, 128, 0, PLE // P, (ple[:, 0], ple[:, 1]))])

        tail_stages(0)
        for name in ("r", "k", "g1", "v"):
            if name == "g1":
                stage("rw_g1", 1, [(W("rw_g1", 0), 0, 0, 0, KT, X)])
                continue
            w = W(f"rw_w{name}", 0)
            stage(f"rw_{name}", 4, [(w, 0, 256, 0, KT, X), (w, 128, 256, 0, KT, X)])
        stage("rw_o", 4, [(W("rw_wo", 0), 0, 256, 0, KT, X), (W("rw_wo", 0), 128, 256, 0, KT, X)])
        tail_stages(1)
        used = {}
        ab = [0, 0]
        for name in order:
            used[name] = tuple(ab)
            n, units = stages[name]
            for s in range(len(units)):
                ab[s] += n

        def each(eng, n, name, body, first=0):
            if n - first > 2:
                with eng.Fori(first, n - 1) as i:
                    body(i, False)
            else:
                for i in range(first, n - 1):
                    body(i, False)
            if n > first:
                body(n - 1, True)

        def sp_stage(sp, name):
            n, units = stages[name]

            def load(i):
                for s, (w, c, step, row, kt, _) in enumerate(units):
                    use = used[name][s] + i
                    if not (isinstance(use, int) and use == 0):
                        sp.wait_ge(rest_ok[s], use)
                    src = w[row:row + kt * P, :].rearrange("(k p) n -> p k n", p=P)
                    sp.dma_start(raw[:, s, 0:kt * P].rearrange("p (k n) -> p k n", k=kt),
                                 src[:, :, ds(i * step + c, P)]).then_inc(raw_in[s], 16)

            if n > 2:
                with sp.Fori(0, n) as i:
                    load(i)
            else:
                for i in range(n):
                    load(i)

        def act_head(act, name, s, i):
            use, kt = used[name][s] + i, stages[name][1][s][4]
            act.wait_ge(raw_in[s], 16 * use + 16)
            act.wait_ge(mm_ok[s], use)
            act.activation(wh[:, s, 0:kt * P], raw[:, s, 0:kt * P], ACT.Copy).then_inc(head_ok[s], 1)

        def dve_rest(dve, name, s, i):
            use, kt = used[name][s] + i, stages[name][1][s][4]
            dve.wait_ge(head_ok[s], use + 1)
            dve.tensor_tensor(wl[:, s, 0:kt * P], raw[:, s, 0:kt * P], wh[:, s, 0:kt * P].bitcast(F32),
                              ALU.subtract).then_inc(rest_ok[s], 1)

        def ahead(split, eng, name, s, i, last):
            if not last:
                split(eng, name, s, i + 1)
                return
            at = order.index(name) + 1
            while at < len(order) and len(stages[order[at]][1]) <= s:
                at += 1
            if at < len(order):
                split(eng, order[at], s, 0)

        def unit_products(pe, name, i, s, ready=None, freed=False):
            _, _, _, _, kt, (uh, ul) = stages[name][1][s]
            use = used[name][s] + i
            pe.wait_ge(head_ok[s], use + 1)
            pe.wait_ge(rest_ok[s], use + 1)
            pe.wait_ge(bank_free[s], use)
            for k in range(kt):
                if ready is not None:
                    ready(pe, k)
                for w, x, first in ((wh, uh, True), (wh, ul, False), (wl, uh, False)):
                    for h in range(2):
                        mm = pe.matmul(ps[:, 2 * s + h, 0:TH], w[:, s, k * P:(k + 1) * P],
                                       x[:, k, h * TH:(h + 1) * TH], start=first and k == 0,
                                       stop=k == kt - 1 and w is wl)
                if freed and k < kt - 1:
                    mm.then_inc(x_free, 1)
            mm.then_inc(mm_ok[s], 1)

        def pe_stage(pe, name, ready=None, freed=False):
            n, units = stages[name]

            def products(i, last):
                for s in range(len(units)):
                    unit_products(pe, name, i, s, freed=freed and last and s == len(units) - 1)

            first = 0
            if ready is not None:
                for s in range(len(units)):
                    unit_products(pe, name, 0, s, ready if s == 0 else None, freed and n == 1)
                first = 1
            each(pe, n, name, products, first)

        def out2(s):
            return ps[:, 2 * s:2 * s + 2, 0:TH]

        def two(ap):
            return ap.rearrange("p (h t) -> p h t", h=2)

        def cols(at, *shape):
            n = int(np.prod(shape))
            ap = mix[:, at:at + n]
            if len(shape) == 2:
                return ap.rearrange("p (a b) -> p a b", a=shape[0])
            if len(shape) == 3:
                return ap.rearrange("p (a b c) -> p a b c", a=shape[0], b=shape[1])
            return ap

        xtok = cols(0, 5, D)
        vrow = cols(5 * D, 2, P)
        vT = cols(0, KT, T)
        gate = cols(8 * T, KT, T)
        qq = cols(16 * T, KTILES, T)
        kk = cols(22 * T, KTILES, T)
        lg = cols(28 * T, KTILES, T)
        vtok = cols(34 * T, 5, D)
        ktok = cols(34 * T + 5 * D, 5, KTILES * P)
        soft = cols(34 * T + 5 * D, KTILES, T)
        pT = cols(34 * T + 5 * D + 5 * KTILES * P, 8, 5, CE)
        qk = cols(0, LEVELS, T)
        ee = cols(LEVELS * T, 2, T)
        oT = cols(22 * T, KT, T)
        sq = cols(34 * T, 2, T)
        rstd = cols(36 * T, 2, T)
        nrm = cols(38 * T, 2, T)
        lrT = cols(34 * T + 5 * D, T)
        wgk2 = cols(34 * T + 5 * D + 3300, HA * DKA)
        lbs = cols(34 * T + 5 * D + 5 * KTILES * P + 2500, 40)
        alias = nc.alloc_sbuf_tensor_at("even_scratch", [P, 8704], F32, offset=xs_byte)
        state = [alias[:, at:at + 768].rearrange("p (k v) -> p k v", k=KTILES) for at in (0, 7168)]
        sst = [alias[:, 768:1792], alias[:, 1792:2816]] + [cols(i * NB * DV, NB * DV) for i in range(4)]
        sst = [ap.rearrange("p (b v) -> p b v", b=NB) for ap in sst]
        vx = alias[:, 2816:4864].rearrange("p (a b v) -> p a b v", a=2, b=NB)
        mt = alias[:, 4864:6912].rearrange("p (a c) -> p a c", a=2)
        ebl = alias[:, 6912:7008].rearrange("p (k c) -> p k c", k=KTILES)
        lvmask = tab[:, 0:7 * CE].rearrange("p (l t) -> p l t", l=7)
        resetE = tab[:, 7 * CE:7 * CE + T]
        batE = tab[:, 7 * CE + T:7 * CE + T + NB]

        def rows(h):
            if h < HA:
                return h // 2, 64 * (h % 2), DKA
            return h - HA + 2, 0, NBK

        heads_of = [[0, 1], [2, 3], [4], [5], [6], [7]]
        jobs = [(kt, h) for kt in range(KTILES) for h in heads_of[kt]]

        E0 = Section("embed")

        def act_embed(act):
            act.dma_start(ident[:, :], a["ident"][:, 0:P]).then_inc(*E0.dma.loaded("i"))
            act.dma_start(ones[:, :], a["ident"][:, P:2 * P]).then_inc(*E0.dma.loaded("o"))
            act.dma_start(tab[:, 0:7 * CE + T + NB], a["even_tables"]).then_inc(*E0.dma.loaded("t"))
            for half, table in enumerate((VEC0, VEC1)):
                at = 0
                for name, n in table:
                    shape = a[name].shape
                    flat = a[name]
                    if len(shape) == 1:
                        flat = flat.rearrange("(r c) -> r c", c=P)
                    elif len(shape) == 2:
                        flat = flat.rearrange("i (r c) -> (i r) c", c=P)
                    elif name == "rw_rk":
                        flat = flat.rearrange("i (r e) c -> (i r) (e c)", e=2)
                    elif len(shape) == 3:
                        flat = flat.rearrange("i j (r c) -> (i j r) c", c=P)
                    act.dma_start(vrow[at:at + n, half, :], flat).then_inc(*E0.dma.loaded(name))
                    at += n
            act.dma_start(xtok[:, 0:4, :], a["x_prompt"][0].rearrange("(a p) d -> p a d", p=P)).then_inc(
                *E0.dma.loaded("xp"))
            act.dma_start(xtok[0:TS, 4, :], a["x_sample"].rearrange("b t d -> (b t) d")).then_inc(
                *E0.dma.loaded("all"))

        def pe_embed(pe):
            pe.wait_ge(*E0.dma.at("all"))
            for half, n in ((0, P), (1, 104)):
                mm = pe.transpose(ps[:, 4 + half, 0:n], vrow[0:n, half, :], ident[0:n, 0:n])
            mm.then_inc(*E0.pe.done("vec"))
            for j, (tt, k4) in enumerate((t, k) for t in range(5) for k in range(2)):
                n = P if tt < 4 else TS
                if j < 2:
                    bank = 6 + j
                else:
                    bank = 4 + (j - 2) % 4
                if j >= 6:
                    pe.wait_ge(*E0.dve.at(f"x{j - 4}"))
                elif j >= 2 and j < 4:
                    pe.wait_ge(*E0.dve.at("vec"))
                elif j >= 4:
                    pe.wait_ge(*E0.dve.at(f"x{j - 4}"))
                for k in range(4):
                    mm = pe.transpose(ps[:, bank, k * n:(k + 1) * n], xtok[0:n, tt, (4 * k4 + k) * P:(4 * k4 + k + 1) * P],
                                      ident[0:n, 0:n])
                mm.then_inc(*E0.pe.done(f"x{j}"))

        def dve_embed(dve):
            dve.memset(eps_rms, RMS_EPS)
            dve.memset(eps_gn, GN_EPS)
            dve.memset(bias17, 8.5 * float(np.log(2.0)))
            dve.wait_ge(*E0.pe.at("vec"))
            dve.tensor_copy(vec[:, 0, :], ps[:, 4, 0:P])
            dve.tensor_copy(vec[:, 1, 0:104], ps[:, 5, 0:104]).then_inc(*E0.dve.done("vec"))
            for j, (tt, k4) in enumerate((t, k) for t in range(5) for k in range(2)):
                n = P if tt < 4 else TS
                bank = 6 + j if j < 2 else 4 + (j - 2) % 4
                dve.wait_ge(*E0.pe.at(f"x{j}"))
                dve.tensor_copy(hT[:, 4 * k4:4 * k4 + 4, tt * P:tt * P + n],
                                ps[:, bank, 0:4 * n].rearrange("p (k t) -> p k t", k=4)).then_inc(*E0.dve.done(f"x{j}"))
            dve.wait_ge(*E0.dve.at("x9"))

        sq_ok, sum_ok = sem("norm_square"), sem("norm_sum")

        class Norm:

            def __init__(self, name, gain, before, number=None, at=MIXC - 4 * T, out=None):
                self.s, self.gain, self.before, self.number, self.out = Section(f"norm_{name}"), gain, before, number, out
                self.sq, self.sum, self.rs = cols(at, 2, T), cols(at + 2 * T, T), cols(at + 3 * T, T)
                self.y = cols(at, 3, T)
                self.squares = None if number is None else 8 * number
                self.sums = None if number is None else 9 * number + 1

        def clear_sum(dve, n):
            dve.memset(n.sum, 0.0).then_inc(sum_ok, 1)

        def square(act, n, s, t):
            act.wait_ge(sum_ok, t + n.sums)
            act.activation(n.sq[:, s, :], hT[:, ds(t, 1), :].rearrange("p one t -> p (one t)"),
                           ACT.Square).then_inc(sq_ok, 1)

        def add_squares(dve, n, s, t):
            dve.wait_ge(sq_ok, t + (n.squares + 1))
            dve.wait_ge(sum_ok, t + (n.sums + 1))
            dve.tensor_tensor(n.sum, n.sum, n.sq[:, s, :], ALU.add).then_inc(sum_ok, 1)

        def act_norm(act, n):
            s = n.s
            if n.number is None:
                act.wait_ge(*E0.dve.at("x9"))
                for k in range(KT):
                    if k >= 2:
                        act.wait_ge(*s.dve.at(f"sum{k - 2}"))
                    act.activation(n.sq[:, k % 2, :], hT[:, k, :], ACT.Square).then_inc(*s.act.done(f"sq{k}"))
            act.wait_ge(*s.pe.at("mean"))
            act.activation(two(n.rs), ps[:, 4:6, 0:TH], ACT.Ln, bias=eps_rms, scale=1.0 / D).then_inc(*s.act.done("ln"))
            act.wait_ge(*s.act.at("ln"))
            act.activation(n.rs, n.rs, ACT.Exp, scale=-0.5).then_inc(*s.act.done("rstd"))
            if n.out is None:
                for i in range(2):
                    act.wait_ge(mm_ok[i], used[n.before][i])
                for k in range(KT):
                    act.wait_ge(*(s.dve if k % 2 == 0 else s.pool).at(f"y{k}"))
                    act.activation(xh[:, k, :], n.y[:, k % 3, :], ACT.Copy, scale=n.gain(k)).then_inc(*s.act.done(f"h{k}"))

        def scaled(eng, signal, n, k):
            if n.out is not None:
                eng.scalar_tensor_tensor(out=n.out[:, k, :], in0=hT[:, k, :], scalar=n.gain(k), in1=n.rs, op0=ALU.mult,
                                         op1=ALU.mult).then_inc(*signal.done(f"y{k}"))
                return
            if k >= 3:
                eng.wait_ge(*n.s.dve.at(f"l{k - 3}"))
            eng.tensor_tensor(n.y[:, k % 3, :], hT[:, k, :], n.rs, ALU.mult).then_inc(*signal.done(f"y{k}"))

        def dve_norm(dve, n):
            s = n.s
            for k in range(KT if n.number is None else 0):
                dve.wait_ge(*s.act.at(f"sq{k}"))
                if k == 0:
                    dve.tensor_copy(n.sum, n.sq[:, 0, :]).then_inc(*s.dve.done("sum0"))
                else:
                    dve.wait_ge(*s.dve.at(f"sum{k - 1}"))
                    dve.tensor_tensor(n.sum, n.sum, n.sq[:, k % 2, :], ALU.add).then_inc(*s.dve.done(f"sum{k}"))
            dve.wait_ge(*s.act.at("rstd"))
            if n.out is not None:
                for k in range(KT):
                    scaled(dve, s.dve, n, k)
                return
            scaled(dve, s.dve, n, 0)
            scaled(dve, s.dve, n, 2)
            for k in range(KT):
                dve.wait_ge(*s.act.at(f"h{k}"))
                dve.scalar_tensor_tensor(out=xl[:, k, :], in0=n.y[:, k % 3, :], scalar=n.gain(k),
                                         in1=xh[:, k, :].bitcast(F32), op0=ALU.mult, op1=ALU.subtract).then_inc(
                    *s.dve.done(f"l{k}"))
                if k in (1, 3):
                    scaled(dve, s.dve, n, k + 3)
            dve.wait_ge(*s.dve.at(f"l{KT - 1}"))

        def pool_norm(pool, n):
            if n.out is None:
                pool.wait_ge(*n.s.act.at("rstd"))
                for k in range(1, KT, 2):
                    scaled(pool, n.s.pool, n, k)

        def pe_norm(pe, n):
            s = n.s
            if n.number is None:
                pe.wait_ge(*s.dve.at(f"sum{KT - 1}"))
            else:
                pe.wait_ge(sum_ok, n.sums + 9)
            for h in range(2):
                mm = pe.matmul(ps[:, 4 + h, 0:TH], ones[:, :], n.sum[:, h * TH:(h + 1) * TH], start=True, stop=True)
            mm.then_inc(*s.pe.done("mean"))

        def tile_ready(n):
            def ready(pe, k):
                pe.wait_ge(*n.s.dve.at(f"l{k}"))
            return ready

        def norm_part(n):
            return dict(tensor=lambda e: pe_norm(e, n), scalar=lambda e: act_norm(e, n),
                        vector=lambda e: dve_norm(e, n), gpsimd=lambda e: pool_norm(e, n))

        norm0 = Norm("mix0", lambda k: col("norm_mix", k), "v_a")

        E1 = Section("even_in")
        E2 = Section("even_decay")
        E3 = Section("even_scores")
        E4 = Section("even_chunks")
        E5 = Section("even_gate")
        K40 = float(2.0 ** 40)

        def pe_even_in(pe):
            pe_stage(pe, "v_a", tile_ready(norm0))
            for name in ("i_b", "gk"):
                pe_stage(pe, name)
            for s in range(2):
                pe.wait_ge(bank_free[s], used["gk"][s])
            for j, (tt, half) in enumerate((t, k) for t in range(5) for k in range(2)):
                n = P if tt < 4 else TS
                if j >= 4:
                    pe.wait_ge(*E1.dve.at(f"vt{j - 4}"))
                for k in range(4):
                    mm = pe.transpose(ps[0:n, 4 + j % 4, k * P:(k + 1) * P], vT[:, 4 * half + k, tt * P:tt * P + n],
                                      ident[:, :])
                mm.then_inc(*E1.pe.done(f"vt{j}"))
            pe.wait_ge(bank_free[0], used["f_b"][0])
            pe.wait_ge(*E1.dma.at("wgk2"))
            pe.wait_ge(*E1.dve.at("vt9"))
            for k in range(2):
                for h in range(2):
                    mm = pe.matmul(ps[:, 4 + 2 * k + h, 0:TH], wgk2[0:16, k * P:(k + 1) * P],
                                   lrT[0:16, h * TH:(h + 1) * TH], start=True, stop=True)
            mm.then_inc(*E1.pe.done("gk2"))
            for name in ("f_b", "k_a", "q_a", "q_b", "g_a", "g_b"):
                pe_stage(pe, name)

        def act_even_in(act):
            act.dma_start(wgk2[0:16, :], a["w_gk2"][0]).then_inc(*E1.dma.loaded("wgk2"))

            for name, fn in (("v_a", None), ("i_b", None), ("gk", "gk"), ("f_b", None), ("k_a", None), ("q_a", None),
                             ("q_b", "q"), ("g_a", "g"), ("g_b", "g")):
                n, units = stages[name]
                for i in range(n):
                    for s in range(len(units)):
                        use = used[name][s] + i
                        act.wait_ge(mm_ok[s], use + 1)
                        ahead(act_head, act, name, s, i, i == n - 1)
                        if fn == "gk":
                            act.activation(two(lrT)[0:16], out2(s)[0:16], ACT.Copy).then_inc(bank_free[s], 1)
                        if fn == "q":
                            act.activation(two(qq[:, 2 + 2 * i + s, :]), out2(s), ACT.Silu).then_inc(bank_free[s], 1)
                        if fn == "g":
                            t = 2 * i + s + (4 if name == "g_b" else 0)
                            act.activation(two(gate[:, t, :]), out2(s), ACT.Silu).then_inc(bank_free[s], 1)

        def dve_even_in(dve):
            for name, fn in (("v_a", 0), ("i_b", 4), ("gk", None), ("f_b", "f"), ("k_a", "k"), ("q_a", "qa"),
                             ("q_b", None), ("g_a", None), ("g_b", None)):
                n, units = stages[name]
                for i in range(n):
                    for s in range(len(units)):
                        use = used[name][s] + i
                        if fn is not None:
                            dve.wait_ge(mm_ok[s], use + 1)
                        if fn in (0, 4):
                            t = fn + 2 * i + s
                            dve.tensor_copy(two(vT[:, t, :]), out2(s)).then_inc(bank_free[s], 1)
                        if fn == "f":
                            dve.tensor_copy(two(lg[:, 2 + 2 * i + s, :]), out2(s)).then_inc(bank_free[s], 1)
                        if fn == "k":
                            dve.tensor_copy(two(kk[:, s, :]), out2(s)).then_inc(bank_free[s], 1)
                        if fn == "qa":
                            dve.tensor_scalar(two(qq[:, s, :]), out2(s), DKA ** -0.5, None, ALU.mult).then_inc(
                                bank_free[s], 1)
                        ahead(dve_rest, dve, name, s, i, i == n - 1)
                if name == "gk":
                    for j, (tt, half) in enumerate((t, k) for t in range(5) for k in range(2)):
                        nt = P if tt < 4 else TS
                        dve.wait_ge(*E1.pe.at(f"vt{j}"))
                        dve.tensor_copy(vtok[0:nt, tt, half * 512:half * 512 + 512], ps[0:nt, 4 + j % 4, :]).then_inc(
                            *E1.dve.done(f"vt{j}"))
                    dve.wait_ge(*E1.pe.at("gk2"))
                    for k in range(2):
                        dve.tensor_scalar(two(lg[:, k, :]), ps[:, 4 + 2 * k:6 + 2 * k, 0:TH], col("b_gk", k), None,
                                          ALU.add).then_inc(*E1.dve.done(f"z{k}"))

        gam = vec[:, 0, VCOL["hgrn_gamma"][1]:VCOL["hgrn_gamma"][1] + 4]
        lb_e, lb_r, lb_sm, lb, lb_c, lb_1m, lb_om, lb_t = (lbs[:, 4 * i:4 * i + 4] for i in range(8))
        zz = lg[:, :, :]
        hz = lg[:, 2:6, :]

        def dve_decay(dve):
            def step(ins, name):
                ins.then_inc(*E2.dve.done(name))
                dve.wait_ge(*E2.dve.at(name))

            step(dve.tensor_tensor(lb_t, gam, gam, ALU.subtract), "g0")
            dve.wait_ge(*E2.act.at("ge"))
            step(dve.reciprocal(lb_r, lb_e), "gr")
            step(dve.tensor_tensor(lb_sm, lb_e, lb_r, ALU.mult), "gsm")
            step(dve.tensor_tensor(lb, lb_sm, lb_sm, ALU.subtract), "lb")
            step(dve.tensor_scalar(lb_t, lb, 1e-20, K40, ALU.max, ALU.mult), "lbt")
            step(dve.tensor_scalar(lb_om, lb, -1.0, 1.0, ALU.mult, ALU.add), "lbo")
            dve.wait_ge(bank_free[0], used["k_a"][0])
            dve.wait_ge(bank_free[1], used["k_a"][1])
            dve.wait_ge(*E1.dve.at("z1"))
            dve.wait_ge(*E1.pe.at("gk2"))
            step(dve.scalar_tensor_tensor(out=soft, in0=zz, scalar=-1.0, in1=zz, op0=ALU.mult, op1=ALU.max), "abs")
            dve.wait_ge(*E2.act.at("ln"))
            step(dve.scalar_tensor_tensor(out=soft, in0=zz, scalar=0.0, in1=soft, op0=ALU.min, op1=ALU.subtract), "lsig")
            step(dve.tensor_tensor(kk[:, 2:6, :], soft[:, 2:6, :], hz, ALU.subtract), "kz")
            step(dve.tensor_scalar(lg[:, 0:2, :], soft[:, 0:2, :], 1.0 / 16.0, None, ALU.mult), "gla")
            dve.wait_ge(*E2.act.at("l1m"))
            for t in range(4):
                dve.tensor_scalar(lg[:, 2 + t, :], soft[:, 2 + t, :], lb_1m[:, t:t + 1], None, ALU.add).then_inc(
                    *E2.dve.done(f"l1{t}"))
            dve.wait_ge(*E2.dve.at("l13"))
            step(dve.tensor_scalar(lb_c, lb_c, -40.0 * float(np.log(2.0)), None, ALU.add), "c")
            for t in range(4):
                dve.tensor_scalar(soft[:, 2 + t, :], lg[:, 2 + t, :], lb_c[:, t:t + 1], None, ALU.subtract).then_inc(
                    *E2.dve.done(f"d{t}"))
            dve.wait_ge(*E2.dve.at("d3"))
            step(dve.scalar_tensor_tensor(out=soft[:, 2:6, :], in0=soft[:, 2:6, :], scalar=-1.0,
                                          in1=soft[:, 2:6, :], op0=ALU.mult, op1=ALU.max), "abs2")
            dve.wait_ge(*E2.act.at("ln2"))
            for t in range(4):
                dve.scalar_tensor_tensor(out=lg[:, 2 + t, :], in0=lg[:, 2 + t, :], scalar=lb_c[:, t:t + 1],
                                         in1=soft[:, 2 + t, :], op0=ALU.max, op1=ALU.add).then_inc(
                    *E2.dve.done(f"lf{t}"))
            dve.wait_ge(*E2.act.at("kb"))
            for t in range(4):
                dve.tensor_scalar(kk[:, 2 + t, :], kk[:, 2 + t, :], lb_om[:, t:t + 1], None, ALU.mult).then_inc(
                    *E2.dve.done(f"kb{t}"))
            dve.wait_ge(bank_free[0], used["g_a"][0])
            dve.wait_ge(bank_free[1], used["g_a"][1])
            dve.tensor_scalar(qq[:, 2:6, :], qq[:, 2:6, :], NBK ** -0.5, None, ALU.mult).then_inc(*E2.dve.done("qb"))
            dve.wait_ge(*E2.dve.at("lf3"))
            for kt in range(KTILES):
                dve.tensor_tensor_scan(lg[:, kt, :], resetE, lg[:, kt, :], 0.0, ALU.mult, ALU.add).then_inc(
                    *E2.dve.done(f"b{kt}"))

        def act_decay(act):
            act.wait_ge(*E2.dve.at("g0"))
            act.activation(lb_e, lb_t, ACT.Exp).then_inc(*E2.act.done("ge"))
            act.wait_ge(*E2.dve.at("lbo"))
            act.activation(lb_c, lb_t, ACT.Ln)
            act.activation(lb_1m, lb_om, ACT.Ln).then_inc(*E2.act.done("l1m"))
            act.wait_ge(*E2.dve.at("abs"))
            act.activation(soft, soft, ACT.Exp, scale=-1.0).then_inc(*E2.act.done("e"))
            act.wait_ge(*E2.act.at("e"))
            act.activation(soft, soft, ACT.Ln, bias=1.0).then_inc(*E2.act.done("ln"))
            act.wait_ge(*E2.dve.at("kz"))
            act.activation(kk[:, 2:6, :], kk[:, 2:6, :], ACT.Exp).then_inc(*E2.act.done("kb"))
            act.wait_ge(*E2.dve.at("abs2"))
            act.activation(soft[:, 2:6, :], soft[:, 2:6, :], ACT.Exp, scale=-1.0).then_inc(*E2.act.done("e2"))
            act.wait_ge(*E2.act.at("e2"))
            act.activation(soft[:, 2:6, :], soft[:, 2:6, :], ACT.Ln, bias=1.0).then_inc(*E2.act.done("ln2"))

        def span(level):
            return T if level <= 2 else TP

        def halves_of(ap, level):
            m = 1 << (level - 1)
            return ap[:, 0:span(level)].rearrange("p (n h m) -> p n h m", h=2, m=m)

        steps = [(kt, level) for kt in range(KTILES) for level in range(1, LEVELS + 1)]

        def dve_scores(dve):
            dve.wait_ge(mm_ok[0], used["w_out"][0])
            dve.wait_ge(mm_ok[1], used["w_out"][1])
            dve.wait_ge(*E2.dve.at(f"b{KTILES - 1}"))

            def distances(n):
                kt, level = steps[n]
                m = 1 << (level - 1)
                b, e = halves_of(lg[:, kt, :], level), halves_of(ee[:, n % 2, :], level)
                mid = b[:, :, 0, m - 1:m].to_broadcast([P, span(level) // (2 * m), m])
                if n >= 2:
                    dve.wait_ge(*E3.dve.at(f"qk{n - 2}"))
                dve.tensor_tensor(e[:, :, 0, :], mid, b[:, :, 0, :], ALU.subtract)
                dve.tensor_tensor(e[:, :, 1, :], b[:, :, 1, :], mid, ALU.subtract).then_inc(*E3.dve.done(f"e{n}"))

            def factors(n):
                kt, level = steps[n]
                e, z = halves_of(ee[:, n % 2, :], level), halves_of(qk[:, level - 1, :], level)
                dve.wait_ge(*E3.act.at(f"e{n}"))
                if kt > 0:
                    dve.wait_ge(*E3.pe.at(f"g{heads_of[kt - 1][-1]}"))
                dve.tensor_tensor(z[:, :, 0, :], e[:, :, 0, :], halves_of(kk[:, kt, :], level)[:, :, 0, :], ALU.mult)
                dve.tensor_tensor(z[:, :, 1, :], e[:, :, 1, :], halves_of(qq[:, kt, :], level)[:, :, 1, :],
                                  ALU.mult).then_inc(*E3.dve.done(f"qk{n}"))

            def masked(j):
                h = jobs[j][1]
                b0 = 4 * (j % 2)
                dve.wait_ge(*E3.pe.at(f"g{h}"))
                if j > 0:
                    dve.wait_ge(*E3.dve.at(f"ps{jobs[j - 1][1]}"))
                for q in range(4):
                    nl = 2 if q < 3 else 1
                    at = 0 if q % 2 else 512
                    out = mt[:, 1, at:at + nl * 256] if q else mt[:, 0, 0:512]
                    m = lvmask[:, 2 * q:2 * q + nl, :].unsqueeze(2).to_broadcast([P, nl, 4, CE])
                    if q == 3:
                        dve.wait_ge(*E3.dve.at(f"a{h}_1"))
                    dve.tensor_tensor(out.rearrange("p (l c t) -> p l c t", l=nl, c=4),
                                      ps[:, b0 + q, 0:nl * 256].rearrange("p (l c t) -> p l c t", l=nl, c=4), m,
                                      ALU.mult).then_inc(*E3.dve.done(f"m{h}_{q}"))
                    if q > 0:
                        dve.wait_ge(*E3.dve.at(f"m{h}_{q}"))
                        if q > 1:
                            dve.wait_ge(*E3.dve.at(f"a{h}_{q - 1}"))
                        dve.tensor_tensor(mt[:, 0, 0:nl * 256], mt[:, 0, 0:nl * 256], out, ALU.add).then_inc(
                            *E3.dve.done(f"a{h}_{q}"))
                dve.wait_ge(*E3.dve.at(f"a{h}_3"))
                dve.tensor_tensor(pT[:, h, 0:4, :], mt[:, 0, 0:256].rearrange("p (c t) -> p c t", c=4),
                                  mt[:, 0, 256:512].rearrange("p (c t) -> p c t", c=4), ALU.add).then_inc(
                    *E3.dve.done(f"p{h}"))
                dve.tensor_tensor(mt[0:TS, 1, 0:96].rearrange("p (l t) -> p l t", l=3),
                                  ps[0:TS, b0 + 3, 256:352].rearrange("p (l t) -> p l t", l=3),
                                  lvmask[0:TS, 0:3, 0:TS], ALU.mult).then_inc(*E3.dve.done(f"s{h}"))
                dve.wait_ge(*E3.dve.at(f"s{h}"))
                dve.tensor_tensor(mt[0:TS, 1, 0:32], mt[0:TS, 1, 0:32], mt[0:TS, 1, 32:64], ALU.add).then_inc(
                    *E3.dve.done(f"s2{h}"))
                dve.wait_ge(*E3.dve.at(f"s2{h}"))
                dve.tensor_tensor(pT[0:TS, h, 4, 0:TS], mt[0:TS, 1, 0:32], mt[0:TS, 1, 64:96], ALU.add).then_inc(
                    *E3.dve.done(f"ps{h}"))

            done = 0
            for n in range(len(steps)):
                distances(n)
                if n >= 1:
                    factors(n - 1)
                kt, level = steps[n]
                if kt > 0 and level == 3:
                    for h in heads_of[kt - 1]:
                        masked(done)
                        done += 1
            factors(len(steps) - 1)
            for h in heads_of[KTILES - 1]:
                masked(done)
                done += 1
            for kt in range(KTILES):
                b, e = lg[:, kt, :], ee[:, kt % 2, :]
                if kt >= 2:
                    dve.wait_ge(*E3.dve.at(f"kh{kt - 2}"))
                else:
                    dve.wait_ge(*E3.dve.at(f"qk{len(steps) - 1}"))
                for lo, n, c in ((0, NCE, CE), (TP, NB, ST)):
                    bb = b[:, lo:lo + n * c].rearrange("p (n c) -> p n c", c=c)
                    ins = dve.tensor_tensor(e[:, lo:lo + n * c].rearrange("p (n c) -> p n c", c=c),
                                            bb[:, :, c - 1:c].to_broadcast([P, n, c]), bb, ALU.subtract)
                ins.then_inc(*E3.dve.done(f"eh{kt}"))
                dve.wait_ge(*E3.act.at(f"eq{kt}"))
                dve.tensor_tensor(kk[:, kt, :], kk[:, kt, :], e, ALU.mult).then_inc(*E3.dve.done(f"kh{kt}"))
                dve.tensor_tensor(qq[:, kt, :], qq[:, kt, :], b, ALU.mult)
                dve.tensor_copy(ebl[:, kt, 0:NCE], b[:, 0:TP].rearrange("p (n c) -> p n c", c=CE)[:, :, CE - 1])
                dve.tensor_copy(ebl[:, kt, NCE:NCE + NB], b[:, TP:T].rearrange("p (n c) -> p n c", c=ST)[:, :, ST - 1]
                                ).then_inc(*E3.dve.done(f"qh{kt}"))

        def act_scores(act):
            for n in range(len(steps)):
                act.wait_ge(*E3.dve.at(f"e{n}"))
                w = span(steps[n][1])
                act.activation(ee[:, n % 2, 0:w], ee[:, n % 2, 0:w], ACT.Exp).then_inc(*E3.act.done(f"e{n}"))
            for kt in range(KTILES):
                act.wait_ge(*E3.dve.at(f"eh{kt}"))
                act.activation(ee[:, kt % 2, :], ee[:, kt % 2, :], ACT.Exp)
                act.activation(lg[:, kt, :], lg[:, kt, :], ACT.Exp).then_inc(*E3.act.done(f"eq{kt}"))

        def pe_scores(pe):
            for s in range(2):
                pe.wait_ge(bank_free[s], used["w_out"][s])
            pe.wait_ge(*E2.dve.at("qb"))
            pe.wait_ge(*E2.dve.at("kb3"))
            for j, (kt, h) in enumerate(jobs):
                _, r0, dk = rows(h)
                b0 = 4 * (j % 2)
                if j >= 2:
                    pe.wait_ge(*E3.dve.at(f"ps{jobs[j - 2][1]}"))
                for level in range(LEVELS + 1):
                    left = kk[r0:r0 + dk, kt, :] if level == 0 else qk[r0:r0 + dk, level - 1, :]
                    right = qq[r0:r0 + dk, kt, :] if level == 0 else left
                    if level:
                        pe.wait_ge(*E3.dve.at(f"qk{steps.index((kt, level))}"))
                    for c in range(NCE):
                        at = (level % 2) * 256 + (c // 2) * CE
                        mm = pe.matmul(ps[64 * (c % 2):64 * (c % 2) + CE, b0 + level // 2, at:at + CE],
                                       left[:, c * CE:(c + 1) * CE], right[:, c * CE:(c + 1) * CE],
                                       start=True, stop=True)
                    if level <= 2:
                        at = 256 + 32 * level
                        pe.matmul(ps[0:TS, b0 + 3, at:at + TS], left[:, TP:T], right[:, TP:T], start=True, stop=True)
                mm.then_inc(*E3.pe.done(f"g{h}"))

        gla_out, hgrn_out, out_sem = sem("gla_sample_out"), sem("hgrn_sample_out"), sem("outputs_out")
        prompt_out = sem("even_prompt_states_out")
        loads4 = [Signal(sem(f"even_states{i}"), f"even_states{i}", seen, known) for i in range(KTILES)]

        def pe_chunks(pe):
            for j in range(KTILES):
                b0 = 2 * (j % 4)
                pe.wait_ge(*E3.dve.at(f"kh{j}"))
                if j < 4:
                    pe.wait_ge(*E3.dve.at(f"ps{HA + HB - 1}"))
                else:
                    pe.wait_ge(*E4.act.at(f"kt{j - 4}"))
                for c in range(4):
                    pe.transpose(ps[:, b0, c * P:(c + 1) * P], kk[:, j, c * P:(c + 1) * P], ident[:, :])
                pe.transpose(ps[0:TS, b0 + 1, 0:P], kk[:, j, TP:T], ident[:, :]).then_inc(*E4.pe.done(f"kt{j}"))
            pe.wait_ge(*E4.act.at(f"kt{KTILES - 1}"))
            pe.wait_ge(*E3.dve.at(f"qh{KTILES - 1}"))
            for c in range(NCE):
                b0 = 4 * (c % 2)
                r, tt = 64 * (c % 2), c // 2
                if c >= 2:
                    pe.wait_ge(*E4.act.at(f"o{c - 2}"))
                    pe.wait_ge(*E4.dve.at(f"s{c - 2}_{KTILES - 1}"))
                for h in range(8):
                    kt, r0, dk = rows(h)
                    mm = pe.matmul(ps[r0:r0 + dk, b0 + 1 + kt // 4, (kt % 4) * DV:(kt % 4 + 1) * DV],
                              ktok[r:r + CE, tt, kt * P + r0:kt * P + r0 + dk],
                              vtok[r:r + CE, tt, h * DV:(h + 1) * DV], start=True, stop=True)
                mm.then_inc(*E4.pe.done(f"s{c}"))
                for h in range(8):
                    mm = pe.matmul(ps[:, b0, h * CE:(h + 1) * CE], vtok[r:r + CE, tt, h * DV:(h + 1) * DV],
                                   pT[r:r + CE, h, tt, :], start=h == 0, stop=c == 0, skip_group_check=True)
                if c > 0:
                    even, odd = [0, 2], [1, 3]
                    for i, h in enumerate((even if r == 0 else odd) + [4, 5, 6, 7] + (odd if r == 0 else even)):
                        kt, r0, dk = rows(h)
                        pe.wait_ge(*E4.dve.at(f"s{c - 1}_{kt}"))
                        if i == 6:
                            pe.wait_ge(*E4.pe.at(f"rows{c}"))
                        mm = pe.matmul(ps[:, b0, h * CE:(h + 1) * CE], state[c % 2][r0:r0 + dk, kt, :],
                                       qq[r0:r0 + dk, kt, c * CE:(c + 1) * CE], start=False, stop=True,
                                       skip_group_check=True)
                        if i == 5:
                            mm.then_inc(*E4.pe.done(f"rows{c}"))
                mm.then_inc(*E4.pe.done(f"o{c}"))
            pe.wait_ge(*E4.act.at(f"o{NCE - 1}"))
            pe.wait_ge(*E4.dve.at(f"s{NCE - 1}_{KTILES - 1}"))
            for kt in range(KTILES):
                b0 = 4 * (kt % 2)
                pe.wait_ge(*loads4[kt].at(f"ss{kt}"))
                if kt >= 2:
                    pe.wait_ge(*E4.dve.at(f"ss{kt - 2}"))
                for h in heads_of[kt]:
                    _, r0, dk = rows(h)
                    pe.wait_ge(*E4.pool.at(f"vx{h}"))
                    for g in range(2):
                        mm = pe.matmul(ps[r0:r0 + dk, b0 + g, :], ktok[0:TS, 4, kt * P + r0:kt * P + r0 + dk],
                                       vx[0:TS, h % 2, 4 * g:4 * g + 4, :].rearrange("p b v -> p (b v)"), start=True,
                                       stop=True)
                    mm.then_inc(*E4.pe.done(f"vx{h}"))
                for h in heads_of[kt]:
                    _, r0, dk = rows(h)
                    if h > 0:
                        pe.wait_ge(*E4.pe.at(f"so{h - 1}"))
                    pe.matmul(ps[:, 3, h * TS:(h + 1) * TS], vtok[0:TS, 4, h * DV:(h + 1) * DV], pT[0:TS, h, 4, 0:TS],
                              start=True, stop=False, skip_group_check=True)
                    for b in range(NB):
                        mm = pe.matmul(ps[:, 3, h * TS + b * ST:h * TS + (b + 1) * ST], sst[kt][r0:r0 + dk, b, :],
                                       qq[r0:r0 + dk, kt, TP + b * ST:TP + (b + 1) * ST], start=False, stop=True,
                                       skip_group_check=True)
                    mm.then_inc(*E4.pe.done(f"so{h}"))

        def act_chunks(act):
            for j in range(KTILES):
                b0 = 2 * (j % 4)
                act.wait_ge(*E4.pe.at(f"kt{j}"))
                if j == 0:
                    act.wait_ge(*E2.dve.at("lf3"))
                act.activation(ktok[:, 0:4, j * P:(j + 1) * P], ps[:, b0, :].rearrange("p (c k) -> p c k", c=4),
                               ACT.Copy)
                act.activation(ktok[0:TS, 4, j * P:(j + 1) * P], ps[0:TS, b0 + 1, 0:P], ACT.Copy).then_inc(
                    *E4.act.done(f"kt{j}"))
            for c in range(NCE):
                act.wait_ge(*E4.pe.at(f"o{c}"))
                act.activation(oT[:, :, c * CE:(c + 1) * CE], ps[:, 4 * (c % 2), :].rearrange("p (h t) -> p h t", h=8),
                               ACT.Copy).then_inc(*E4.act.done(f"o{c}"))
            act.wait_ge(*E4.dve.at(f"s{NCE - 1}_{KTILES - 1}"))
            for kt in range(KTILES):
                if kt < 2:
                    dst = o["gla_prompt"][0, 0][2 * kt:2 * kt + 2].rearrange("h k v -> (h k) v")
                else:
                    dst = o["hgrn_prompt"][0, 0][kt - 2]
                act.dma_start(dst, state[0][:, kt, :]).then_inc(prompt_out, 16)
            act.wait_ge(*E4.pe.at("so7"))
            act.activation(oT[:, :, TP:T], ps[:, 3, 0:8 * TS].rearrange("p (h t) -> p h t", h=8), ACT.Copy).then_inc(
                *E4.act.done("os"))

        def dve_chunks(dve):
            for c in range(NCE):
                b0 = 4 * (c % 2)
                for kt in range(KTILES):
                    src = ps[:, b0 + 1 + kt // 4, (kt % 4) * DV:(kt % 4 + 1) * DV]
                    dve.wait_ge(*E4.pe.at(f"s{c}"))
                    if c == 0:
                        dve.tensor_copy(state[1][:, kt, :], src).then_inc(*E4.dve.done(f"s{c}_{kt}"))
                        continue
                    dve.wait_ge(*E4.dve.at(f"s{c - 1}_{kt}"))
                    if c > 1:
                        dve.wait_ge(*E4.pe.at(f"o{c - 1}"))
                    dve.scalar_tensor_tensor(out=state[(c + 1) % 2][:, kt, :], in0=state[c % 2][:, kt, :], scalar=ebl[:, kt, c:c + 1],
                                             in1=src, op0=ALU.mult, op1=ALU.add).then_inc(*E4.dve.done(f"s{c}_{kt}"))
            for kt in range(KTILES):
                b0 = 4 * (kt % 2)
                dve.wait_ge(*E4.pe.at(f"so{heads_of[kt][-1]}"))
                dve.wait_ge(*loads4[kt].at(f"ss{kt}"))
                new = sst[kt]
                dve.tensor_tensor(new, new, ebl[:, kt, NCE:NCE + NB].unsqueeze(2).to_broadcast([P, NB, DV]),
                                  ALU.mult).then_inc(*E4.dve.done(f"sm{kt}"))
                dve.wait_ge(*E4.dve.at(f"sm{kt}"))
                new = new.rearrange("p (g b) v -> p g (b v)", g=2)
                dve.tensor_tensor(new, new, ps[:, b0:b0 + 2, :], ALU.add).then_inc(*E4.dve.done(f"ss{kt}"))

        def pool_chunks(pool):
            pool.wait_ge(mm_ok[0], used["w_out"][0])
            pool.wait_ge(mm_ok[1], used["w_out"][1])

            def sample_state(name, kt):
                if kt < 2:
                    return [(64 * i, 64, a[name[0]][0][:, 2 * kt + i].rearrange("b k v -> k b v")) for i in range(2)]
                return [(0, P, a[name[1]][0][:, kt - 2].rearrange("b k v -> k b v"))]

            def load(kt):
                parts = sample_state(("state_gla", "state_hgrn"), kt)
                for n, (r0, nr, src) in enumerate(parts):
                    d = pool.dma_start(sst[kt][r0:r0 + nr, :, :], src)
                    d.then_inc(*loads4[kt].loaded(f"ss{kt}"))

            load(0)
            load(1)
            pool.wait_ge(*E3.dve.at(f"ps{HA + HB - 1}"))
            pool.wait_ge(*E3.dve.at(f"qh{KTILES - 1}"))
            for kt in range(2, KTILES):
                load(kt)
            vxs = [h for kt in range(KTILES) for h in heads_of[kt]]
            for h in vxs[0:2]:
                masked_values(pool, h)
            for h in vxs[2:]:
                masked_values(pool, h)
            for kt in range(KTILES):
                pool.wait_ge(*E4.dve.at(f"ss{kt}"))
                for r0, nr, dst in sample_state_out(kt):
                    pool.dma_start(dst, sst[kt][r0:r0 + nr, :, :]).then_inc(gla_out if kt < 2 else hgrn_out, 16)

        def masked_values(pool, h):
            if h >= 2:
                pool.wait_ge(*E4.pe.at(f"vx{h - 2}"))
            pool.tensor_tensor(vx[0:TS, h % 2, :, :],
                               vtok[0:TS, 4, h * DV:(h + 1) * DV].unsqueeze(1).to_broadcast([TS, NB, DV]),
                               batE[0:TS, :].unsqueeze(2).to_broadcast([TS, NB, DV]), ALU.mult).then_inc(
                *E4.pool.done(f"vx{h}"))

        def sample_state_out(kt):
            if kt < 2:
                return [(64 * i, 64, o["gla_sample"][0][:, 2 * kt + i].rearrange("b k v -> k b v")) for i in range(2)]
            return [(0, P, o["hgrn_sample"][0][:, kt - 2].rearrange("b k v -> k b v"))]

        def act_gate(act):
            act.wait_ge(*E4.act.at("os"))
            for h in range(8):
                if h >= 2:
                    act.wait_ge(*E5.pe.at(f"m{h - 2}"))
                act.activation(sq[:, h % 2, :], oT[:, h, :], ACT.Square).then_inc(*E5.act.done(f"sq{h}"))
                act.wait_ge(*E5.pe.at(f"m{h}"))
                if h >= 2:
                    act.wait_ge(*E5.dve.at(f"n{h - 2}"))
                act.activation(two(rstd[:, h % 2, :]), ps[:, 4 + 2 * (h % 2):6 + 2 * (h % 2), 0:TH], ACT.Sqrt,
                               bias=eps_rms, scale=1.0 / DV).then_inc(*E5.act.done(f"m{h}"))
                if h >= 1:
                    head(act, h - 1)
            head(act, 7)

        def head(act, h):
            act.wait_ge(*E5.dve.at(f"y{h}"))
            act.activation(xh[:, h, :], nrm[:, h % 2, :], ACT.Copy).then_inc(*E5.act.done(f"h{h}"))

        def pe_gate(pe):
            for h in range(8):
                pe.wait_ge(*E5.act.at(f"sq{h}"))
                if h == 0:
                    pe.wait_ge(*E4.dve.at(f"ss{KTILES - 1}"))
                if h >= 2:
                    pe.wait_ge(*E5.act.at(f"m{h - 2}"))
                for g in range(2):
                    mm = pe.matmul(ps[:, 4 + 2 * (h % 2) + g, 0:TH], ones[:, :], sq[:, h % 2, g * TH:(g + 1) * TH],
                                   start=True, stop=True)
                mm.then_inc(*E5.pe.done(f"m{h}"))

        def dve_gate(dve):
            dve.wait_ge(gla_out, 16 * 4)
            dve.wait_ge(prompt_out, 16 * KTILES)
            dve.wait_ge(*E4.act.at("os"))
            for h in range(8):
                gain = col("gla_norm") if h < HA else col("hgrn_norm")
                y = nrm[:, h % 2, :]
                dve.wait_ge(*E5.act.at(f"m{h}"))
                dve.reciprocal(rstd[:, h % 2, :], rstd[:, h % 2, :]).then_inc(*E5.dve.done(f"r{h}"))
                dve.wait_ge(*E5.dve.at(f"r{h}"))
                if h >= 2:
                    dve.wait_ge(*E5.dve.at(f"l{h - 2}"))
                dve.scalar_tensor_tensor(out=y, in0=oT[:, h, :], scalar=gain, in1=rstd[:, h % 2, :], op0=ALU.mult,
                                         op1=ALU.mult).then_inc(*E5.dve.done(f"n{h}"))
                dve.wait_ge(*E5.dve.at(f"n{h}"))
                dve.tensor_tensor(y, y, gate[:, h, :], ALU.mult).then_inc(*E5.dve.done(f"y{h}"))
                dve.wait_ge(*E5.act.at(f"h{h}"))
                dve.tensor_tensor(xl[:, h, :], y, xh[:, h, :].bitcast(F32), ALU.subtract).then_inc(
                    *E5.dve.done(f"l{h}"))

        def add_stage(name, ready, norm=None):
            n, units = stages[name]

            def pe_part(pe):
                pe_stage(pe, name, ready)

            def act_part(act):
                def body(i, last):
                    for s in range(2):
                        act.wait_ge(mm_ok[s], used[name][s] + i + 1)
                        ahead(act_head, act, name, s, i, last)
                        if norm is not None:
                            act.wait_ge(bank_free[s], used[name][s] + i + 1)
                            square(act, norm, s, 2 * i + s)
                each(act, n, name, body)

            def dve_part(dve):
                if norm is not None:
                    clear_sum(dve, norm)

                def body(i, last):
                    for s in range(2):
                        dve.wait_ge(mm_ok[s], used[name][s] + i + 1)
                        h = hT[:, ds(2 * i + s, 1), :].rearrange("p one (h t) -> p (one h) t", h=2)
                        dve.tensor_tensor(h, h, out2(s), ALU.add).then_inc(bank_free[s], 1)
                        ahead(dve_rest, dve, name, s, i, last)
                        if norm is not None:
                            add_squares(dve, norm, s, 2 * i + s)
                each(dve, n, name, body)

            return pe_part, act_part, dve_part

        def gate_ready(pe, k):
            pe.wait_ge(*E5.dve.at(f"l{k}"))

        norm_f0 = Norm("ffn0", lambda k: col("norm_ffn", k), "up00", 0)
        out_even = add_stage("w_out", gate_ready, norm_f0)

        def act_hgrn_out(act):
            act.wait_ge(hgrn_out, 16 * 4)

        silu_ok, prod_ok = sem("ffn_silu"), sem("ffn_product")
        hhead_ok, hrest_ok = sem("hidden_head"), sem("hidden_rest")
        sig_ok, gated_ok, added_ok = sem("ple_sigmoid"), sem("ple_gated"), sem("ple_added")
        ptok = cols(MIXF, 5, PLE)
        pf = cols(MIXF + 5 * PLE, PLE // P, T)
        act_out = cols(MIXF + 5 * PLE + 2 * T, T)
        prod = cols(MIXF + 5 * PLE + 3 * T, T)

        norm_o = Norm("mix1", lambda k: col("norm_mix", 8 + k), "rw_r", 2, out=cols(21760, KT, T))
        norm_f1 = Norm("ffn1", lambda k: col("norm_ffn", 8 + k), "up10", 3, at=21760)

        yT = cols(4 * T, KT, T)
        ytok = cols(12 * T, 5, D)
        norm_y = Norm("final", lambda k: col("norm_final", k), "final", 5, out=yT)

        def first_counts(dve):
            for s in (sum_ok, prod_ok, hrest_ok, hhead_ok, gated_ok, added_ok):
                dve.sem_inc(s, 1)

        def tail_of(i):
            S = Section(f"ple_in{i}")
            last = [(bank_free[s], used[f"up{i}0"][s]) for s in range(2)]
            norm_f = norm_f0 if i == 0 else norm_f1
            norm_p = Norm(f"ple{i}", lambda k: col("norm_ple", 8 * i + k), f"ple{i}", 3 * i + 1)
            norm_n = norm_o if i == 0 else norm_y

            def act_in(act):
                for r in last:
                    act.wait_ge(*r)
                act.dma_start(ptok[:, 0:4, :], a["p_prompt"][i, 0].rearrange("(a p) d -> p a d", p=P)).then_inc(
                    *S.dma.loaded("pp"))
                act.dma_start(ptok[0:TS, 4, :], a["p_sample"][i].rearrange("b t d -> (b t) d")).then_inc(
                    *S.dma.loaded("p"))

            def pe_in(pe):
                pe.wait_ge(*S.dma.at("p"))
                for tt in range(5):
                    n = P if tt < 4 else TS
                    bank = 4 + tt if tt < 2 else 6 + tt % 2
                    if tt == 4:
                        pe.wait_ge(*S.dve.at("t2"))
                    for k in range(2):
                        mm = pe.transpose(ps[:, bank, k * n:(k + 1) * n], ptok[0:n, tt, k * P:(k + 1) * P],
                                          ident[0:n, 0:n])
                    mm.then_inc(*S.pe.done(f"t{tt}"))

            def dve_in(dve):
                for tt in range(5):
                    n = P if tt < 4 else TS
                    bank = 4 + tt if tt < 2 else 6 + tt % 2
                    dve.wait_ge(*S.pe.at(f"t{tt}"))
                    dve.tensor_copy(pf[:, :, tt * P:tt * P + n],
                                    ps[:, bank, 0:2 * n].rearrange("p (k t) -> p k t", k=2)).then_inc(
                        *S.dve.done(f"t{tt}"))
                dve.wait_ge(*S.act.at("head"))
                dve.tensor_tensor(ple[:, 1, :, :], pf, ple[:, 0, :, :].bitcast(F32), ALU.subtract).then_inc(
                    *S.dve.done("rest"))

            def act_split(act):
                act.wait_ge(*S.dve.at("t4"))
                act.activation(ple[:, 0, :, :], pf, ACT.Copy).then_inc(*S.act.done("head"))

            def up(half):
                name = f"up{i}{half}"
                base = FT * (2 * i + half) + 1

                def pe_part(pe):
                    pe_stage(pe, name, tile_ready(norm_f) if half == 0 else None)

                def act_part(act):
                    def body(j, last):
                        act.wait_ge(mm_ok[0], used[name][0] + j + 1)
                        ahead(act_head, act, name, 0, j, last)
                        act.wait_ge(prod_ok, base + j)
                        act.activation(two(act_out), out2(0), ACT.Silu).then_inc(bank_free[0], 1)
                        act.wait_ge(bank_free[0], used[name][0] + j + 1)
                        act.sem_inc(silu_ok, 1)
                        act.wait_ge(mm_ok[1], used[name][1] + j + 1)
                        ahead(act_head, act, name, 1, j, last)
                        act.wait_ge(prod_ok, base + j + 1)
                        act.activation(hid[:, 0, ds(j, 1), :], prod.unsqueeze(1), ACT.Copy).then_inc(hhead_ok, 1)
                    each(act, FT, name, body)

                def dve_part(dve):
                    def body(j, last):
                        ahead(dve_rest, dve, name, 0, j, last)
                        dve.wait_ge(bank_free[0], used[name][0] + j + 1)
                        dve.wait_ge(mm_ok[1], used[name][1] + j + 1)
                        dve.wait_ge(hrest_ok, base + j)
                        dve.tensor_tensor(two(prod), two(act_out), out2(1), ALU.mult).then_inc(prod_ok, 1)
                        dve.wait_ge(prod_ok, base + j + 1)
                        dve.sem_inc(bank_free[1], 1)
                        ahead(dve_rest, dve, name, 1, j, last)
                        dve.wait_ge(hhead_ok, base + j + 1)
                        dve.tensor_tensor(hid[:, 1, ds(j, 1), :], prod.unsqueeze(1),
                                          hid[:, 0, ds(j, 1), :].bitcast(F32), ALU.subtract).then_inc(hrest_ok, 1)
                    each(dve, FT, name, body)

                return dict(tensor=pe_part, scalar=act_part, vector=dve_part)

            def down(half):
                def hidden(pe, k):
                    pe.wait_ge(hrest_ok, FT * (2 * i + half) + k + 2)
                pe_part, act_part, dve_part = add_stage(f"down{i}{half}", hidden, norm_p if half else None)
                return dict(tensor=pe_part, scalar=act_part, vector=dve_part)

            name = f"ple{i}"

            def pe_ple(pe):
                pe.wait_ge(*S.dve.at("rest"))
                pe_stage(pe, name, tile_ready(norm_p))

            def act_ple(act):
                def body(j, last):
                    act.wait_ge(mm_ok[0], used[name][0] + j + 1)
                    ahead(act_head, act, name, 0, j, last)
                    act.wait_ge(gated_ok, 8 * i + 1 + j)
                    act.activation(two(act_out), out2(0), ACT.Sigmoid).then_inc(bank_free[0], 1)
                    act.wait_ge(mm_ok[1], used[name][1] + j + 1)
                    ahead(act_head, act, name, 1, j, last)
                    act.wait_ge(added_ok, 8 * i + j + 2)
                    if last:
                        square(act, norm_n, 1, j)
                    else:
                        square(act, norm_n, 0, j)
                each(act, 8, name, body)

            def dve_ple(dve):
                clear_sum(dve, norm_n)

                def body(j, last):
                    ahead(dve_rest, dve, name, 0, j, last)
                    dve.wait_ge(bank_free[0], used[name][0] + j + 1)
                    dve.wait_ge(mm_ok[1], used[name][1] + j + 1)
                    dve.wait_ge(added_ok, 8 * i + 1 + j)
                    dve.tensor_tensor(two(prod), two(act_out), out2(1), ALU.mult).then_inc(gated_ok, 1)
                    dve.wait_ge(gated_ok, 8 * i + j + 2)
                    dve.sem_inc(bank_free[1], 1)
                    h = hT[:, ds(j, 1), :]
                    dve.tensor_tensor(h, h, prod.unsqueeze(1), ALU.add).then_inc(added_ok, 1)
                    ahead(dve_rest, dve, name, 1, j, last)
                    add_squares(dve, norm_n, 1 if last else 0, j)
                each(dve, 8, name, body)

            return [norm_part(norm_f), dict(scalar=act_in), up(0), down(0),
                    dict(tensor=pe_in, scalar=act_split, vector=dve_in), up(1), down(1),
                    norm_part(norm_p), dict(tensor=pe_ple, scalar=act_ple, vector=dve_ple)]

        F = Section("final")
        def act_final(act):
            for j, (tt, half) in enumerate((t, k) for t in range(5) for k in range(2)):
                n = P if tt < 4 else TS
                act.wait_ge(*F.pe.at(f"t{j}"))
                act.activation(ytok[0:n, tt, half * 512:half * 512 + 512], ps[0:n, 4 + j % 4, :], ACT.Copy).then_inc(
                    *F.act.done(f"t{j}"))

        def pe_final(pe):
            pe.wait_ge(*norm_y.s.act.at("ln"))
            for j, (tt, half) in enumerate((t, k) for t in range(5) for k in range(2)):
                n = P if tt < 4 else TS
                if j >= 4:
                    pe.wait_ge(*F.act.at(f"t{j - 4}"))
                if j < 2:
                    pe.wait_ge(*norm_y.s.dve.at(f"y{4 * half + 3}"))
                for k in range(4):
                    mm = pe.transpose(ps[0:n, 4 + j % 4, k * P:(k + 1) * P], yT[:, 4 * half + k, tt * P:tt * P + n],
                                      ident[:, :])
                mm.then_inc(*F.pe.done(f"t{j}"))

        def pool_final(pool):
            for tt in range(4):
                pool.wait_ge(*F.act.at(f"t{2 * tt + 1}"))
                pool.dma_start(o["y_prompt"][0, tt * P:(tt + 1) * P, :], ytok[:, tt, :]).then_inc(out_sem, 16)
            pool.wait_ge(*F.act.at("t9"))
            pool.dma_start(o["y_sample"].rearrange("b t d -> (b t) d"), ytok[0:TS, 4, :]).then_inc(out_sem, 16)
            pool.wait_ge(out_sem, 16 * OUTS)
            pool.wait_ge(prompt_out, 16 * KTILES)
            pool.wait_ge(gla_out, 16 * 4)
            pool.wait_ge(hgrn_out, 16 * 4)

        O0 = Section("odd_mix")
        O1 = Section("odd_proj")
        O2 = Section("odd_quads")
        O3 = Section("odd_gate")
        kb = mix[:, 0:8704].rearrange("p (i n s t) -> p i n s t", i=KT, n=NCO, s=2)
        qr = mix[:, 8704:17408].rearrange("p (i n s t) -> p i n s t", i=KT, n=NCO, s=2)
        vF = cols(17408, KT, T)
        dx = vF
        xn = cols(21760, KT, T)
        hs = mix[:, 21760:21760 + NB * 512].rearrange("p (b i v) -> p b i v", b=NB, i=KT)
        SC0 = 26112
        ymix = cols(SC0, 2, T)
        t1, t2, e1, e2 = (cols(SC0 + (2 + i) * T, T) for i in range(4))
        gs = cols(SC0 + 6 * T, T)
        omka = mix[:, SC0 + 7 * T:SC0 + 7 * T + KT]
        shT = mix[:, SC0 + 7 * T + 8:SC0 + 7 * T + 88]
        hst = mix[:, SC0:SC0 + 512].rearrange("p (i v) -> p i v", i=KT)
        rb_ = mix[:, SC0 + 512:SC0 + 1536].rearrange("p (g i v) -> p g i v", g=2, i=KT)
        lio = mix[:, SC0 + 1536:SC0 + 1536 + 1024]
        rts = mix[:, SC0 + 2560:SC0 + 3072].rearrange("p (i s t) -> p i s t", i=KT, s=2)
        wc = raw[:, :, D + TH:D + TH + 96].rearrange("p s (i n) -> p s i n", i=4)
        small = nc.alloc_sbuf_tensor_at("odd_small", [P, 8704], F32, offset=xs_byte)
        w1 = small[:, 0:512].rearrange("p (k n) -> p k n", k=KT)
        a1 = small[:, 512:1024].rearrange("p (k n) -> p k n", k=KT)
        w2, a2 = small[0:64, 1024:2048], small[0:64, 2048:3072]
        lw_, la_ = small[0:64, 3072:3072 + T], small[0:64, 3072 + T:3072 + 2 * T]
        quad = nc.alloc_sbuf_tensor_at("odd_quad", [P, 8704], F32, offset=xs_byte)
        vu = quad[:, 0:2048].rearrange("p (c g i v) -> p c g i v", c=2, g=2, i=KT)
        kbt = quad[:, 2048:4096].rearrange("p (c i k) -> p c i k", c=2, i=KT)
        sc = quad[:, 4096:6144].rearrange("p (c g i t) -> p c g i t", c=2, g=2, i=KT)
        aT, xT, xx, bT, pp = (quad[:, 6144 + 512 * i:6144 + 512 * (i + 1)] for i in range(5))
        vux = quad[0:64, 4096 + 1024:4096 + 2048]
        g2s = nc.alloc_sbuf_tensor_at("odd_gate_w", [P, 8704], F32, offset=xs_byte)
        resetO = tab[:, 0:T]
        s16 = tab[0:HC, 0:T]
        same = tab[:, 544:672]
        lvO = tab[:, 672:832].rearrange("p (l t) -> p l t", l=5)
        scm = tab[:, 832:960].rearrange("p (m t) -> p m t", m=2)
        hsel = tab[:, 960:1088].rearrange("p (k h) -> p k h", k=KT)
        batO = tab[:, 1088:1096]
        chunked = lambda ap: ap.rearrange("p (n t) -> p n t", t=CO)


        def act_mix(act):
            act.wait_ge(added_ok, 9)
            for i in range(2):
                act.wait_ge(mm_ok[i], used["rw_r"][i])
            act.dma_start(tab[:, 0:1096], a["odd_tables"]).then_inc(*O0.dma.loaded("tab"))
            act.dma_start(w1, a["rw_w1"][0].rearrange("(k p) n -> p k n", p=P)).then_inc(*O0.dma.loaded("w1"))
            act.dma_start(a1, a["rw_a1"][0].rearrange("(k p) n -> p k n", p=P)).then_inc(*O0.dma.loaded("a1"))
            act.dma_start(w2, a["rw_w2"][0]).then_inc(*O0.dma.loaded("w2"))
            act.dma_start(a2, a["rw_a2"][0]).then_inc(*O0.dma.loaded("all"))

        def act_mix2(act):
            act.wait_ge(*O0.pe.at(f"mix{KT - 1}"))
            act.activation(lw_.rearrange("p (h t) -> p h t", h=2), ps[0:64, 4:6, 0:TH], ACT.Tanh).then_inc(
                *O0.act.done("lw"))
            act.wait_ge(*O0.pe.at(f"mix{2 * KT - 1}"))
            act.activation(la_.rearrange("p (h t) -> p h t", h=2), ps[0:64, 6:8, 0:TH], ACT.Copy).then_inc(
                *O0.act.done("la"))
            for i in range(KT):
                act.wait_ge(*O0.pe.at(f"w2{i}"))
                b0 = 2 * (i % 2)
                if i >= 2:
                    act.wait_ge(*O0.dve.at(f"a{i - 2}"))
                act.activation(two((t1, t2)[i % 2]), ps[:, b0:b0 + 2, 0:TH], ACT.Sigmoid, bias=col("rw_w0", i)).then_inc(
                    *O0.act.done(f"w{i}"))
                act.wait_ge(*O0.pe.at(f"a2{i}"))
                act.activation(two((e1, e2)[i % 2]), ps[:, 4 + b0:6 + b0, 0:TH], ACT.Sigmoid, bias=col("rw_a0", i)).then_inc(
                    *O0.act.done(f"a{i}"))

        def dve_mix(dve):
            dve.wait_ge(*norm_o.s.dve.at(f"y{KT - 1}"))
            pr = TP - 1
            dve.tensor_tensor(dx[:, :, 1:TP], xn[:, :, 0:pr], xn[:, :, 1:TP], ALU.subtract)
            dve.tensor_scalar(dx[:, :, 0:1], xn[:, :, 0:1], -1.0, None, ALU.mult)
            ends = xn[:, :, TP - 1:TP]
            dve.tensor_copy(shT[:, 0:KT].unsqueeze(2), ends)
            last = vec[:, 1, VCOL["state_shift"][1]:VCOL["state_shift"][1] + 64].rearrange("p (b k) -> p k b", k=KT)
            for k in range(KT):
                x4 = xn[:, k, TP:T].rearrange("p (b t) -> p b t", t=ST)
                d4 = dx[:, k, TP:T].rearrange("p (b t) -> p b t", t=ST)
                dve.tensor_tensor(d4[:, :, 1:ST], x4[:, :, 0:ST - 1], x4[:, :, 1:ST], ALU.subtract)
                dve.tensor_tensor(d4[:, :, 0], last[:, k, :], x4[:, :, 0], ALU.subtract)
                mm = dve.tensor_copy(shT[:, KT:KT + 64].rearrange("p (b k) -> p k b", k=KT)[:, k, :],
                                     x4[:, :, ST - 1])
            mm.then_inc(*O0.dve.done("dx"))
            dve.wait_ge(*O0.dve.at("dx"))
            dve.tensor_scalar(omka, vec[:, 1, VCOL["rw_ka"][1]:VCOL["rw_ka"][1] + KT], -1.0, 1.0, ALU.mult,
                              ALU.add).then_inc(*O0.dve.done("omka"))
            for m, name in ((1, "lw"), (4, "la")):
                for k in range(KT):
                    j = (0 if m == 1 else KT) + k
                    if j >= 2:
                        dve.wait_ge(*O0.pe.at(f"mix{j - 2}"))
                    dve.scalar_tensor_tensor(out=ymix[:, k % 2, :], in0=dx[:, k, :], scalar=col("rw_mu", 8 * m + k),
                                             in1=xn[:, k, :], op0=ALU.mult, op1=ALU.add).then_inc(
                        *O0.dve.done(f"mix{j}"))
            dve.wait_ge(*O0.pe.at("shift"))
            dve.tensor_copy(lioS, ps[0:72, 3, 0:P]).then_inc(*O0.dve.done("shift"))
            for i in range(KT):
                t, u = (t1, t2)[i % 2], (e1, e2)[i % 2]
                dve.wait_ge(*O0.act.at(f"w{i}"))
                dve.tensor_scalar(qr[:, i, :, 0, :], chunked(t), -float(np.exp(-0.5)), None, ALU.mult).then_inc(
                    *O0.dve.done(f"lw{i}"))
                dve.tensor_scalar(t, t, -float(np.exp(-0.5)), None, ALU.mult).then_inc(*O0.dve.done(f"lt{i}"))
                dve.wait_ge(*O0.dve.at(f"lt{i}"))
                dve.tensor_tensor_scan(t, resetO, t, 0.0, ALU.mult, ALU.add).then_inc(*O0.dve.done(f"b{i}"))
                dve.wait_ge(*O0.dve.at(f"b{i}"))
                dve.tensor_copy(qr[:, i, :, 1, :], chunked(t))
                dve.wait_ge(*O0.act.at(f"a{i}"))
                dve.tensor_copy(kb[:, i, :, 0, :], chunked(u)).then_inc(*O0.dve.done(f"a{i}"))

        def pe_mix(pe):
            pe.wait_ge(*O0.dma.at("all"))
            pe.wait_ge(*norm_o.s.act.at("ln"))
            for m, w in enumerate((w1, a1)):
                for k in range(KT):
                    j = m * KT + k
                    pe.wait_ge(*O0.dve.at(f"mix{j}"))
                    for h in range(2):
                        mm = pe.matmul(ps[0:64, 4 + 2 * m + h, 0:TH], w[:, k, :], ymix[:, k % 2, h * TH:(h + 1) * TH],
                                       start=k == 0, stop=k == KT - 1)
                    mm.then_inc(*O0.pe.done(f"mix{j}"))
            for s in range(2):
                pe.wait_ge(bank_free[s], used["rw_r"][s])
            pe.transpose(ps[0:72, 3, 0:P], shT[:, 0:72], ident[:, :]).then_inc(*O0.pe.done("shift"))
            pe.wait_ge(*O0.dve.at("shift"))
            pe.wait_ge(*O0.act.at("la"))
            for i in range(KT):
                b0 = 2 * (i % 2)
                if i >= 2:
                    pe.wait_ge(*O0.act.at(f"a{i - 2}"))
                for w, x, b, name in ((w2, lw_, b0, "w2"), (a2, la_, 4 + b0, "a2")):
                    for h in range(2):
                        mm = pe.matmul(ps[:, b + h, 0:TH], w[:, i * P:(i + 1) * P], x[:, h * TH:(h + 1) * TH],
                                       start=True, stop=True)
                    mm.then_inc(*O0.pe.done(f"{name}{i}"))

        lioS = small[0:72, 4224:4352]

        def pool_shift(pool):
            pool.wait_ge(*O0.dve.at("shift"))
            pool.dma_start(o["shift_prompt"].rearrange("i b (k c) -> (i b k) c", c=P), lioS[0:KT, :]).then_inc(out_sem, 16)
            pool.dma_start(o["shift_sample"].rearrange("i b (k c) -> (i b k) c", c=P), lioS[KT:72, :]).then_inc(
                out_sem, 16)

        mixes = {"rw_r": 0, "rw_k": 2, "rw_g1": 5, "rw_v": 3}
        seq = ["rw_r", "rw_k", "rw_g1", "rw_v"]

        ymixes = [two(ymix[:, 1, :]), raw[:, :, D:D + TH], two(resetO)]

        def mixed(dve, name, k):
            if k >= 3:
                dve.wait_ge(*O1.dve.at(f"{name}l{k - 3}"))
            elif name != seq[0]:
                dve.wait_ge(*O1.dve.at(f"{seq[seq.index(name) - 1]}l{KT - 1}"))
            else:
                dve.wait_ge(*O0.pe.at(f"mix{2 * KT - 1}"))
            dve.scalar_tensor_tensor(out=ymixes[k % 3], in0=two(dx[:, k, :]),
                                     scalar=col("rw_mu", 8 * mixes[name] + k), in1=two(xn[:, k, :]), op0=ALU.mult,
                                     op1=ALU.add).then_inc(*O1.dve.done(f"{name}y{k}"))

        def dve_x(dve, name):
            for k in range(3):
                mixed(dve, name, k)
            for k in range(KT):
                dve.wait_ge(*O1.act.at(f"{name}h{k}"))
                dve.tensor_tensor(two(xl[:, k, :]), ymixes[k % 3], two(xh[:, k, :].bitcast(F32)),
                                  ALU.subtract).then_inc(*O1.dve.done(f"{name}l{k}"))
                if k + 3 < KT:
                    mixed(dve, name, k + 3)

        def act_x(act, name):
            at = seq.index(name)
            if at == 0:
                act.wait_ge(*O0.act.at(f"a{KT - 1}"))
                act.wait_ge(*O0.pe.at(f"a2{KT - 1}"))
                act.wait_ge(out_sem, 16 * 2)
            for k in range(KT):
                if at > 0 and k < KT - 1:
                    act.wait_ge(x_free, (KT - 1) * (at - 1) + k + 1)
                elif at > 0:
                    for s in range(2):
                        act.wait_ge(mm_ok[s], used[name][s])
                act.wait_ge(*O1.dve.at(f"{name}y{k}"))
                act.activation(two(xh[:, k, :]), ymixes[k % 3], ACT.Copy).then_inc(*O1.act.done(f"{name}h{k}"))

        def x_ready(name):
            def ready(pe, k):
                pe.wait_ge(*O1.dve.at(f"{name}l{k}"))
            return ready

        def units_of(name):
            n, units = stages[name]
            return [(i, s, len(units) * i + s, i == n - 1) for i in range(n) for s in range(len(units))]

        def plain(eng_split, name):
            def run(eng):
                for i, s, t, last in units_of(name):
                    eng.wait_ge(mm_ok[s], used[name][s] + i + 1)
                    ahead(eng_split, eng, name, s, i, last)
            return run

        def dve_r(dve):
            for i, s, t, last in units_of("rw_r"):
                if t == KT - 1:
                    dve_x(dve, "rw_k")
                dve.wait_ge(mm_ok[s], used["rw_r"][s] + i + 1)
                ahead(dve_rest, dve, "rw_r", s, i, last)

        def act_r(act):
            for i, s, t, last in units_of("rw_r"):
                if t == KT - 1:
                    act_x(act, "rw_k")
                act.wait_ge(mm_ok[s], used["rw_r"][s] + i + 1)
                ahead(act_head, act, "rw_r", s, i, last)
                act.activation(kb[:, t, 0:8, 1, :], chunked(ps[:, 2 * s, 0:256]), ACT.Copy)
                act.activation(kb[:, t, 8, 1, 0:16], ps[:, 2 * s, 256:272], ACT.Copy)
                act.activation(kb[:, t, 8, 1, 16:32], ps[:, 2 * s + 1, 0:16], ACT.Copy)
                act.activation(kb[:, t, 9:17, 1, :], chunked(ps[:, 2 * s + 1, 16:272]), ACT.Copy).then_inc(
                    bank_free[s], 1)

        def act_k(act):
            for i, s, t, last in units_of("rw_k"):
                if t == KT - 1:
                    act_x(act, "rw_g1")
                act.wait_ge(mm_ok[s], used["rw_k"][s] + i + 1)
                ahead(act_head, act, "rw_k", s, i, last)
                if t == KT - 1:
                    act_g1(act)
                    act_x(act, "rw_v")
                if t > 0:
                    act.wait_ge(*O1.dve.at(f"end{t - 1}"))
                act.activation(two(t1), out2(s), ACT.Copy, scale=col("rw_kk", t))
                act.activation(two(e1), out2(s), ACT.Square, scale=col("rw_kk", t)).then_inc(*O1.act.done(f"sq{t}"))
                act.wait_ge(*O1.dve.at(f"nn{t}"))
                act.activation(e2, e2, ACT.Ln, scale=float(2.0 ** 17)).then_inc(*O1.act.done(f"ln{t}"))
                act.wait_ge(*O1.act.at(f"ln{t}"))
                act.activation(e2, e2, ACT.Exp, scale=-0.5, bias=bias17).then_inc(*O1.act.done(f"rs{t}"))
                act.wait_ge(*O1.dve.at(f"d{t}"))
                act.activation(e1, e1, ACT.Exp).then_inc(*O1.act.done(f"e1{t}"))
                act.wait_ge(*O1.dve.at(f"kn{t}"))
                act.activation(chunked(e2), qr[:, t, :, 1, :], ACT.Exp, scale=-1.0).then_inc(*O1.act.done(f"e2{t}"))
                act.wait_ge(*O1.dve.at(f"kk{t}"))
                act.activation(chunked(e1), qr[:, t, :, 1, :], ACT.Exp).then_inc(*O1.act.done(f"e3{t}"))

        def pe_k(pe):
            for i, s, t, last in units_of("rw_k"):
                unit_products(pe, "rw_k", i, s, x_ready("rw_k") if t == 0 else None, t == KT - 1)
                if t == 0:
                    pe.wait_ge(*O0.act.at(f"a{KT - 1}"))
                else:
                    k_sums(pe, t - 1)
            pe_stage(pe, "rw_g1", x_ready("rw_g1"), freed=True)
            unit_products(pe, "rw_v", 0, 0, x_ready("rw_v"))
            k_sums(pe, KT - 1)
            for i, s, t, last in units_of("rw_v")[1:]:
                unit_products(pe, "rw_v", i, s)

        def k_sums(pe, t):
            pe.wait_ge(*O1.act.at(f"sq{t}"))
            for h in range(2):
                mm = pe.matmul(ps[:, 4 + h, 0:TH], same, e1[:, h * TH:(h + 1) * TH], start=True, stop=True)
            mm.then_inc(*O1.pe.done(f"nn{t}"))
            pe.wait_ge(*O1.dve.at(f"s{t}"))
            for h in range(2):
                mm = pe.matmul(ps[0:HC, 6 + h, 0:TH], hsel[:, t, :], t2s[:, h * TH:(h + 1) * TH], start=t == 0,
                               stop=t == KT - 1)
            mm.then_inc(*O1.pe.done(f"s{t}"))

        t2s = ymix[:, 0, :]

        def dve_k(dve):
            for i, s, t, last in units_of("rw_k"):
                if t == KT - 1:
                    dve_x(dve, "rw_g1")
                dve.wait_ge(mm_ok[s], used["rw_k"][s] + i + 1)
                ahead(dve_rest, dve, "rw_k", s, i, last)
                if t == KT - 1:
                    plain(dve_rest, "rw_g1")(dve)
                    dve_x(dve, "rw_v")
                dve.wait_ge(*O1.pe.at(f"nn{t}"))
                dve.tensor_scalar(two(e2), ps[:, 4:6, 0:TH], 1e-24, None, ALU.max).then_inc(*O1.dve.done(f"nn{t}"))
                dve.tensor_tensor(chunked(e1), qr[:, t, :, 1, :], qr[:, t, :, 0, :], ALU.subtract).then_inc(
                    *O1.dve.done(f"d{t}"))
                dve.tensor_scalar(chunked(t2), kb[:, t, :, 0, :], col("rw_ka", t), omka[:, t:t + 1], ALU.mult,
                                  ALU.add).then_inc(*O1.dve.done(f"f{t}"))
                dve.wait_ge(*O1.dve.at(f"f{t}"))
                dve.tensor_tensor(two(t2), two(t2), out2(s), ALU.mult).then_inc(*O1.dve.done(f"kp{t}"))
                dve.wait_ge(*O1.dve.at(f"kp{t}"))
                dve.wait_ge(*O1.act.at(f"sq{t}"))
                dve.sem_inc(bank_free[s], 1)
                if t > 0:
                    dve.wait_ge(*O1.pe.at(f"s{t - 1}"))
                dve.scalar_tensor_tensor(out=chunked(t2s), in0=chunked(t2), scalar=col("rw_rk", t),
                                         in1=kb[:, t, :, 1, :], op0=ALU.mult, op1=ALU.mult).then_inc(
                    *O1.dve.done(f"s{t}"))
                dve.wait_ge(*O1.act.at(f"rs{t}"))
                dve.tensor_tensor(t1, t1, e2, ALU.mult).then_inc(*O1.dve.done(f"kn{t}"))
                dve.wait_ge(*O1.act.at(f"e1{t}"))
                dve.wait_ge(*O1.dve.at(f"kn{t}"))
                dve.tensor_tensor(qr[:, t, :, 0, :], chunked(t1), chunked(e1), ALU.mult).then_inc(
                    *O1.dve.done(f"kk{t}"))
                dve.tensor_tensor(chunked(t1), chunked(t1), kb[:, t, :, 0, :], ALU.mult).then_inc(
                    *O1.dve.done(f"be{t}"))
                dve.wait_ge(*O1.act.at(f"e3{t}"))
                dve.wait_ge(*O1.dve.at(f"be{t}"))
                dve.tensor_tensor(qr[:, t, :, 1, :], kb[:, t, :, 1, :], chunked(e1), ALU.mult).then_inc(
                    *O1.dve.done(f"r{t}"))
                dve.tensor_copy(wc[:, t // 4, t % 4, 0:16], chunked(e1)[:, 0:16, CO - 1])
                dve.tensor_copy(wc[:, t // 4, t % 4, 16:24], e1[:, TP:T].rearrange("p (b t) -> p b t", t=ST)[:, :, ST - 1])
                dve.tensor_tensor(kb[:, t, :, 0, :], chunked(t2), chunked(e2), ALU.mult)
                dve.wait_ge(*O1.dve.at(f"r{t}"))
                dve.tensor_tensor(kb[:, t, :, 1, :], chunked(t1), chunked(e2), ALU.mult).then_inc(
                    *O1.dve.done(f"end{t}"))
            dve.wait_ge(*O1.pe.at(f"s{KT - 1}"))
            dve.tensor_copy(two(s16), ps[0:HC, 6:8, 0:TH]).then_inc(*O1.dve.done("s16"))

        def act_g1(act):
            for i, s, t, last in units_of("rw_g1"):
                act.wait_ge(mm_ok[s], used["rw_g1"][s] + i + 1)
                ahead(act_head, act, "rw_g1", s, i, last)
                act.activation(two(gs), out2(s), ACT.Sigmoid).then_inc(bank_free[s], 1)

        def dve_v(dve):
            for i, s, t, last in units_of("rw_v"):
                dve.wait_ge(mm_ok[s], used["rw_v"][s] + i + 1)
                ahead(dve_rest, dve, "rw_v", s, i, last)
                if t == 0:
                    dve.wait_ge(*O1.dve.at(f"rw_vl{KT - 1}"))
                dve.tensor_copy(two(vF[:, t, :]), out2(s)).then_inc(bank_free[s], 1)

        odd_parts = [
            dict(scalar=act_mix),
            norm_part(norm_o),
            dict(tensor=pe_mix, scalar=act_mix2, vector=dve_mix, gpsimd=pool_shift),
            dict(tensor=lambda e: pe_stage(e, "rw_r", x_ready("rw_r"), freed=True),
                 scalar=lambda e: (act_x(e, "rw_r"), act_r(e)), vector=lambda e: (dve_x(e, "rw_r"), dve_r(e))),
            dict(tensor=pe_k, scalar=act_k, vector=dve_k),
            dict(scalar=plain(act_head, "rw_v"), vector=dve_v),
        ]

        QUADS = TP // P
        slot_in = [sem("state_in_even"), sem("state_in_odd")]
        slot_out = [sem("state_out_even"), sem("state_out_odd")]
        id32 = mix[:, SC0 + 3072:SC0 + 3072 + CO]
        spread = mix[0:HC, D:2 * D]
        g2 = mix[:, 0:D]
        heads2 = [(g, i) for i in range(KT) for g in range(2)]

        def quad_shape(q):
            return (list(range(4)), P, 2, P) if q < QUADS else ([0], 64, 1, TS)

        def spots(q):
            js, _, ncp, _ = quad_shape(q)
            return [(2 * par + g, cp, g, i) for cp in range(ncp) for i in range(KT) for par in range(min(2, len(js)))
                    for g in range(2)]

        def level_count(q):
            return 5 if q < QUADS else 2

        def blocks(ap, q):
            js, pr, ncp, _ = quad_shape(q)
            return ap[0:pr, 0:256 * ncp].rearrange("p (c t) -> p c t", t=CO)

        def at_block(ap, tile, cp, i):
            c = (cp * KT + i) * CO
            return ap[32 * tile:32 * tile + 32, c:c + CO]

        def pe_quad(pe, q):
            js, pr, ncp, nt = quad_shape(q)
            first = q == 0
            if first:
                for s in range(2):
                    pe.wait_ge(bank_free[s], used["rw_o"][s])
                pe.wait_ge(*O1.dve.at("s16"))
            else:
                pe.wait_ge(*O2.dve.at(f"H{4 * q - 1}"))
                pe.wait_ge(*O2.act.at(f"o{4 * q - 1}"))
            for cp in range(ncp):
                for g in range(2):
                    for par in range(min(2, len(js))):
                        n = 4 * q + 2 * cp + par
                        for i in range(KT):
                            mm = pe.matmul(ps[64 * par:64 * par + 64, 2 * cp + g, i * 64:(i + 1) * 64],
                                           kb[64 * g:64 * g + 64, i, n, :, :], qr[64 * g:64 * g + 64, i, n, :, :],
                                           start=True, stop=True)
                    mm.then_inc(*O2.pe.done(f"sc{q}{cp}{g}"))
            for b in range(2):
                for i in range(4):
                    mm = pe.transpose(ps[0:nt, 4 + b, i * P:(i + 1) * P], vF[:, 4 * b + i, q * P:q * P + nt], ident[:, :])
                mm.then_inc(*O2.pe.done(f"vt{q}{b}"))
            for j, (cp, half) in enumerate((c, h) for c in range(ncp) for h in range(2)):
                bank = (6, 7, 4, 5)[j]
                if j == 2:
                    pe.wait_ge(*O2.act.at(f"vt{q}"))
                    pe.wait_ge(*O2.dve.at(f"vt{q}"))
                n = 4 * q + 2 * cp
                for i in range(4):
                    mm = pe.transpose(ps[0:pr, bank, i * P:(i + 1) * P], kb[:, 4 * half + i, n:n + (pr // 64), :, :],
                                      ident[:, :])
                mm.then_inc(*O2.pe.done(f"kt{q}{j}"))
            if q == QUADS:
                pe_rts(pe)
            for level in range(2, level_count(q) + 1):
                pe.wait_ge(*O2.dve.at(f"b{q}{level}"))
                for k, (tile, cp, g, i) in enumerate(spots(q)):
                    mm = pe.matmul(at_block(ps[:, 0, :], tile, cp, i), at_block(bT, tile, cp, i),
                                   at_block(xx, tile, cp, i), start=True, stop=True)
                mm.then_inc(*O2.pe.done(f"P{q}{level}"))
                pe.wait_ge(*O2.act.at(f"P{q}{level}"))
                for k, (tile, cp, g, i) in enumerate(spots(q)):
                    mm = pe.matmul(at_block(ps[:, 1, :], tile, cp, i), at_block(pp, tile, cp, i),
                                   at_block(xT, tile, cp, i), start=True, stop=True)
                mm.then_inc(*O2.pe.done(f"X{q}{level}"))
            pe.wait_ge(*O2.act.at(f"kt{q}"))
            pe.wait_ge(*O2.dve.at(f"x{q}{level_count(q)}"))
            for j in js:
                pe_chunk(pe, q, j)

        def pe_chunk(pe, q, j):
            n, cp, par = 4 * q + j, j // 2, j % 2
            rb, sample = 64 * par, q == QUADS
            for g in range(2):
                for i in range(KT):
                    mm = pe.matmul(ps[rb + 32 * g:rb + 32 * g + 32, 2 + g, i * NC:(i + 1) * NC],
                                   sc[rb:rb + 32, cp, g, i, 0:CO], vu[rb:rb + 32, cp, g, i, :],
                                   start=i == 0, stop=False, skip_group_check=True)
            mm.then_inc(*O2.pe.done(f"av{n}" if n else "R0"))
            if sample:
                pe.wait_ge(*O2.dve.at("rts"))
            elif n > 0:
                pe.wait_ge(*O2.dve.at(f"H{n - 1}"))
                pe.wait_ge(*O2.act.at(f"o{n - 1}"))
            if n > 0:
                pe.wait_ge(*O2.pe.at(f"av{n}"))
                for g in range(2):
                    r = slice(64 * g, 64 * g + 64)
                    for i in range(KT):
                        w = rts[r, i, 0, :] if sample else qr[r, i, n, 0, :]
                        x = ident[r, r] if sample else hst[r, i, :]
                        mm = pe.matmul(ps[rb + 32 * g:rb + 32 * g + 32, 2 + g, i * NC:(i + 1) * NC], w, x, start=False,
                                       stop=True, skip_group_check=True)
                mm.then_inc(*O2.pe.done(f"R{n}"))
                for g in range(2):
                    r = slice(64 * g, 64 * g + 64)
                    for i in range(KT):
                        w = ident[r, r] if sample else hst[r, i, :]
                        x = rts[r, i, 1, :] if sample else qr[r, i, n, 1, :]
                        pe.matmul(ps[r, 6, i * CO:(i + 1) * CO], w, x, start=i == 0, stop=False, skip_group_check=True)
            pe.wait_ge(*O2.act.at(f"R{n}"))
            pe.wait_ge(*O2.dve.at(f"R{n}"))
            for i in range(KT):
                for g in range(2):
                    rows_g = slice(rb + 32 * g, rb + 32 * g + 32)
                    mm = pe.matmul(ps[rb + 32:rb + 64, 4 + g, i * NC:(i + 1) * NC], at_block(xT, 2 * par + g, cp, i),
                                   rb_[rows_g, g, i, :], start=True, stop=True)
            mm.then_inc(*O2.pe.done(f"U{n}"))
            pe.wait_ge(*O2.act.at(f"U{n}"))
            pe.wait_ge(*O2.dve.at(f"U{n}"))
            r = slice(rb, rb + 64)
            if not sample:
                for i in range(KT):
                    for g in range(2):
                        mm = pe.matmul(ps[64 * g:64 * g + 64, 7, i * NC:(i + 1) * NC],
                                       kbt[r, cp, i, g * NC:(g + 1) * NC], vu[r, cp, g, i, :], start=True, stop=True)
                mm.then_inc(*O2.pe.done(f"H{n}"))
            for i in range(KT):
                for g in range(2):
                    mm = pe.matmul(ps[64 * g:64 * g + 64, 6, i * CO:(i + 1) * CO], vu[r, cp, g, i, :],
                                   sc[r, cp, g, i, CO:2 * CO], start=n == 0 and i == 0, stop=True,
                                   skip_group_check=True)
            mm.then_inc(*O2.pe.done(f"o{n}"))

        def act_quad(act, q):
            js, pr, ncp, nt = quad_shape(q)
            act.wait_ge(*O2.pe.at(f"vt{q}0"))
            for j in js:
                act.activation(vu[64 * (j % 2):64 * (j % 2) + 32, j // 2, :, 0:4, :].rearrange("p g i v -> p i g v"),
                               ps[32 * j:32 * j + 32, 4, :].rearrange("p (i g v) -> p i g v", i=4, g=2),
                               ACT.Copy).then_inc(*O2.act.done(f"vt{q}" if j == js[-1] else f"vt{q}_{j}"))
            for j in range(2 * ncp):
                act.wait_ge(*O2.pe.at(f"kt{q}{j}"))
                act.activation(kbt[0:pr, j // 2, 4 * (j % 2):4 * (j % 2) + 4, :],
                               ps[0:pr, (6, 7, 4, 5)[j], :].rearrange("p (i k) -> p i k", i=4),
                               ACT.Copy).then_inc(*O2.act.done(f"kt{q}" if j == 2 * ncp - 1 else f"kt{q}_{j}"))
            for level in range(2, level_count(q) + 1):
                act.wait_ge(*O2.pe.at(f"P{q}{level}"))
                act.activation(pp[0:pr, 0:256 * ncp], ps[0:pr, 0, 0:256 * ncp], ACT.Copy).then_inc(
                    *O2.act.done(f"P{q}{level}"))
            for j in js:
                n, rb, cp = 4 * q + j, 64 * (j % 2), j // 2
                act.wait_ge(*O2.pe.at(f"R{n}"))
                act.activation(rb_[rb:rb + 32, 0, :, :], ps[rb:rb + 32, 2, :].rearrange("p (i v) -> p i v", i=KT),
                               ACT.Copy).then_inc(*O2.act.done(f"R{n}"))
                act.wait_ge(*O2.pe.at(f"U{n}"))
                act.activation(vu[rb + 32:rb + 64, cp, 0, :, :],
                               ps[rb + 32:rb + 64, 4, :].rearrange("p (i v) -> p i v", i=KT), ACT.Copy,
                               scale=-1.0).then_inc(*O2.act.done(f"U{n}"))
                act.wait_ge(*O2.pe.at(f"o{n}"))
                act.activation(qr[:, :, n, 0, :], ps[:, 6, 0:256].rearrange("p (i t) -> p i t", i=KT),
                               ACT.Copy).then_inc(*O2.act.done(f"o{n}"))

        def dve_quad(dve, q):
            js, pr, ncp, nt = quad_shape(q)
            if q == 0:
                for k in range(4):
                    r = slice(32 * k, 32 * k + 32)
                    mm = dve.tensor_copy(id32[r, :], ident[r, r])
                mm.then_inc(*O2.dve.done("id32"))
                dve.wait_ge(*O2.dve.at("id32"))
            for cp in range(ncp):
                for g in range(2):
                    dve.wait_ge(*O2.pe.at(f"sc{q}{cp}{g}"))
                    dve.tensor_tensor(sc[0:pr, cp, g, :, :], ps[0:pr, 2 * cp + g, :].rearrange("p (i t) -> p i t", i=KT),
                                      scm[0:pr, q // QUADS, :].unsqueeze(1).to_broadcast([pr, KT, 64]),
                                      ALU.mult).then_inc(*O2.dve.done(f"sc{q}{cp}{g}"))
            dve.wait_ge(*O2.pe.at(f"vt{q}1"))
            for j in js:
                dve.tensor_copy(vu[64 * (j % 2):64 * (j % 2) + 32, j // 2, :, 4:8, :].rearrange("p g i v -> p i g v"),
                                ps[32 * j:32 * j + 32, 5, :].rearrange("p (i g v) -> p i g v", i=4, g=2)).then_inc(
                    *O2.dve.done(f"vt{q}" if j == js[-1] else f"vt{q}_{j}"))
            dve.wait_ge(*O2.dve.at(f"vt{q}"))
            for par in range(min(2, len(js))):
                for g in range(2):
                    k = 2 * par + g
                    dve.tensor_copy(aT[32 * k:32 * k + 32, 0:256 * ncp].rearrange("p (c i t) -> p c i t", c=ncp, i=KT),
                                    sc[64 * par + 32:64 * par + 64, 0:ncp, g, :, 0:CO]).then_inc(
                        *O2.dve.done(f"aT{q}{k}"))
            dve.wait_ge(*O2.dve.at(f"aT{q}{k}"))
            nb = 8 * ncp

            def halving(level):
                return lvO[0:pr, level - 1, :].unsqueeze(1).to_broadcast([pr, nb, CO])

            dve.tensor_tensor(blocks(bT, q), blocks(aT, q), halving(1), ALU.mult).then_inc(*O2.dve.done(f"b{q}1"))
            dve.wait_ge(*O2.dve.at(f"b{q}1"))
            dve.tensor_tensor(blocks(xT, q), id32[0:pr].unsqueeze(1).to_broadcast([pr, nb, CO]), blocks(bT, q),
                              ALU.subtract).then_inc(*O2.dve.done(f"x{q}1"))
            for level in range(2, level_count(q) + 1):
                dve.wait_ge(*O2.dve.at(f"x{q}{level - 1}"))
                dve.transpose(xx[0:pr, 0:32 * nb], xT[0:pr, 0:32 * nb])
                dve.tensor_tensor(blocks(bT, q), blocks(aT, q), halving(level), ALU.mult).then_inc(
                    *O2.dve.done(f"b{q}{level}"))
                dve.wait_ge(*O2.pe.at(f"X{q}{level}"))
                dve.tensor_tensor(xT[0:pr, 0:32 * nb], xT[0:pr, 0:32 * nb], ps[0:pr, 1, 0:32 * nb],
                                  ALU.subtract).then_inc(*O2.dve.done(f"x{q}{level}"))
            if q == QUADS:
                dve.wait_ge(*O2.pe.at("rts"))
                dve.tensor_copy(rts, ps[:, 7, :].rearrange("p (i s t) -> p i s t", i=KT, s=2)).then_inc(
                    *O2.dve.done("rts"))
            for j in js:
                n, rb, cp = 4 * q + j, 64 * (j % 2), j // 2
                dve.wait_ge(*O2.pe.at(f"R{n}"))
                dve.tensor_copy(rb_[rb + 32:rb + 64, 1, :, :],
                                ps[rb + 32:rb + 64, 3, :].rearrange("p (i v) -> p i v", i=KT)).then_inc(
                    *O2.dve.done(f"R{n}"))
                dve.wait_ge(*O2.pe.at(f"U{n}"))
                dve.tensor_scalar(vu[rb + 32:rb + 64, cp, 1, :, :],
                                  ps[rb + 32:rb + 64, 5, :].rearrange("p (i v) -> p i v", i=KT), -1.0, None,
                                  ALU.mult).then_inc(*O2.dve.done(f"U{n}"))
                if q == QUADS:
                    continue
                dve.wait_ge(*O2.pe.at(f"H{n}"))
                total = ps[:, 7, :].rearrange("p (i v) -> p i v", i=KT)
                if n > 0:
                    dve.tensor_tensor(hst, hst, total, ALU.add).then_inc(*O2.dve.done(f"h{n}"))
                    dve.wait_ge(*O2.dve.at(f"h{n}"))
                    total = hst
                by4 = lambda ap: ap.rearrange("p (s i) v -> p s i v", s=2)
                dve.tensor_tensor(by4(hst), by4(total), wc[:, :, :, n:n + 1].to_broadcast([P, 2, 4, NC]), ALU.mult).then_inc(
                    *O2.dve.done(f"H{n}"))

        def pool_states(pool):
            pool.wait_ge(*O1.dve.at(f"end{KT - 1}"))
            for b in range(NB):
                if b >= 2:
                    pool.wait_ge(*O2.pe.at(f"st{b - 2}"))
                pool.dma_start(lio[64 * (b % 2):64 * (b % 2) + 64, :].rearrange("p (h k) -> p h k", h=HC),
                               a["state_rwkv"][0, b].rearrange("h v k -> v h k")).then_inc(slot_in[b % 2], 16)

        def pe_states(pe, b0):
            pe.wait_ge(*(O2.act.at(f"o{2 * b0 - 1}") if b0 else O1.dve.at("s16")))
            if b0:
                pe.wait_ge(*O2.dve.at(f"H{2 * b0 - 1}"))
            for b in (b0, b0 + 1):
                r = slice(64 * (b % 2), 64 * (b % 2) + 64)
                pe.wait_ge(slot_in[b % 2], 8 * (b - b % 2) + 16)
                for i in range(KT):
                    mm = pe.transpose(ps[:, 6 + b % 2, i * NC:(i + 1) * NC], lio[r, i * P:(i + 1) * P], ident[r, r])
                mm.then_inc(*O2.pe.done(f"st{b}"))
            pe.wait_ge(*O2.act.at(f"st{b0}"))
            pe.wait_ge(*O2.dve.at(f"st{b0 + 1}"))

        def act_states(act, b):
            act.wait_ge(*O2.pe.at(f"st{b}"))
            act.activation(hs[:, b, :, :], ps[:, 6, :].rearrange("p (i v) -> p i v", i=KT), ACT.Copy).then_inc(
                *O2.act.done(f"st{b}"))

        def dve_states(dve, b):
            dve.wait_ge(*O2.pe.at(f"st{b}"))
            dve.tensor_copy(hs[:, b, :, :], ps[:, 7, :].rearrange("p (i v) -> p i v", i=KT)).then_inc(
                *O2.dve.done(f"st{b}"))

        def pe_rts(pe):
            pe.wait_ge(*O2.act.at(f"kt{QUADS}"))
            for b in range(NB):
                for i in range(KT):
                    for g in range(2):
                        r = slice(64 * g, 64 * g + 64)
                        out = ps[r, 7, i * 64:(i + 1) * 64].rearrange("p (s t) -> p s t", s=2)
                        mm = pe.matmul(out[:, :, b * ST:(b + 1) * ST], hs[r, b, i, :],
                                       qr[r, i, NCO - 1, :, b * ST:(b + 1) * ST], start=True, stop=True)
            mm.then_inc(*O2.pe.done("rts"))

        def pe_new_states(pe):
            for k, (g, i) in enumerate(heads2):
                bank = i % 2
                pe.wait_ge(*O2.dve.at(f"vx{k}"))
                if k >= 4 and g == 0:
                    pe.wait_ge(*O2.dve.at(f"ns{i - 2}"))
                pe.matmul(ps[64 * g:64 * g + 64, bank, :], kbt[0:64, 0, i, g * NC:(g + 1) * NC],
                          vux2[k % 2], start=True, stop=True).then_inc(*O2.pe.done(f"ns{k}"))
            for b in range(NB + 1):
                b0 = 2 + 2 * (b % 2)
                if b == 0:
                    pe.wait_ge(*O2.dve.at(f"ns{KT - 1}"))
                elif b >= 2:
                    pe.wait_ge(*O2.act.at(f"so{b - 2}"))
                    pe.wait_ge(*O2.dve.at(f"so{b - 2}"))
                for i in range(KT):
                    src = hs[:, b, i, :] if b < NB else hst[:, i, :]
                    mm = pe.transpose(ps[0:64, b0 + i // 4, (i % 4) * P:(i % 4 + 1) * P], src, ident[:, :])
                mm.then_inc(*O2.pe.done(f"so{b}"))

        vux2 = [quad[0:64, 5120 + 512 * k:5632 + 512 * k] for k in range(2)]

        def dve_new_states(dve):
            dve.wait_ge(*O2.act.at(f"U{4 * QUADS}"))
            dve.wait_ge(*O2.dve.at(f"U{4 * QUADS}"))
            for k, (g, i) in enumerate(heads2):
                if k >= 2:
                    dve.wait_ge(*O2.pe.at(f"ns{k - 2}"))
                dve.tensor_tensor(vux2[k % 2].rearrange("p (b v) -> p b v", b=NB),
                                  vu[0:64, 0, g, i, :].unsqueeze(1).to_broadcast([64, NB, NC]),
                                  batO[0:64, :].unsqueeze(2).to_broadcast([64, NB, NC]), ALU.mult).then_inc(
                    *O2.dve.done(f"vx{k}"))
                if k % 2 == 0 and i > 0:
                    new_state(dve, i - 1)
            new_state(dve, KT - 1)
            dve.wait_ge(*O2.dve.at(f"ns{KT - 1}"))
            for b in range(NB + 1):
                state_rows(dve, O2.dve, b)

        def new_state(dve, i):
            dve.wait_ge(*O2.pe.at(f"ns{2 * i + 1}"))
            h = hs[:, :, i, :]
            dve.tensor_tensor(h, h, ps[:, i % 2, :].rearrange("p (b v) -> p b v", b=NB), ALU.add).then_inc(
                *O2.dve.done(f"na{i}"))
            dve.wait_ge(*O2.dve.at(f"na{i}"))
            dve.tensor_tensor(h, h, wc[:, i // 4, i % 4, 16:24].unsqueeze(2).to_broadcast([P, NB, NC]), ALU.mult).then_inc(
                *O2.dve.done(f"ns{i}"))

        def state_rows(eng, signal, b):
            half = 0 if signal is O2.act else 1
            eng.wait_ge(*O2.pe.at(f"so{b}"))
            if b >= 2:
                eng.wait_ge(slot_out[b % 2], 16 * (b // 2))
            elif half == 0:
                eng.wait_ge(*O2.pe.at(f"st{NB - 2 + b}"))
            dst = lio[64 * (b % 2):64 * (b % 2) + 64, half * 512:half * 512 + 512]
            src = ps[0:64, 2 + 2 * (b % 2) + half, :]
            if half == 0:
                eng.activation(dst, src, ACT.Copy).then_inc(*signal.done(f"so{b}"))
            else:
                eng.tensor_copy(dst, src).then_inc(*signal.done(f"so{b}"))

        def pool_out(pool):
            pool.wait_ge(*O2.pe.at(f"kt{QUADS}1"))
            pool.dma_start(g2, a["rw_g2"][0]).then_inc(*O3.dma.loaded("g2"))
            pool.dma_start(spread, a["head_spread"]).then_inc(*O3.dma.loaded("all"))
            for b in range(NB + 1):
                pool.wait_ge(*O2.act.at(f"so{b}"))
                pool.wait_ge(*O2.dve.at(f"so{b}"))
                dst = o["rwkv_sample"][0, b] if b < NB else o["rwkv_prompt"][0, 0]
                pool.dma_start(dst.rearrange("h v k -> v h k"),
                               lio[64 * (b % 2):64 * (b % 2) + 64, :].rearrange("p (h k) -> p h k", h=HC)).then_inc(
                    slot_out[b % 2], 16)

        ot, xc, sqo, rso, bo = (cols(2 * D + 2 * T * i, 2, T) for i in range(5))

        def act_ogate(act):
            act.wait_ge(*O2.pe.at(f"kt{QUADS}1"))
            for i in range(KT + 1):
                if i < KT:
                    if i >= 2:
                        act.wait_ge(*O3.dve.at(f"xc{i - 2}"))
                    else:
                        act.wait_ge(*O2.act.at(f"o{4 * QUADS}"))
                    act.activation(chunked(ot[:, i % 2, :]), qr[:, i, :, 0, :], ACT.Copy).then_inc(
                        *O3.act.done(f"o{i}"))
                if i > 0:
                    k = i - 1
                    act.wait_ge(*O3.dve.at(f"y{k}"))
                    act.activation(xh[:, k, :], bo[:, k % 2, :], ACT.Copy).then_inc(*O3.act.done(f"h{k}"))
                if i == KT:
                    continue
                act.wait_ge(*O3.dve.at(f"xc{i}"))
                act.activation(sqo[:, i % 2, :], xc[:, i % 2, :], ACT.Square).then_inc(*O3.act.done(f"sq{i}"))
                act.wait_ge(*O3.pe.at(f"var{i}"))
                act.activation(two(rso[:, i % 2, :]), ps[:, 6:8, 0:TH], ACT.Ln, bias=eps_gn, scale=1.0 / NC).then_inc(
                    *O3.act.done(f"ln{i}"))
                act.wait_ge(*O3.act.at(f"ln{i}"))
                act.activation(rso[:, i % 2, :], rso[:, i % 2, :], ACT.Exp, scale=-0.5).then_inc(*O3.act.done(f"rs{i}"))

        def pe_ogate(pe):
            pe.wait_ge(*O2.act.at(f"so{NB}"))
            pe.wait_ge(*O2.dve.at(f"so{NB}"))
            pe.wait_ge(*O3.dma.at("all"))
            pe.wait_ge(*O1.dve.at("s16"))
            for i in range(KT):
                pe.wait_ge(*O3.act.at(f"o{i}"))
                if i > 0:
                    pe.wait_ge(*O3.dve.at(f"xc{i - 1}"))
                for h in range(2):
                    mm = pe.matmul(ps[:, 4 + h, 0:TH], same, ot[:, i % 2, h * TH:(h + 1) * TH], start=True, stop=True)
                mm.then_inc(*O3.pe.done(f"mean{i}"))
                if i > 0:
                    pe.wait_ge(*O3.dve.at(f"y{i - 1}"))
                for h in range(2):
                    pe.matmul(ps[:, h, 0:TH], spread[:, i * P:(i + 1) * P], s16[:, h * TH:(h + 1) * TH], start=True,
                              stop=True)
                for h in range(2):
                    mm = pe.matmul(ps[:, 2 + h, 0:TH], g2[:, i * P:(i + 1) * P], gs[:, h * TH:(h + 1) * TH], start=True,
                                   stop=True)
                mm.then_inc(*O3.pe.done(f"g{i}"))
                pe.wait_ge(*O3.act.at(f"sq{i}"))
                for h in range(2):
                    mm = pe.matmul(ps[:, 6 + h, 0:TH], same, sqo[:, i % 2, h * TH:(h + 1) * TH], start=True, stop=True)
                mm.then_inc(*O3.pe.done(f"var{i}"))

        def dve_ogate(dve):
            for i in range(KT):
                y, x = bo[:, i % 2, :], xc[:, i % 2, :]
                dve.wait_ge(*O3.pe.at(f"mean{i}"))
                if i >= 2:
                    dve.wait_ge(*O3.dve.at(f"l{i - 2}"))
                dve.scalar_tensor_tensor(out=two(x), in0=ps[:, 4:6, 0:TH], scalar=-1.0 / NC,
                                         in1=two(ot[:, i % 2, :]), op0=ALU.mult, op1=ALU.add).then_inc(
                    *O3.dve.done(f"xc{i}"))
                dve.wait_ge(*O3.pe.at(f"g{i}"))
                dve.tensor_tensor(two(y), ps[:, 0:2, 0:TH], two(vF[:, i, :]), ALU.mult).then_inc(
                    *O3.dve.done(f"bo{i}"))
                dve.wait_ge(*O3.act.at(f"rs{i}"))
                dve.scalar_tensor_tensor(out=x, in0=x, scalar=col("rw_lnw", i), in1=rso[:, i % 2, :], op0=ALU.mult,
                                         op1=ALU.mult).then_inc(*O3.dve.done(f"n{i}"))
                dve.wait_ge(*O3.dve.at(f"n{i}"))
                dve.scalar_tensor_tensor(out=y, in0=x, scalar=col("rw_lnb", i), in1=y, op0=ALU.add,
                                         op1=ALU.add).then_inc(*O3.dve.done(f"on{i}"))
                dve.wait_ge(*O3.dve.at(f"on{i}"))
                dve.tensor_tensor(two(y), two(y), ps[:, 2:4, 0:TH], ALU.mult).then_inc(*O3.dve.done(f"y{i}"))
                dve.wait_ge(*O3.act.at(f"h{i}"))
                dve.tensor_tensor(xl[:, i, :], y, xh[:, i, :].bitcast(F32), ALU.subtract).then_inc(
                    *O3.dve.done(f"l{i}"))

        def o_ready(pe, k):
            if k == 0:
                pe.wait_ge(*O3.dve.at(f"y{KT - 1}"))
            pe.wait_ge(*O3.dve.at(f"l{k}"))

        out_odd = add_stage("rw_o", o_ready, norm_f1)

        def states_out(eng):
            eng.wait_ge(slot_out[0], 16 * (NB // 2 + 1))
            eng.wait_ge(slot_out[1], 16 * (NB // 2))

        odd_late = [dict(gpsimd=pool_states)]
        for _q in range(QUADS + 1):
            def _pe(e, q=_q):
                if q < 4:
                    pe_states(e, 2 * q)
                pe_quad(e, q)

            def _act(e, q=_q):
                if q < 4:
                    act_states(e, 2 * q)
                act_quad(e, q)

            def _dve(e, q=_q):
                if q < 4:
                    dve_states(e, 2 * q + 1)
                dve_quad(e, q)
            odd_late.append(dict(tensor=_pe, scalar=_act, vector=_dve))
        odd_late += [
            dict(tensor=pe_new_states, scalar=lambda e: [state_rows(e, O2.act, b) for b in range(NB + 1)],
                 vector=dve_new_states, gpsimd=pool_out),
            dict(tensor=pe_ogate, scalar=act_ogate, vector=dve_ogate),
            dict(tensor=out_odd[0], scalar=lambda e: (out_odd[1](e), states_out(e)), vector=out_odd[2]),
        ]
        OUTS = 2 + 5

        tail_parts = [tail_of(0), tail_of(1)]

        todo = [
            dict(sync=lambda e: [sp_stage(e, n) for n in order[:order.index("rw_r")]]),
            dict(vector=first_counts),
            dict(tensor=pe_embed, scalar=act_embed, vector=dve_embed),
            dict(scalar=lambda e: [act_head(e, "v_a", s, 0) for s in range(2)],
                 vector=lambda e: [dve_rest(e, "v_a", s, 0) for s in range(2)]),
            norm_part(norm0),
            dict(tensor=pe_even_in, scalar=act_even_in, vector=dve_even_in),
            dict(scalar=act_decay, vector=dve_decay),
            dict(tensor=pe_scores, scalar=act_scores, vector=dve_scores),
            dict(tensor=pe_chunks, scalar=act_chunks, vector=dve_chunks, gpsimd=pool_chunks),
            dict(tensor=pe_gate, scalar=act_gate, vector=dve_gate),
            dict(tensor=out_even[0], scalar=out_even[1], vector=out_even[2]),
            dict(scalar=act_hgrn_out),
        ] + tail_parts[0] + [
            dict(sync=lambda e: [sp_stage(e, n) for n in order[order.index("rw_r"):order.index("rw_o") + 1]]),
        ] + odd_parts + odd_late + [
            dict(sync=lambda e: [sp_stage(e, n) for n in order[order.index("rw_o") + 1:]]),
        ] + tail_parts[1] + [
            norm_part(norm_y), dict(tensor=pe_final, scalar=act_final, gpsimd=pool_final),
        ]
        todo = todo[:stop]
        with nc.Block() as block:
            @block.sync
            def _(sp):
                for part in todo:
                    if "sync" in part:
                        part["sync"](sp)

            @block.tensor
            def _(pe):
                for part in todo:
                    if "tensor" in part:
                        part["tensor"](pe)

            @block.scalar
            def _(act):
                for part in todo:
                    if "scalar" in part:
                        part["scalar"](act)

            @block.vector
            def _(dve):
                for part in todo:
                    if "vector" in part:
                        part["vector"](dve)

            @block.gpsimd
            def _(pool):
                for part in todo:
                    if "gpsimd" in part:
                        part["gpsimd"](pool)


_INS = ["x_prompt", "x_sample", "p_prompt", "p_sample", "state_gla", "state_hgrn", "state_rwkv", "state_shift",
        "norm_mix", "norm_ffn", "norm_ple", "norm_final", "w_in_even", "w_gk2", "b_gk", "gla_norm", "hgrn_gamma",
        "hgrn_norm", "w_out_even", "rw_mu", "rw_wr", "rw_wk", "rw_wv", "rw_wo", "rw_w0", "rw_w1", "rw_w2", "rw_a0",
        "rw_a1", "rw_a2", "rw_g1", "rw_g2", "rw_kk", "rw_ka", "rw_rk", "rw_lnw", "rw_lnb", "w_ffn_gate", "w_ffn_up",
        "w_ffn_down", "w_ple", "w_ple_gate"]
_OUTS = [("y_prompt", (1, TP, D)), ("y_sample", (NB, ST, D)), ("gla_prompt", (1, 1, HA, DKA, DV)),
         ("hgrn_prompt", (1, 1, HB, NBK, DV)), ("rwkv_prompt", (1, 1, HC, NC, NC)), ("shift_prompt", (1, 1, D)),
         ("gla_sample", (1, NB, HA, DKA, DV)), ("hgrn_sample", (1, NB, HB, NBK, DV)),
         ("rwkv_sample", (1, NB, HC, NC, NC)), ("shift_sample", (1, NB, D))]


def _constants():
    return {"ident": np.concatenate([np.eye(P), np.ones((P, P))], 1).astype(np.float32),
            "even_tables": even_tables(), "odd_tables": odd_tables(), "head_spread": head_spread()}


def build(new_core, shapes, stop=99):
    known = None
    for _ in range(2):
        nc, seen = new_core(), {}
        a = {n: nc.dram_tensor(f"in_{n}", s, F32, kind="ExternalInput").ap() for n, s in shapes.items()}
        o = {n: nc.dram_tensor(f"out_{n}", s, F32, kind="ExternalOutput").ap() for n, s in _OUTS}
        trunk(nc, a, o, known, seen, stop)
        known = seen
    return nc


def kernel(**inputs):
    import concourse.bacc as bacc
    from concourse.bass_utils import run_bass_kernel_spmd

    arrays = {n: np.ascontiguousarray(inputs[n]) for n in _INS}
    arrays.update(_constants())
    nc = build(lambda: bacc.Bacc("TRN2", target_bir_lowering=False, num_devices=1),
               {n: x.shape for n, x in arrays.items()})
    r = run_bass_kernel_spmd(nc, [{f"in_{n}": x for n, x in arrays.items()}], core_ids=[0])
    return tuple(r.results[0][f"out_{n}"] for n, _ in _OUTS)
```

```python
from contextlib import ExitStack

import numpy as np

import concourse.bass as bass
from concourse import mybir

F32 = mybir.dt.float32
F32R = mybir.dt.float32r
ACT = mybir.ActivationFunctionType
ALU = mybir.AluOpType
ds = bass.ds

P = 128
D = 1024
KT = D // P
TP = 512
NB, ST = 8, 4
TS = NB * ST
T = TP + TS
TH = T // 2
FFN = 2816
FT = FFN // P // 2
PLE = 256
RMS_EPS = 1e-6

HA, DKA, HB, NBK, DV = 4, 64, 4, 128, 128
KTILES = HA * DKA // P + HB
CE = 64
NCE = TP // CE
LEVELS = 6
EVEN_IN = {"q_a": 0, "k_a": 256, "v_a": 512, "g_a": 1024, "gk": 1536, "q_b": 1552, "f_b": 2064, "i_b": 2576,
           "g_b": 3088}
HC, NC = 16, 64
CO = 32
NCO = T // CO
GN_EPS = 64e-5


class Signal:

    def __init__(self, sem, name, seen, known):
        self.sem, self.name, self.seen, self.known, self.n = sem, name, seen, known, 0

    def done(self, step):
        self.n += 1
        assert (self.name, step) not in self.seen, (self.name, step)
        self.seen[self.name, step] = self.n
        return self.sem, 1

    def loaded(self, step):
        self.n += 16
        self.seen[self.name, step] = self.n
        return self.sem, 16

    def at(self, step):
        if self.known is not None:
            return self.sem, self.known[self.name, step]
        return self.sem, 1


VEC0 = [("norm_mix", 16), ("norm_ffn", 16), ("norm_ple", 16), ("norm_final", 8), ("b_gk", 2), ("gla_norm", 1),
        ("hgrn_gamma", 4), ("hgrn_norm", 1), ("rw_mu", 48), ("rw_w0", 8), ("rw_a0", 8)]
VEC1 = [("rw_kk", 8), ("rw_ka", 8), ("rw_rk", 8), ("rw_lnw", 8), ("rw_lnb", 8), ("state_shift", 64)]
VCOL = {}
for _half, _table in enumerate((VEC0, VEC1)):
    _at = 0
    for _name, _rows in _table:
        VCOL[_name] = (_half, _at, _rows)
        _at += _rows



def even_tables():
    p, t = np.arange(P)[:, None], np.arange(CE)[None, :]
    s = p % CE
    masks = [s == t]
    for level in range(1, LEVELS + 1):
        m = 1 << (level - 1)
        masks.append((s // (2 * m) == t // (2 * m)) & (s % (2 * m) < m) & (t % (2 * m) >= m))
    return np.concatenate(masks + [scan_resets(CE), p // ST == np.arange(NB)[None, :]], 1).astype(np.float32)


def scan_resets(chunk):
    t = np.arange(T)
    keep = np.where(t < TP, t % chunk != 0, t % ST != 0)
    return np.broadcast_to(keep, (P, T))


def odd_tables():
    p, t = np.arange(P)[:, None], np.arange(CO)[None, :]
    s = p % CO
    same_head = p // NC == np.arange(P)[None, :] // NC
    halves = []
    for level in range(1, 6):
        m = 1 << (level - 1)
        halves.append((s // (2 * m) == t // (2 * m)) & (s % (2 * m) < m) & (t % (2 * m) >= m))
    prompt = [s < t, s <= t]
    sample = [(s < t) & (s // ST == t // ST), (s <= t) & (s // ST == t // ST)]
    head = [(2 * k + p // NC) == np.arange(HC)[None, :] for k in range(KT)]
    batch = [s // ST == np.arange(NB)[None, :]]
    return np.concatenate([scan_resets(CO), same_head] + halves + prompt + sample + head + batch, 1).astype(np.float32)


def head_spread():
    return (np.arange(HC)[:, None] == np.arange(D)[None, :] // NC).astype(np.float32)


TABC = 1104


def trunk(nc, a, o, known, seen, stop=99):
    ctx = ExitStack()
    with ctx:
        def sb(name, shape, dt=F32):
            return ctx.enter_context(nc.sbuf_tensor(name, shape, dt))

        def sem(name):
            return ctx.enter_context(nc.semaphore(name))

        class Section:
            def __init__(self, name):
                def signal(by):
                    return Signal(sem(f"{name}_{by}"), f"{name}_{by}", seen, known)

                self.pe, self.act, self.dve = signal("pe"), signal("act"), signal("dve")
                self.pool, self.dma = signal("pool"), signal("dma")

        hT = sb("hT", [P, KT, T])
        xs_byte = (nc.sbuf_base + 31) // 32 * 32
        xs = sb("x_split", [P, 2 * KT * T], F32R)
        xh = xs[:, 0:KT * T].rearrange("p (k t) -> p k t", k=KT)
        xl = xs[:, KT * T:2 * KT * T].rearrange("p (k t) -> p k t", k=KT)
        raw = sb("w_raw", [P, 2, FT * P])
        wh = sb("w_head", [P, 2, FT * P], F32R)
        wl = sb("w_rest", [P, 2, FT * P], F32R)
        ident = sb("ident", [P, P])
        ones = sb("ones", [P, P])
        vec = sb("vectors", [P, 2, P])
        eps = sb("epsilons", [P, 3])
        eps_rms, eps_gn, bias17 = eps[:, 0:1], eps[:, 1:2], eps[:, 2:3]
        tab = sb("tables", [P, TABC])
        MIXC = 30016
        mix_byte = (nc.sbuf_base + 31) // 32 * 32
        mix = sb("mix", [P, MIXC])
        ps = ctx.enter_context(nc.psum_tensor("ps", [P, 8, 512], F32))

        def col(name, i=0):
            half, at, _ = VCOL[name]
            return vec[:, half, at + i:at + i + 1]

        raw_in = [sem("slabA_loaded"), sem("slabB_loaded")]
        head_ok = [sem("slabA_head"), sem("slabB_head")]
        rest_ok = [sem("slabA_rest"), sem("slabB_rest")]
        mm_ok = [sem("productA"), sem("productB")]
        bank_free = [sem("banksA_read"), sem("banksB_read")]
        x_free = sem("input_tile_read")

        def W(name, layer):
            return a[name][layer]

        w_in = W("w_in_even", 0)
        stages = {}
        order = []

        def stage(name, n, units):
            stages[name] = (n, units)
            order.append(name)

        X = (xh, xl)
        stage("v_a", 2, [(w_in, EVEN_IN["v_a"], 256, 0, KT, X), (w_in, EVEN_IN["v_a"] + 128, 256, 0, KT, X)])
        stage("i_b", 2, [(w_in, EVEN_IN["i_b"], 256, 0, KT, X), (w_in, EVEN_IN["i_b"] + 128, 256, 0, KT, X)])
        stage("gk", 1, [(w_in, EVEN_IN["gk"], 0, 0, KT, X)])
        for name, n in (("f_b", 2), ("k_a", 1), ("q_a", 1), ("q_b", 2), ("g_a", 2), ("g_b", 2)):
            stage(name, n, [(w_in, EVEN_IN[name], 256, 0, KT, X), (w_in, EVEN_IN[name] + 128, 256, 0, KT, X)])
        stage("w_out", 4, [(W("w_out_even", 0), 0, 256, 0, KT, X), (W("w_out_even", 0), 128, 256, 0, KT, X)])

        base = mix_byte
        hid = nc.alloc_sbuf_tensor_at("hidden_split", [P, 2, FT, T], F32R, offset=base)
        ple = nc.alloc_sbuf_tensor_at("ple_split", [P, 2, PLE // P, T], F32R, offset=base + 4 * 2 * FT * T)
        MIXF = 2 * FT * T + 2 * (PLE // P) * T

        def tail_stages(i):
            for half in range(2):
                c = half * FT * P
                stage(f"up{i}{half}", FT, [(W("w_ffn_gate", i), c, 128, 0, KT, X), (W("w_ffn_up", i), c, 128, 0, KT, X)])
                stage(f"down{i}{half}", 4, [(W("w_ffn_down", i), 0, 256, c, FT, (hid[:, 0], hid[:, 1])),
                                            (W("w_ffn_down", i), 128, 256, c, FT, (hid[:, 0], hid[:, 1]))])
            stage(f"ple{i}", 8, [(W("w_ple_gate", i), 0, 128, 0, KT, X),
                                 (W("w_ple", i), 0, 128, 0, PLE // P, (ple[:, 0], ple[:, 1]))])

        tail_stages(0)
        for name in ("r", "k", "g1", "v"):
            if name == "g1":
                stage("rw_g1", 1, [(W("rw_g1", 0), 0, 0, 0, KT, X)])
                continue
            w = W(f"rw_w{name}", 0)
            stage(f"rw_{name}", 4, [(w, 0, 256, 0, KT, X), (w, 128, 256, 0, KT, X)])
        stage("rw_o", 4, [(W("rw_wo", 0), 0, 256, 0, KT, X), (W("rw_wo", 0), 128, 256, 0, KT, X)])
        tail_stages(1)
        used = {}
        ab = [0, 0]
        for name in order:
            used[name] = tuple(ab)
            n, units = stages[name]
            for s in range(len(units)):
                ab[s] += n

        def each(eng, n, name, body, first=0):
            if n - first > 2:
                with eng.Fori(first, n - 1) as i:
                    body(i, False)
            else:
                for i in range(first, n - 1):
                    body(i, False)
            if n > first:
                body(n - 1, True)

        def sp_stage(sp, name):
            n, units = stages[name]

            def load(i):
                for s, (w, c, step, row, kt, _) in enumerate(units):
                    use = used[name][s] + i
                    if not (isinstance(use, int) and use == 0):
                        sp.wait_ge(rest_ok[s], use)
                    src = w[row:row + kt * P, :].rearrange("(k p) n -> p k n", p=P)
                    sp.dma_start(raw[:, s, 0:kt * P].rearrange("p (k n) -> p k n", k=kt),
                                 src[:, :, ds(i * step + c, P)]).then_inc(raw_in[s], 16)

            if n > 2:
                with sp.Fori(0, n) as i:
                    load(i)
            else:
                for i in range(n):
                    load(i)

        def act_head(act, name, s, i):
            use, kt = used[name][s] + i, stages[name][1][s][4]
            act.wait_ge(raw_in[s], 16 * use + 16)
            act.wait_ge(mm_ok[s], use)
            act.activation(wh[:, s, 0:kt * P], raw[:, s, 0:kt * P], ACT.Copy).then_inc(head_ok[s], 1)

        def dve_rest(dve, name, s, i):
            use, kt = used[name][s] + i, stages[name][1][s][4]
            dve.wait_ge(head_ok[s], use + 1)
            dve.tensor_tensor(wl[:, s, 0:kt * P], raw[:, s, 0:kt * P], wh[:, s, 0:kt * P].bitcast(F32),
                              ALU.subtract).then_inc(rest_ok[s], 1)

        def ahead(split, eng, name, s, i, last):
            if not last:
                split(eng, name, s, i + 1)
                return
            at = order.index(name) + 1
            while at < len(order) and len(stages[order[at]][1]) <= s:
                at += 1
            if at < len(order):
                split(eng, order[at], s, 0)

        def unit_products(pe, name, i, s, ready=None, freed=False):
            _, _, _, _, kt, (uh, ul) = stages[name][1][s]
            use = used[name][s] + i
            pe.wait_ge(head_ok[s], use + 1)
            pe.wait_ge(rest_ok[s], use + 1)
            pe.wait_ge(bank_free[s], use)
            for k in range(kt):
                if ready is not None:
                    ready(pe, k)
                for w, x, first in ((wh, uh, True), (wh, ul, False), (wl, uh, False)):
                    for h in range(2):
                        mm = pe.matmul(ps[:, 2 * s + h, 0:TH], w[:, s, k * P:(k + 1) * P],
                                       x[:, k, h * TH:(h + 1) * TH], start=first and k == 0,
                                       stop=k == kt - 1 and w is wl)
                if freed and k < kt - 1:
                    mm.then_inc(x_free, 1)
            mm.then_inc(mm_ok[s], 1)

        def pe_stage(pe, name, ready=None, freed=False):
            n, units = stages[name]

            def products(i, last):
                for s in range(len(units)):
                    unit_products(pe, name, i, s, freed=freed and last and s == len(units) - 1)

            first = 0
            if ready is not None:
                for s in range(len(units)):
                    unit_products(pe, name, 0, s, ready if s == 0 else None, freed and n == 1)
                first = 1
            each(pe, n, name, products, first)

        def out2(s):
            return ps[:, 2 * s:2 * s + 2, 0:TH]

        def two(ap):
            return ap.rearrange("p (h t) -> p h t", h=2)

        def cols(at, *shape):
            n = int(np.prod(shape))
            ap = mix[:, at:at + n]
            if len(shape) == 2:
                return ap.rearrange("p (a b) -> p a b", a=shape[0])
            if len(shape) == 3:
                return ap.rearrange("p (a b c) -> p a b c", a=shape[0], b=shape[1])
            return ap

        xtok = cols(0, 5, D)
        vrow = cols(5 * D, 2, P)
        vT = cols(0, KT, T)
        gate = cols(8 * T, KT, T)
        qq = cols(16 * T, KTILES, T)
        kk = cols(22 * T, KTILES, T)
        lg = cols(28 * T, KTILES, T)
        vtok = cols(34 * T, 5, D)
        ktok = cols(34 * T + 5 * D, 5, KTILES * P)
        soft = cols(34 * T + 5 * D, KTILES, T)
        pT = cols(34 * T + 5 * D + 5 * KTILES * P, 8, 5, CE)
        qk = cols(0, LEVELS, T)
        ee = cols(LEVELS * T, 2, T)
        oT = cols(22 * T, KT, T)
        sq = cols(34 * T, 2, T)
        rstd = cols(36 * T, 2, T)
        nrm = cols(38 * T, 2, T)
        lrT = cols(34 * T + 5 * D, T)
        wgk2 = cols(34 * T + 5 * D + 3300, HA * DKA)
        lbs = cols(34 * T + 5 * D + 5 * KTILES * P + 2500, 40)
        alias = nc.alloc_sbuf_tensor_at("even_scratch", [P, 8704], F32, offset=xs_byte)
        state = [alias[:, at:at + 768].rearrange("p (k v) -> p k v", k=KTILES) for at in (0, 7168)]
        sst = [alias[:, 768:1792], alias[:, 1792:2816]] + [cols(i * NB * DV, NB * DV) for i in range(4)]
        sst = [ap.rearrange("p (b v) -> p b v", b=NB) for ap in sst]
        vx = alias[:, 2816:4864].rearrange("p (a b v) -> p a b v", a=2, b=NB)
        mt = alias[:, 4864:6912].rearrange("p (a c) -> p a c", a=2)
        ebl = alias[:, 6912:7008].rearrange("p (k c) -> p k c", k=KTILES)
        lvmask = tab[:, 0:7 * CE].rearrange("p (l t) -> p l t", l=7)
        resetE = tab[:, 7 * CE:7 * CE + T]
        batE = tab[:, 7 * CE + T:7 * CE + T + NB]

        def rows(h):
            if h < HA:
                return h // 2, 64 * (h % 2), DKA
            return h - HA + 2, 0, NBK

        heads_of = [[0, 1], [2, 3], [4], [5], [6], [7]]
        jobs = [(kt, h) for kt in range(KTILES) for h in heads_of[kt]]

        E0 = Section("embed")

        x_in = sem("input_loaded")

        def act_embed(act):
            act.dma_start(ident[:, :], a["ident"][:, 0:P]).then_inc(x_in, 16)
            act.dma_start(xtok[:, 0:4, :], a["x_prompt"][0].rearrange("(a p) d -> p a d", p=P)).then_inc(x_in, 16)
            act.dma_start(xtok[0:TS, 4, :], a["x_sample"].rearrange("b t d -> (b t) d")).then_inc(x_in, 16)
            act.dma_start(ones[:, :], a["ident"][:, P:2 * P]).then_inc(*E0.dma.loaded("o"))
            act.dma_start(tab[:, 0:7 * CE + T + NB], a["even_tables"]).then_inc(*E0.dma.loaded("t"))
            for half, table in enumerate((VEC0, VEC1)):
                at = 0
                for name, n in table:
                    shape = a[name].shape
                    flat = a[name]
                    if len(shape) == 1:
                        flat = flat.rearrange("(r c) -> r c", c=P)
                    elif len(shape) == 2:
                        flat = flat.rearrange("i (r c) -> (i r) c", c=P)
                    elif name == "rw_rk":
                        flat = flat.rearrange("i (r e) c -> (i r) (e c)", e=2)
                    elif len(shape) == 3:
                        flat = flat.rearrange("i j (r c) -> (i j r) c", c=P)
                    act.dma_start(vrow[at:at + n, half, :], flat).then_inc(
                        *E0.dma.loaded("all" if name == VEC1[-1][0] else name))
                    at += n

        def pe_embed(pe):
            pe.wait_ge(x_in, 16 * 3)
            for j, (tt, k4) in enumerate((t, k) for t in range(5) for k in range(2)):
                n = P if tt < 4 else TS
                if j >= 4:
                    pe.wait_ge(*E0.dve.at(f"x{j - 4}"))
                for k in range(4):
                    mm = pe.transpose(ps[:, 4 + j % 4, k * n:(k + 1) * n],
                                      xtok[0:n, tt, (4 * k4 + k) * P:(4 * k4 + k + 1) * P], ident[0:n, 0:n])
                mm.then_inc(*E0.pe.done(f"x{j}"))
            pe.wait_ge(*E0.dma.at("all"))
            pe.wait_ge(*E0.dve.at("x7"))
            for half, n in ((0, P), (1, 104)):
                mm = pe.transpose(ps[:, 6 + half, 0:n], vrow[0:n, half, :], ident[0:n, 0:n])
            mm.then_inc(*E0.pe.done("vec"))

        def dve_embed(dve):
            dve.memset(eps_rms, RMS_EPS)
            dve.memset(eps_gn, GN_EPS)
            dve.memset(bias17, 8.5 * float(np.log(2.0)))
            for j, (tt, k4) in enumerate((t, k) for t in range(5) for k in range(2)):
                n = P if tt < 4 else TS
                dve.wait_ge(*E0.pe.at(f"x{j}"))
                dve.tensor_copy(hT[:, 4 * k4:4 * k4 + 4, tt * P:tt * P + n],
                                ps[:, 4 + j % 4, 0:4 * n].rearrange("p (k t) -> p k t", k=4)).then_inc(*E0.dve.done(f"x{j}"))
            dve.wait_ge(*E0.pe.at("vec"))
            dve.tensor_copy(vec[:, 0, :], ps[:, 6, 0:P])
            dve.tensor_copy(vec[:, 1, 0:104], ps[:, 7, 0:104]).then_inc(*E0.dve.done("vec"))
            dve.wait_ge(*E0.dve.at("vec"))

        sq_ok, sum_ok = sem("norm_square"), sem("norm_sum")

        class Norm:

            def __init__(self, name, gain, before, number=None, at=MIXC - 4 * T, out=None):
                self.s, self.gain, self.before, self.number, self.out = Section(f"norm_{name}"), gain, before, number, out
                self.sq, self.sum, self.rs = cols(at, 2, T), cols(at + 2 * T, T), cols(at + 3 * T, T)
                self.y = cols(at, 3, T)
                self.squares = None if number is None else 8 * number
                self.sums = None if number is None else 9 * number + 1

        def clear_sum(dve, n):
            dve.memset(n.sum, 0.0).then_inc(sum_ok, 1)

        def square(act, n, s, t):
            act.wait_ge(sum_ok, t + n.sums)
            act.activation(n.sq[:, s, :], hT[:, ds(t, 1), :].rearrange("p one t -> p (one t)"),
                           ACT.Square).then_inc(sq_ok, 1)

        def add_squares(dve, n, s, t):
            dve.wait_ge(sq_ok, t + (n.squares + 1))
            dve.wait_ge(sum_ok, t + (n.sums + 1))
            dve.tensor_tensor(n.sum, n.sum, n.sq[:, s, :], ALU.add).then_inc(sum_ok, 1)

        def act_norm(act, n):
            s = n.s
            if n.number is None:
                act.wait_ge(*E0.dve.at("vec"))
                for k in range(KT):
                    if k >= 2:
                        act.wait_ge(*s.dve.at(f"sum{k - 2}"))
                    act.activation(n.sq[:, k % 2, :], hT[:, k, :], ACT.Square).then_inc(*s.act.done(f"sq{k}"))
            act.wait_ge(*s.pe.at("mean"))
            act.activation(two(n.rs), ps[:, 4:6, 0:TH], ACT.Ln, bias=eps_rms, scale=1.0 / D).then_inc(*s.act.done("ln"))
            act.wait_ge(*s.act.at("ln"))
            act.activation(n.rs, n.rs, ACT.Exp, scale=-0.5).then_inc(*s.act.done("rstd"))
            if n.out is None:
                for i in range(2):
                    act.wait_ge(mm_ok[i], used[n.before][i])
                for k in range(KT):
                    act.wait_ge(*(s.dve if k % 2 == 0 else s.pool).at(f"y{k}"))
                    act.activation(xh[:, k, :], n.y[:, k % 3, :], ACT.Copy, scale=n.gain(k)).then_inc(*s.act.done(f"h{k}"))

        def scaled(eng, signal, n, k):
            if n.out is not None:
                eng.scalar_tensor_tensor(out=n.out[:, k, :], in0=hT[:, k, :], scalar=n.gain(k), in1=n.rs, op0=ALU.mult,
                                         op1=ALU.mult).then_inc(*signal.done(f"y{k}"))
                return
            if k >= 3:
                eng.wait_ge(*n.s.dve.at(f"l{k - 3}"))
            eng.tensor_tensor(n.y[:, k % 3, :], hT[:, k, :], n.rs, ALU.mult).then_inc(*signal.done(f"y{k}"))

        def dve_norm(dve, n):
            s = n.s
            for k in range(KT if n.number is None else 0):
                dve.wait_ge(*s.act.at(f"sq{k}"))
                if k == 0:
                    dve.tensor_copy(n.sum, n.sq[:, 0, :]).then_inc(*s.dve.done("sum0"))
                else:
                    dve.wait_ge(*s.dve.at(f"sum{k - 1}"))
                    dve.tensor_tensor(n.sum, n.sum, n.sq[:, k % 2, :], ALU.add).then_inc(*s.dve.done(f"sum{k}"))
            dve.wait_ge(*s.act.at("rstd"))
            if n.out is not None:
                for k in range(KT):
                    scaled(dve, s.dve, n, k)
                return
            scaled(dve, s.dve, n, 0)
            scaled(dve, s.dve, n, 2)
            for k in range(KT):
                dve.wait_ge(*s.act.at(f"h{k}"))
                dve.scalar_tensor_tensor(out=xl[:, k, :], in0=n.y[:, k % 3, :], scalar=n.gain(k),
                                         in1=xh[:, k, :].bitcast(F32), op0=ALU.mult, op1=ALU.subtract).then_inc(
                    *s.dve.done(f"l{k}"))
                if k in (1, 3):
                    scaled(dve, s.dve, n, k + 3)
            dve.wait_ge(*s.dve.at(f"l{KT - 1}"))

        def pool_norm(pool, n):
            if n.out is None:
                pool.wait_ge(*n.s.act.at("rstd"))
                for k in range(1, KT, 2):
                    scaled(pool, n.s.pool, n, k)

        def pe_norm(pe, n):
            s = n.s
            if n.number is None:
                pe.wait_ge(*s.dve.at(f"sum{KT - 1}"))
            else:
                pe.wait_ge(sum_ok, n.sums + 9)
            for h in range(2):
                mm = pe.matmul(ps[:, 4 + h, 0:TH], ones[:, :], n.sum[:, h * TH:(h + 1) * TH], start=True, stop=True)
            mm.then_inc(*s.pe.done("mean"))

        def tile_ready(n):
            def ready(pe, k):
                pe.wait_ge(*n.s.dve.at(f"l{k}"))
            return ready

        def norm_part(n):
            return dict(tensor=lambda e: pe_norm(e, n), scalar=lambda e: act_norm(e, n),
                        vector=lambda e: dve_norm(e, n), gpsimd=lambda e: pool_norm(e, n))

        norm0 = Norm("mix0", lambda k: col("norm_mix", k), "v_a")

        E1 = Section("even_in")
        E2 = Section("even_decay")
        E3 = Section("even_scores")
        E4 = Section("even_chunks")
        E5 = Section("even_gate")
        K40 = float(2.0 ** 40)

        def pe_even_in(pe):
            pe_stage(pe, "v_a", tile_ready(norm0))
            for name in ("i_b", "gk"):
                pe_stage(pe, name)
            for s in range(2):
                pe.wait_ge(bank_free[s], used["gk"][s])
            for j, (tt, half) in enumerate((t, k) for t in range(5) for k in range(2)):
                n = P if tt < 4 else TS
                if j >= 4:
                    pe.wait_ge(*E1.dve.at(f"vt{j - 4}"))
                for k in range(4):
                    mm = pe.transpose(ps[0:n, 4 + j % 4, k * P:(k + 1) * P], vT[:, 4 * half + k, tt * P:tt * P + n],
                                      ident[:, :])
                mm.then_inc(*E1.pe.done(f"vt{j}"))
            pe.wait_ge(bank_free[0], used["f_b"][0])
            pe.wait_ge(*E1.dma.at("wgk2"))
            pe.wait_ge(*E1.dve.at("vt9"))
            for k in range(2):
                for h in range(2):
                    mm = pe.matmul(ps[:, 4 + 2 * k + h, 0:TH], wgk2[0:16, k * P:(k + 1) * P],
                                   lrT[0:16, h * TH:(h + 1) * TH], start=True, stop=True)
            mm.then_inc(*E1.pe.done("gk2"))
            for name in ("f_b", "k_a", "q_a", "q_b", "g_a", "g_b"):
                pe_stage(pe, name)

        def act_even_in(act):
            act.dma_start(wgk2[0:16, :], a["w_gk2"][0]).then_inc(*E1.dma.loaded("wgk2"))
            decay = act_decay(act)

            for name, fn in (("v_a", None), ("i_b", None), ("gk", "gk"), ("f_b", None), ("k_a", None), ("q_a", None),
                             ("q_b", "q"), ("g_a", "g"), ("g_b", "g")):
                n, units = stages[name]
                for i in range(n):
                    for s in range(len(units)):
                        use = used[name][s] + i
                        act.wait_ge(mm_ok[s], use + 1)
                        ahead(act_head, act, name, s, i, i == n - 1)
                        if fn == "gk":
                            act.activation(two(lrT)[0:16], out2(s)[0:16], ACT.Copy).then_inc(bank_free[s], 1)
                        if fn == "q":
                            act.activation(two(qq[:, 2 + 2 * i + s, :]), out2(s), ACT.Silu).then_inc(bank_free[s], 1)
                        if fn == "g":
                            t = 2 * i + s + (4 if name == "g_b" else 0)
                            act.activation(two(gate[:, t, :]), out2(s), ACT.Silu).then_inc(bank_free[s], 1)
                        if fn == "g" or (name, i, s) == ("q_b", 1, 1):
                            next(decay, None)

        def dve_even_in(dve):
            decay = dve_decay(dve)
            for name, fn in (("v_a", 0), ("i_b", 4), ("gk", None), ("f_b", "f"), ("k_a", "k"), ("q_a", "qa"),
                             ("q_b", None), ("g_a", None), ("g_b", None)):
                n, units = stages[name]
                for i in range(n):
                    for s in range(len(units)):
                        use = used[name][s] + i
                        if fn is not None:
                            dve.wait_ge(mm_ok[s], use + 1)
                        if fn in (0, 4):
                            t = fn + 2 * i + s
                            dve.tensor_copy(two(vT[:, t, :]), out2(s)).then_inc(bank_free[s], 1)
                        if fn == "f":
                            dve.tensor_copy(two(lg[:, 2 + 2 * i + s, :]), out2(s)).then_inc(bank_free[s], 1)
                        if fn == "k":
                            dve.tensor_copy(two(kk[:, s, :]), out2(s)).then_inc(bank_free[s], 1)
                        if fn == "qa":
                            dve.tensor_scalar(two(qq[:, s, :]), out2(s), DKA ** -0.5, None, ALU.mult).then_inc(
                                bank_free[s], 1)
                        ahead(dve_rest, dve, name, s, i, i == n - 1)
                        if name in ("g_a", "g_b") or (name, i, s) == ("q_b", 1, 1):
                            next(decay, None)
                if name == "gk":
                    for j, (tt, half) in enumerate((t, k) for t in range(5) for k in range(2)):
                        nt = P if tt < 4 else TS
                        dve.wait_ge(*E1.pe.at(f"vt{j}"))
                        dve.tensor_copy(vtok[0:nt, tt, half * 512:half * 512 + 512], ps[0:nt, 4 + j % 4, :]).then_inc(
                            *E1.dve.done(f"vt{j}"))
                    dve.wait_ge(*E1.pe.at("gk2"))
                    for k in range(2):
                        dve.tensor_scalar(two(lg[:, k, :]), ps[:, 4 + 2 * k:6 + 2 * k, 0:TH], col("b_gk", k), None,
                                          ALU.add).then_inc(*E1.dve.done(f"z{k}"))

        gam = vec[:, 0, VCOL["hgrn_gamma"][1]:VCOL["hgrn_gamma"][1] + 4]
        lb_e, lb_r, lb_sm, lb, lb_c, lb_1m, lb_om, lb_t = (lbs[:, 4 * i:4 * i + 4] for i in range(8))
        zz = lg[:, :, :]
        hz = lg[:, 2:6, :]

        def dve_decay(dve):
            def step(ins, name):
                ins.then_inc(*E2.dve.done(name))
                dve.wait_ge(*E2.dve.at(name))

            step(dve.tensor_tensor(lb_t, gam, gam, ALU.subtract), "g0")
            dve.wait_ge(*E2.act.at("ge"))
            step(dve.reciprocal(lb_r, lb_e), "gr")
            step(dve.tensor_tensor(lb_sm, lb_e, lb_r, ALU.mult), "gsm")
            step(dve.tensor_tensor(lb, lb_sm, lb_sm, ALU.subtract), "lb")
            step(dve.tensor_scalar(lb_t, lb, 1e-20, K40, ALU.max, ALU.mult), "lbt")
            step(dve.tensor_scalar(lb_om, lb, -1.0, 1.0, ALU.mult, ALU.add), "lbo")
            dve.wait_ge(bank_free[0], used["k_a"][0])
            dve.wait_ge(bank_free[1], used["k_a"][1])
            dve.wait_ge(*E1.dve.at("z1"))
            dve.wait_ge(*E1.pe.at("gk2"))
            step(dve.scalar_tensor_tensor(out=soft, in0=zz, scalar=-1.0, in1=zz, op0=ALU.mult, op1=ALU.max), "abs")
            yield
            dve.wait_ge(*E2.act.at("ln"))
            step(dve.scalar_tensor_tensor(out=soft, in0=zz, scalar=0.0, in1=soft, op0=ALU.min, op1=ALU.subtract), "lsig")
            step(dve.tensor_tensor(kk[:, 2:6, :], soft[:, 2:6, :], hz, ALU.subtract), "kz")
            step(dve.tensor_scalar(lg[:, 0:2, :], soft[:, 0:2, :], 1.0 / 16.0, None, ALU.mult), "gla")
            yield
            dve.wait_ge(*E2.act.at("l1m"))
            for t in range(4):
                dve.tensor_scalar(lg[:, 2 + t, :], soft[:, 2 + t, :], lb_1m[:, t:t + 1], None, ALU.add).then_inc(
                    *E2.dve.done(f"l1{t}"))
            dve.wait_ge(*E2.dve.at("l13"))
            step(dve.tensor_scalar(lb_c, lb_c, -40.0 * float(np.log(2.0)), None, ALU.add), "c")
            for t in range(4):
                dve.tensor_scalar(soft[:, 2 + t, :], lg[:, 2 + t, :], lb_c[:, t:t + 1], None, ALU.subtract).then_inc(
                    *E2.dve.done(f"d{t}"))
            dve.wait_ge(*E2.dve.at("d3"))
            step(dve.scalar_tensor_tensor(out=soft[:, 2:6, :], in0=soft[:, 2:6, :], scalar=-1.0,
                                          in1=soft[:, 2:6, :], op0=ALU.mult, op1=ALU.max), "abs2")
            yield
            dve.wait_ge(*E2.act.at("ln2"))
            for t in range(4):
                dve.scalar_tensor_tensor(out=lg[:, 2 + t, :], in0=lg[:, 2 + t, :], scalar=lb_c[:, t:t + 1],
                                         in1=soft[:, 2 + t, :], op0=ALU.max, op1=ALU.add).then_inc(
                    *E2.dve.done(f"lf{t}"))
            dve.wait_ge(*E2.act.at("kb"))
            for t in range(4):
                dve.tensor_scalar(kk[:, 2 + t, :], kk[:, 2 + t, :], lb_om[:, t:t + 1], None, ALU.mult).then_inc(
                    *E2.dve.done(f"kb{t}"))
            yield
            dve.wait_ge(bank_free[0], used["g_a"][0])
            dve.wait_ge(bank_free[1], used["g_a"][1])
            dve.tensor_scalar(qq[:, 2:6, :], qq[:, 2:6, :], NBK ** -0.5, None, ALU.mult).then_inc(*E2.dve.done("qb"))
            dve.wait_ge(*E2.dve.at("lf3"))
            for kt in range(KTILES):
                dve.tensor_tensor_scan(lg[:, kt, :], resetE, lg[:, kt, :], 0.0, ALU.mult, ALU.add).then_inc(
                    *E2.dve.done(f"b{kt}"))
                if kt % 2:
                    yield

        def act_decay(act):
            act.wait_ge(*E2.dve.at("g0"))
            act.activation(lb_e, lb_t, ACT.Exp).then_inc(*E2.act.done("ge"))
            act.wait_ge(*E2.dve.at("lbo"))
            act.activation(lb_c, lb_t, ACT.Ln)
            act.activation(lb_1m, lb_om, ACT.Ln).then_inc(*E2.act.done("l1m"))
            act.wait_ge(*E2.dve.at("abs"))
            act.activation(soft, soft, ACT.Exp, scale=-1.0).then_inc(*E2.act.done("e"))
            act.wait_ge(*E2.act.at("e"))
            act.activation(soft, soft, ACT.Ln, bias=1.0).then_inc(*E2.act.done("ln"))
            yield
            act.wait_ge(*E2.dve.at("kz"))
            act.activation(kk[:, 2:6, :], kk[:, 2:6, :], ACT.Exp).then_inc(*E2.act.done("kb"))
            yield
            act.wait_ge(*E2.dve.at("abs2"))
            act.activation(soft[:, 2:6, :], soft[:, 2:6, :], ACT.Exp, scale=-1.0).then_inc(*E2.act.done("e2"))
            act.wait_ge(*E2.act.at("e2"))
            act.activation(soft[:, 2:6, :], soft[:, 2:6, :], ACT.Ln, bias=1.0).then_inc(*E2.act.done("ln2"))
            yield

        def span(level):
            return T if level <= 2 else TP

        def halves_of(ap, level):
            m = 1 << (level - 1)
            return ap[:, 0:span(level)].rearrange("p (n h m) -> p n h m", h=2, m=m)

        steps = [(kt, level) for kt in range(KTILES) for level in range(1, LEVELS + 1)]

        def pool_scores(pool):
            pool.wait_ge(*E2.dve.at(f"b{KTILES - 1}"))
            for n, (kt, level) in enumerate(steps):
                m = 1 << (level - 1)
                b, e = halves_of(lg[:, kt, :], level), halves_of(ee[:, n % 2, :], level)
                mid = b[:, :, 0, m - 1:m].to_broadcast([P, span(level) // (2 * m), m])
                if n >= 2:
                    pool.wait_ge(*E3.dve.at(f"qk{n - 2}"))
                pool.tensor_tensor(e[:, :, 0, :], mid, b[:, :, 0, :], ALU.subtract)
                pool.tensor_tensor(e[:, :, 1, :], b[:, :, 1, :], mid, ALU.subtract).then_inc(*E3.pool.done(f"e{n}"))
            for kt in range(KTILES):
                b, e = lg[:, kt, :], ee[:, kt % 2, :]
                if kt >= 2:
                    pool.wait_ge(*E3.dve.at(f"kh{kt - 2}"))
                else:
                    pool.wait_ge(*E3.dve.at(f"qk{len(steps) - 2 + kt}"))
                for lo, n, c in ((0, NCE, CE), (TP, NB, ST)):
                    bb = b[:, lo:lo + n * c].rearrange("p (n c) -> p n c", c=c)
                    ins = pool.tensor_tensor(e[:, lo:lo + n * c].rearrange("p (n c) -> p n c", c=c),
                                             bb[:, :, c - 1:c].to_broadcast([P, n, c]), bb, ALU.subtract)
                ins.then_inc(*E3.pool.done(f"eh{kt}"))

        def dve_scores(dve):
            dve.wait_ge(mm_ok[0], used["w_out"][0])
            dve.wait_ge(mm_ok[1], used["w_out"][1])
            dve.wait_ge(*E2.dve.at(f"b{KTILES - 1}"))

            def factors(n):
                kt, level = steps[n]
                e, z = halves_of(ee[:, n % 2, :], level), halves_of(qk[:, level - 1, :], level)
                dve.wait_ge(*E3.act.at(f"e{n}"))
                if kt > 0:
                    dve.wait_ge(*E3.pe.at(f"g{heads_of[kt - 1][-1]}"))
                dve.tensor_tensor(z[:, :, 0, :], e[:, :, 0, :], halves_of(kk[:, kt, :], level)[:, :, 0, :], ALU.mult)
                dve.tensor_tensor(z[:, :, 1, :], e[:, :, 1, :], halves_of(qq[:, kt, :], level)[:, :, 1, :],
                                  ALU.mult).then_inc(*E3.dve.done(f"qk{n}"))

            def masked(j):
                h = jobs[j][1]
                b0 = 4 * (j % 2)
                dve.wait_ge(*E3.pe.at(f"g{h}"))
                if j > 0:
                    dve.wait_ge(*E3.dve.at(f"ps{jobs[j - 1][1]}"))
                for q in range(4):
                    nl = 2 if q < 3 else 1
                    at = 0 if q % 2 else 512
                    out = mt[:, 1, at:at + nl * 256] if q else mt[:, 0, 0:512]
                    m = lvmask[:, 2 * q:2 * q + nl, :].unsqueeze(2).to_broadcast([P, nl, 4, CE])
                    if q == 3:
                        dve.wait_ge(*E3.dve.at(f"a{h}_1"))
                    dve.tensor_tensor(out.rearrange("p (l c t) -> p l c t", l=nl, c=4),
                                      ps[:, b0 + q, 0:nl * 256].rearrange("p (l c t) -> p l c t", l=nl, c=4), m,
                                      ALU.mult).then_inc(*E3.dve.done(f"m{h}_{q}"))
                    if q > 0:
                        dve.wait_ge(*E3.dve.at(f"m{h}_{q}"))
                        if q > 1:
                            dve.wait_ge(*E3.dve.at(f"a{h}_{q - 1}"))
                        dve.tensor_tensor(mt[:, 0, 0:nl * 256], mt[:, 0, 0:nl * 256], out, ALU.add).then_inc(
                            *E3.dve.done(f"a{h}_{q}"))
                dve.wait_ge(*E3.dve.at(f"a{h}_3"))
                dve.tensor_tensor(pT[:, h, 0:4, :], mt[:, 0, 0:256].rearrange("p (c t) -> p c t", c=4),
                                  mt[:, 0, 256:512].rearrange("p (c t) -> p c t", c=4), ALU.add).then_inc(
                    *E3.dve.done(f"p{h}"))
                dve.tensor_tensor(mt[0:TS, 1, 0:96].rearrange("p (l t) -> p l t", l=3),
                                  ps[0:TS, b0 + 3, 256:352].rearrange("p (l t) -> p l t", l=3),
                                  lvmask[0:TS, 0:3, 0:TS], ALU.mult).then_inc(*E3.dve.done(f"s{h}"))
                dve.wait_ge(*E3.dve.at(f"s{h}"))
                dve.tensor_tensor(mt[0:TS, 1, 0:32], mt[0:TS, 1, 0:32], mt[0:TS, 1, 32:64], ALU.add).then_inc(
                    *E3.dve.done(f"s2{h}"))
                dve.wait_ge(*E3.dve.at(f"s2{h}"))
                dve.tensor_tensor(pT[0:TS, h, 4, 0:TS], mt[0:TS, 1, 0:32], mt[0:TS, 1, 64:96], ALU.add).then_inc(
                    *E3.dve.done(f"ps{h}"))

            done = 0
            for n in range(len(steps)):
                if n >= 1:
                    factors(n - 1)
                kt, level = steps[n]
                if kt > 0 and level == 3:
                    for h in heads_of[kt - 1]:
                        masked(done)
                        done += 1
            factors(len(steps) - 1)
            for h in heads_of[KTILES - 1]:
                masked(done)
                done += 1
            for kt in range(KTILES):
                b, e = lg[:, kt, :], ee[:, kt % 2, :]
                dve.wait_ge(*E3.act.at(f"eq{kt}"))
                dve.tensor_tensor(kk[:, kt, :], kk[:, kt, :], e, ALU.mult).then_inc(*E3.dve.done(f"kh{kt}"))
                dve.tensor_tensor(qq[:, kt, :], qq[:, kt, :], b, ALU.mult)
                dve.tensor_copy(ebl[:, kt, 0:NCE], b[:, 0:TP].rearrange("p (n c) -> p n c", c=CE)[:, :, CE - 1])
                dve.tensor_copy(ebl[:, kt, NCE:NCE + NB], b[:, TP:T].rearrange("p (n c) -> p n c", c=ST)[:, :, ST - 1]
                                ).then_inc(*E3.dve.done(f"qh{kt}"))

        def act_scores(act):
            for n in range(len(steps)):
                act.wait_ge(*E3.pool.at(f"e{n}"))
                w = span(steps[n][1])
                act.activation(ee[:, n % 2, 0:w], ee[:, n % 2, 0:w], ACT.Exp).then_inc(*E3.act.done(f"e{n}"))
            for kt in range(KTILES):
                act.wait_ge(*E3.pool.at(f"eh{kt}"))
                act.activation(ee[:, kt % 2, :], ee[:, kt % 2, :], ACT.Exp)
                act.activation(lg[:, kt, :], lg[:, kt, :], ACT.Exp).then_inc(*E3.act.done(f"eq{kt}"))

        def pe_scores(pe):
            for s in range(2):
                pe.wait_ge(bank_free[s], used["w_out"][s])
            pe.wait_ge(*E2.dve.at("qb"))
            pe.wait_ge(*E2.dve.at("kb3"))
            for j, (kt, h) in enumerate(jobs):
                _, r0, dk = rows(h)
                b0 = 4 * (j % 2)
                if j >= 2:
                    pe.wait_ge(*E3.dve.at(f"ps{jobs[j - 2][1]}"))
                for level in range(LEVELS + 1):
                    left = kk[r0:r0 + dk, kt, :] if level == 0 else qk[r0:r0 + dk, level - 1, :]
                    right = qq[r0:r0 + dk, kt, :] if level == 0 else left
                    if level:
                        pe.wait_ge(*E3.dve.at(f"qk{steps.index((kt, level))}"))
                    for c in range(NCE):
                        at = (level % 2) * 256 + (c // 2) * CE
                        mm = pe.matmul(ps[64 * (c % 2):64 * (c % 2) + CE, b0 + level // 2, at:at + CE],
                                       left[:, c * CE:(c + 1) * CE], right[:, c * CE:(c + 1) * CE],
                                       start=True, stop=True)
                    if level <= 2:
                        at = 256 + 32 * level
                        pe.matmul(ps[0:TS, b0 + 3, at:at + TS], left[:, TP:T], right[:, TP:T], start=True, stop=True)
                mm.then_inc(*E3.pe.done(f"g{h}"))

        gla_out, hgrn_out, out_sem = sem("gla_sample_out"), sem("hgrn_sample_out"), sem("outputs_out")
        prompt_out = sem("even_prompt_states_out")
        loads4 = [Signal(sem(f"even_states{i}"), f"even_states{i}", seen, known) for i in range(KTILES)]

        def pe_chunks(pe):
            for j in range(KTILES):
                b0 = 2 * (j % 4)
                pe.wait_ge(*E3.dve.at(f"kh{j}"))
                if j < 4:
                    pe.wait_ge(*E3.dve.at(f"ps{HA + HB - 1}"))
                else:
                    pe.wait_ge(*E4.act.at(f"kt{j - 4}"))
                for c in range(4):
                    pe.transpose(ps[:, b0, c * P:(c + 1) * P], kk[:, j, c * P:(c + 1) * P], ident[:, :])
                pe.transpose(ps[0:TS, b0 + 1, 0:P], kk[:, j, TP:T], ident[:, :]).then_inc(*E4.pe.done(f"kt{j}"))
            pe.wait_ge(*E4.act.at(f"kt{KTILES - 1}"))
            pe.wait_ge(*E3.dve.at(f"qh{KTILES - 1}"))
            for c in range(NCE):
                b0 = 4 * (c % 2)
                r, tt = 64 * (c % 2), c // 2
                if c >= 2:
                    pe.wait_ge(*E4.act.at(f"o{c - 2}"))
                    pe.wait_ge(*E4.dve.at(f"s{c - 2}_{KTILES - 1}"))
                for h in range(8):
                    kt, r0, dk = rows(h)
                    mm = pe.matmul(ps[r0:r0 + dk, b0 + 1 + kt // 4, (kt % 4) * DV:(kt % 4 + 1) * DV],
                              ktok[r:r + CE, tt, kt * P + r0:kt * P + r0 + dk],
                              vtok[r:r + CE, tt, h * DV:(h + 1) * DV], start=True, stop=True)
                mm.then_inc(*E4.pe.done(f"s{c}"))
                for h in range(8):
                    mm = pe.matmul(ps[:, b0, h * CE:(h + 1) * CE], vtok[r:r + CE, tt, h * DV:(h + 1) * DV],
                                   pT[r:r + CE, h, tt, :], start=h == 0, stop=c == 0, skip_group_check=True)
                if c > 0:
                    even, odd = [0, 2], [1, 3]
                    for i, h in enumerate((even if r == 0 else odd) + [4, 5, 6, 7] + (odd if r == 0 else even)):
                        kt, r0, dk = rows(h)
                        pe.wait_ge(*E4.dve.at(f"s{c - 1}_{kt}"))
                        if i == 6:
                            pe.wait_ge(*E4.pe.at(f"rows{c}"))
                        mm = pe.matmul(ps[:, b0, h * CE:(h + 1) * CE], state[c % 2][r0:r0 + dk, kt, :],
                                       qq[r0:r0 + dk, kt, c * CE:(c + 1) * CE], start=False, stop=True,
                                       skip_group_check=True)
                        if i == 5:
                            mm.then_inc(*E4.pe.done(f"rows{c}"))
                mm.then_inc(*E4.pe.done(f"o{c}"))
            pe.wait_ge(*E4.act.at(f"o{NCE - 1}"))
            pe.wait_ge(*E4.dve.at(f"s{NCE - 1}_{KTILES - 1}"))
            for kt in range(KTILES):
                b0 = 4 * (kt % 2)
                pe.wait_ge(*loads4[kt].at(f"ss{kt}"))
                if kt >= 2:
                    pe.wait_ge(*E4.dve.at(f"ss{kt - 2}"))
                for h in heads_of[kt]:
                    _, r0, dk = rows(h)
                    pe.wait_ge(*E4.pool.at(f"vx{h}"))
                    for g in range(2):
                        mm = pe.matmul(ps[r0:r0 + dk, b0 + g, :], ktok[0:TS, 4, kt * P + r0:kt * P + r0 + dk],
                                       vx[0:TS, h % 2, 4 * g:4 * g + 4, :].rearrange("p b v -> p (b v)"), start=True,
                                       stop=True)
                    mm.then_inc(*E4.pe.done(f"vx{h}"))
                for h in heads_of[kt]:
                    _, r0, dk = rows(h)
                    if h > 0:
                        pe.wait_ge(*E4.pe.at(f"so{h - 1}"))
                    pe.matmul(ps[:, 3, h * TS:(h + 1) * TS], vtok[0:TS, 4, h * DV:(h + 1) * DV], pT[0:TS, h, 4, 0:TS],
                              start=True, stop=False, skip_group_check=True)
                    for b in range(NB):
                        mm = pe.matmul(ps[:, 3, h * TS + b * ST:h * TS + (b + 1) * ST], sst[kt][r0:r0 + dk, b, :],
                                       qq[r0:r0 + dk, kt, TP + b * ST:TP + (b + 1) * ST], start=False, stop=True,
                                       skip_group_check=True)
                    mm.then_inc(*E4.pe.done(f"so{h}"))

        def act_chunks(act):
            for j in range(KTILES):
                b0 = 2 * (j % 4)
                act.wait_ge(*E4.pe.at(f"kt{j}"))
                if j == 0:
                    act.wait_ge(*E2.dve.at("lf3"))
                act.activation(ktok[:, 0:4, j * P:(j + 1) * P], ps[:, b0, :].rearrange("p (c k) -> p c k", c=4),
                               ACT.Copy)
                act.activation(ktok[0:TS, 4, j * P:(j + 1) * P], ps[0:TS, b0 + 1, 0:P], ACT.Copy).then_inc(
                    *E4.act.done(f"kt{j}"))
            for c in range(NCE):
                act.wait_ge(*E4.pe.at(f"o{c}"))
                act.activation(oT[:, :, c * CE:(c + 1) * CE], ps[:, 4 * (c % 2), :].rearrange("p (h t) -> p h t", h=8),
                               ACT.Copy).then_inc(*E4.act.done(f"o{c}"))
            act.wait_ge(*E4.dve.at(f"s{NCE - 1}_{KTILES - 1}"))
            for kt in range(KTILES):
                if kt < 2:
                    dst = o["gla_prompt"][0, 0][2 * kt:2 * kt + 2].rearrange("h k v -> (h k) v")
                else:
                    dst = o["hgrn_prompt"][0, 0][kt - 2]
                act.dma_start(dst, state[0][:, kt, :]).then_inc(prompt_out, 16)
            act.wait_ge(*E4.pe.at("so7"))
            act.activation(oT[:, :, TP:T], ps[:, 3, 0:8 * TS].rearrange("p (h t) -> p h t", h=8), ACT.Copy).then_inc(
                *E4.act.done("os"))

        def dve_chunks(dve):
            for c in range(NCE):
                b0 = 4 * (c % 2)
                for kt in range(KTILES):
                    src = ps[:, b0 + 1 + kt // 4, (kt % 4) * DV:(kt % 4 + 1) * DV]
                    dve.wait_ge(*E4.pe.at(f"s{c}"))
                    if c == 0:
                        dve.tensor_copy(state[1][:, kt, :], src).then_inc(*E4.dve.done(f"s{c}_{kt}"))
                        continue
                    dve.wait_ge(*E4.dve.at(f"s{c - 1}_{kt}"))
                    if c > 1:
                        dve.wait_ge(*E4.pe.at(f"o{c - 1}"))
                    dve.scalar_tensor_tensor(out=state[(c + 1) % 2][:, kt, :], in0=state[c % 2][:, kt, :], scalar=ebl[:, kt, c:c + 1],
                                             in1=src, op0=ALU.mult, op1=ALU.add).then_inc(*E4.dve.done(f"s{c}_{kt}"))
            for kt in range(KTILES):
                b0 = 4 * (kt % 2)
                dve.wait_ge(*E4.pe.at(f"so{heads_of[kt][-1]}"))
                dve.wait_ge(*loads4[kt].at(f"ss{kt}"))
                new = sst[kt]
                dve.tensor_tensor(new, new, ebl[:, kt, NCE:NCE + NB].unsqueeze(2).to_broadcast([P, NB, DV]),
                                  ALU.mult).then_inc(*E4.dve.done(f"sm{kt}"))
                dve.wait_ge(*E4.dve.at(f"sm{kt}"))
                new = new.rearrange("p (g b) v -> p g (b v)", g=2)
                dve.tensor_tensor(new, new, ps[:, b0:b0 + 2, :], ALU.add).then_inc(*E4.dve.done(f"ss{kt}"))

        def pool_chunks(pool):
            pool.wait_ge(mm_ok[0], used["w_out"][0])
            pool.wait_ge(mm_ok[1], used["w_out"][1])

            def sample_state(name, kt):
                if kt < 2:
                    return [(64 * i, 64, a[name[0]][0][:, 2 * kt + i].rearrange("b k v -> k b v")) for i in range(2)]
                return [(0, P, a[name[1]][0][:, kt - 2].rearrange("b k v -> k b v"))]

            def load(kt):
                parts = sample_state(("state_gla", "state_hgrn"), kt)
                for n, (r0, nr, src) in enumerate(parts):
                    d = pool.dma_start(sst[kt][r0:r0 + nr, :, :], src)
                    d.then_inc(*loads4[kt].loaded(f"ss{kt}"))

            load(0)
            load(1)
            pool.wait_ge(*E3.dve.at(f"ps{HA + HB - 1}"))
            pool.wait_ge(*E3.dve.at(f"qh{KTILES - 1}"))
            for kt in range(2, KTILES):
                load(kt)
            vxs = [h for kt in range(KTILES) for h in heads_of[kt]]
            for h in vxs[0:2]:
                masked_values(pool, h)
            for h in vxs[2:]:
                masked_values(pool, h)
            for kt in range(KTILES):
                pool.wait_ge(*E4.dve.at(f"ss{kt}"))
                for r0, nr, dst in sample_state_out(kt):
                    pool.dma_start(dst, sst[kt][r0:r0 + nr, :, :]).then_inc(gla_out if kt < 2 else hgrn_out, 16)

        def masked_values(pool, h):
            if h >= 2:
                pool.wait_ge(*E4.pe.at(f"vx{h - 2}"))
            pool.tensor_tensor(vx[0:TS, h % 2, :, :],
                               vtok[0:TS, 4, h * DV:(h + 1) * DV].unsqueeze(1).to_broadcast([TS, NB, DV]),
                               batE[0:TS, :].unsqueeze(2).to_broadcast([TS, NB, DV]), ALU.mult).then_inc(
                *E4.pool.done(f"vx{h}"))

        def sample_state_out(kt):
            if kt < 2:
                return [(64 * i, 64, o["gla_sample"][0][:, 2 * kt + i].rearrange("b k v -> k b v")) for i in range(2)]
            return [(0, P, o["hgrn_sample"][0][:, kt - 2].rearrange("b k v -> k b v"))]

        def act_gate(act):
            act.wait_ge(*E4.act.at("os"))
            act.activation(sq[:, 0, :], oT[:, 0, :], ACT.Square).then_inc(*E5.act.done("sq0"))
            for h in range(8):
                if h < 7:
                    if h >= 1:
                        act.wait_ge(*E5.pe.at(f"m{h - 1}"))
                    act.activation(sq[:, (h + 1) % 2, :], oT[:, h + 1, :], ACT.Square).then_inc(
                        *E5.act.done(f"sq{h + 1}"))
                act.wait_ge(*E5.pe.at(f"m{h}"))
                if h >= 2:
                    act.wait_ge(*E5.dve.at(f"n{h - 2}"))
                act.activation(two(rstd[:, h % 2, :]), ps[:, 4 + 2 * (h % 2):6 + 2 * (h % 2), 0:TH], ACT.Ln,
                               bias=eps_rms, scale=1.0 / DV).then_inc(*E5.act.done(f"m{h}"))
                act.wait_ge(*E5.act.at(f"m{h}"))
                act.activation(rstd[:, h % 2, :], rstd[:, h % 2, :], ACT.Exp, scale=-0.5).then_inc(*E5.act.done(f"r{h}"))
                if h >= 1:
                    head(act, h - 1)
            head(act, 7)

        def head(act, h):
            act.wait_ge(*E5.dve.at(f"y{h}"))
            act.activation(xh[:, h, :], nrm[:, h % 2, :], ACT.Copy).then_inc(*E5.act.done(f"h{h}"))

        def pe_gate(pe):
            for h in range(8):
                pe.wait_ge(*E5.act.at(f"sq{h}"))
                if h == 0:
                    pe.wait_ge(*E4.dve.at(f"ss{KTILES - 1}"))
                if h >= 2:
                    pe.wait_ge(*E5.act.at(f"m{h - 2}"))
                for g in range(2):
                    mm = pe.matmul(ps[:, 4 + 2 * (h % 2) + g, 0:TH], ones[:, :], sq[:, h % 2, g * TH:(g + 1) * TH],
                                   start=True, stop=True)
                mm.then_inc(*E5.pe.done(f"m{h}"))

        def dve_gate(dve):
            dve.wait_ge(gla_out, 16 * 4)
            dve.wait_ge(prompt_out, 16 * KTILES)
            dve.wait_ge(*E4.act.at("os"))
            for h in range(8):
                gain = col("gla_norm") if h < HA else col("hgrn_norm")
                y = nrm[:, h % 2, :]
                dve.wait_ge(*E5.act.at(f"r{h}"))
                if h >= 2:
                    dve.wait_ge(*E5.dve.at(f"l{h - 2}"))
                dve.scalar_tensor_tensor(out=y, in0=oT[:, h, :], scalar=gain, in1=rstd[:, h % 2, :], op0=ALU.mult,
                                         op1=ALU.mult).then_inc(*E5.dve.done(f"n{h}"))
                dve.wait_ge(*E5.dve.at(f"n{h}"))
                dve.tensor_tensor(y, y, gate[:, h, :], ALU.mult).then_inc(*E5.dve.done(f"y{h}"))
                dve.wait_ge(*E5.act.at(f"h{h}"))
                dve.tensor_tensor(xl[:, h, :], y, xh[:, h, :].bitcast(F32), ALU.subtract).then_inc(
                    *E5.dve.done(f"l{h}"))

        def add_stage(name, ready, norm=None):
            n, units = stages[name]

            def pe_part(pe):
                pe_stage(pe, name, ready)

            def act_part(act):
                def body(i, last):
                    for s in range(2):
                        act.wait_ge(mm_ok[s], used[name][s] + i + 1)
                        ahead(act_head, act, name, s, i, last)
                        if norm is not None:
                            act.wait_ge(bank_free[s], used[name][s] + i + 1)
                            square(act, norm, s, 2 * i + s)
                each(act, n, name, body)

            def dve_part(dve):
                if norm is not None:
                    clear_sum(dve, norm)

                def body(i, last):
                    for s in range(2):
                        dve.wait_ge(mm_ok[s], used[name][s] + i + 1)
                        h = hT[:, ds(2 * i + s, 1), :].rearrange("p one (h t) -> p (one h) t", h=2)
                        dve.tensor_tensor(h, h, out2(s), ALU.add).then_inc(bank_free[s], 1)
                        ahead(dve_rest, dve, name, s, i, last)
                        if norm is not None:
                            add_squares(dve, norm, s, 2 * i + s)
                each(dve, n, name, body)

            return pe_part, act_part, dve_part

        def gate_ready(pe, k):
            pe.wait_ge(*E5.dve.at(f"l{k}"))

        norm_f0 = Norm("ffn0", lambda k: col("norm_ffn", k), "up00", 0)
        out_even = add_stage("w_out", gate_ready, norm_f0)

        def act_hgrn_out(act):
            act.wait_ge(hgrn_out, 16 * 4)

        silu_ok, prod_ok = sem("ffn_silu"), sem("ffn_product")
        hhead_ok, hrest_ok = sem("hidden_head"), sem("hidden_rest")
        sig_ok, gated_ok, added_ok = sem("ple_sigmoid"), sem("ple_gated"), sem("ple_added")
        ptok = cols(MIXF, 5, PLE)
        pf = cols(MIXF + 5 * PLE, PLE // P, T)
        act_out = cols(MIXF + 5 * PLE + 2 * T, T)
        prod = cols(MIXF + 5 * PLE + 3 * T, T)

        norm_o = Norm("mix1", lambda k: col("norm_mix", 8 + k), "rw_r", 2, out=cols(21760, KT, T))
        norm_f1 = Norm("ffn1", lambda k: col("norm_ffn", 8 + k), "up10", 3, at=21760)

        yT = cols(4 * T, KT, T)
        ytok = cols(12 * T, 5, D)
        norm_y = Norm("final", lambda k: col("norm_final", k), "final", 5, out=yT)

        def first_counts(dve):
            for s in (sum_ok, prod_ok, hrest_ok, hhead_ok, gated_ok, added_ok):
                dve.sem_inc(s, 1)

        def tail_of(i):
            S = Section(f"ple_in{i}")
            last = [(bank_free[s], used[f"up{i}0"][s]) for s in range(2)]
            norm_f = norm_f0 if i == 0 else norm_f1
            norm_p = Norm(f"ple{i}", lambda k: col("norm_ple", 8 * i + k), f"ple{i}", 3 * i + 1)
            norm_n = norm_o if i == 0 else norm_y

            def act_in(act):
                for r in last:
                    act.wait_ge(*r)
                act.dma_start(ptok[:, 0:4, :], a["p_prompt"][i, 0].rearrange("(a p) d -> p a d", p=P)).then_inc(
                    *S.dma.loaded("pp"))
                act.dma_start(ptok[0:TS, 4, :], a["p_sample"][i].rearrange("b t d -> (b t) d")).then_inc(
                    *S.dma.loaded("p"))

            def pe_in(pe):
                pe.wait_ge(*S.dma.at("p"))
                for tt in range(5):
                    n = P if tt < 4 else TS
                    bank = 4 + tt if tt < 2 else 6 + tt % 2
                    if tt == 4:
                        pe.wait_ge(*S.dve.at("t2"))
                    for k in range(2):
                        mm = pe.transpose(ps[:, bank, k * n:(k + 1) * n], ptok[0:n, tt, k * P:(k + 1) * P],
                                          ident[0:n, 0:n])
                    mm.then_inc(*S.pe.done(f"t{tt}"))

            def dve_in(dve):
                for tt in range(5):
                    n = P if tt < 4 else TS
                    bank = 4 + tt if tt < 2 else 6 + tt % 2
                    dve.wait_ge(*S.pe.at(f"t{tt}"))
                    dve.tensor_copy(pf[:, :, tt * P:tt * P + n],
                                    ps[:, bank, 0:2 * n].rearrange("p (k t) -> p k t", k=2)).then_inc(
                        *S.dve.done(f"t{tt}"))
                dve.wait_ge(*S.act.at("head"))
                dve.tensor_tensor(ple[:, 1, :, :], pf, ple[:, 0, :, :].bitcast(F32), ALU.subtract).then_inc(
                    *S.dve.done("rest"))

            def act_split(act):
                act.wait_ge(*S.dve.at("t4"))
                act.activation(ple[:, 0, :, :], pf, ACT.Copy).then_inc(*S.act.done("head"))

            def up(half):
                name = f"up{i}{half}"
                base = FT * (2 * i + half) + 1

                def pe_part(pe):
                    pe_stage(pe, name, tile_ready(norm_f) if half == 0 else None)

                def act_part(act):
                    def body(j, last):
                        act.wait_ge(mm_ok[0], used[name][0] + j + 1)
                        ahead(act_head, act, name, 0, j, last)
                        act.wait_ge(prod_ok, base + j)
                        act.activation(two(act_out), out2(0), ACT.Silu).then_inc(bank_free[0], 1)
                        act.wait_ge(bank_free[0], used[name][0] + j + 1)
                        act.sem_inc(silu_ok, 1)
                        act.wait_ge(mm_ok[1], used[name][1] + j + 1)
                        ahead(act_head, act, name, 1, j, last)
                        act.wait_ge(prod_ok, base + j + 1)
                        act.activation(hid[:, 0, ds(j, 1), :], prod.unsqueeze(1), ACT.Copy).then_inc(hhead_ok, 1)
                    each(act, FT, name, body)

                def dve_part(dve):
                    def body(j, last):
                        ahead(dve_rest, dve, name, 0, j, last)
                        dve.wait_ge(bank_free[0], used[name][0] + j + 1)
                        dve.wait_ge(mm_ok[1], used[name][1] + j + 1)
                        dve.wait_ge(hrest_ok, base + j)
                        dve.tensor_tensor(two(prod), two(act_out), out2(1), ALU.mult).then_inc(prod_ok, 1)
                        dve.wait_ge(prod_ok, base + j + 1)
                        dve.sem_inc(bank_free[1], 1)
                        ahead(dve_rest, dve, name, 1, j, last)
                        dve.wait_ge(hhead_ok, base + j + 1)
                        dve.tensor_tensor(hid[:, 1, ds(j, 1), :], prod.unsqueeze(1),
                                          hid[:, 0, ds(j, 1), :].bitcast(F32), ALU.subtract).then_inc(hrest_ok, 1)
                    each(dve, FT, name, body)

                return dict(tensor=pe_part, scalar=act_part, vector=dve_part)

            def down(half):
                def hidden(pe, k):
                    pe.wait_ge(hrest_ok, FT * (2 * i + half) + k + 2)
                pe_part, act_part, dve_part = add_stage(f"down{i}{half}", hidden, norm_p if half else None)
                return dict(tensor=pe_part, scalar=act_part, vector=dve_part)

            name = f"ple{i}"

            def pe_ple(pe):
                pe.wait_ge(*S.dve.at("rest"))
                pe_stage(pe, name, tile_ready(norm_p))

            def act_ple(act):
                def body(j, last):
                    act.wait_ge(mm_ok[0], used[name][0] + j + 1)
                    ahead(act_head, act, name, 0, j, last)
                    act.wait_ge(gated_ok, 8 * i + 1 + j)
                    act.activation(two(act_out), out2(0), ACT.Sigmoid).then_inc(bank_free[0], 1)
                    act.wait_ge(mm_ok[1], used[name][1] + j + 1)
                    ahead(act_head, act, name, 1, j, last)
                    act.wait_ge(added_ok, 8 * i + j + 2)
                    if last:
                        square(act, norm_n, 1, j)
                    else:
                        square(act, norm_n, 0, j)
                each(act, 8, name, body)

            def dve_ple(dve):
                clear_sum(dve, norm_n)

                def body(j, last):
                    ahead(dve_rest, dve, name, 0, j, last)
                    dve.wait_ge(bank_free[0], used[name][0] + j + 1)
                    dve.wait_ge(mm_ok[1], used[name][1] + j + 1)
                    dve.wait_ge(added_ok, 8 * i + 1 + j)
                    dve.tensor_tensor(two(prod), two(act_out), out2(1), ALU.mult).then_inc(gated_ok, 1)
                    dve.wait_ge(gated_ok, 8 * i + j + 2)
                    dve.sem_inc(bank_free[1], 1)
                    h = hT[:, ds(j, 1), :]
                    dve.tensor_tensor(h, h, prod.unsqueeze(1), ALU.add).then_inc(added_ok, 1)
                    ahead(dve_rest, dve, name, 1, j, last)
                    add_squares(dve, norm_n, 1 if last else 0, j)
                each(dve, 8, name, body)

            return [norm_part(norm_f), dict(scalar=act_in), up(0), down(0),
                    dict(tensor=pe_in, scalar=act_split, vector=dve_in), up(1), down(1),
                    norm_part(norm_p), dict(tensor=pe_ple, scalar=act_ple, vector=dve_ple)]

        F = Section("final")
        def act_final(act):
            for j, (tt, half) in enumerate((t, k) for t in range(5) for k in range(2)):
                n = P if tt < 4 else TS
                act.wait_ge(*F.pe.at(f"t{j}"))
                act.activation(ytok[0:n, tt, half * 512:half * 512 + 512], ps[0:n, 4 + j % 4, :], ACT.Copy).then_inc(
                    *F.act.done(f"t{j}"))

        def pe_final(pe):
            pe.wait_ge(*norm_y.s.act.at("ln"))
            for j, (tt, half) in enumerate((t, k) for t in range(5) for k in range(2)):
                n = P if tt < 4 else TS
                if j >= 4:
                    pe.wait_ge(*F.act.at(f"t{j - 4}"))
                if j < 2:
                    pe.wait_ge(*norm_y.s.dve.at(f"y{4 * half + 3}"))
                for k in range(4):
                    mm = pe.transpose(ps[0:n, 4 + j % 4, k * P:(k + 1) * P], yT[:, 4 * half + k, tt * P:tt * P + n],
                                      ident[:, :])
                mm.then_inc(*F.pe.done(f"t{j}"))

        def pool_final(pool):
            for tt in range(4):
                pool.wait_ge(*F.act.at(f"t{2 * tt + 1}"))
                pool.dma_start(o["y_prompt"][0, tt * P:(tt + 1) * P, :], ytok[:, tt, :]).then_inc(out_sem, 16)
            pool.wait_ge(*F.act.at("t9"))
            pool.dma_start(o["y_sample"].rearrange("b t d -> (b t) d"), ytok[0:TS, 4, :]).then_inc(out_sem, 16)
            pool.wait_ge(out_sem, 16 * OUTS)
            pool.wait_ge(prompt_out, 16 * KTILES)
            pool.wait_ge(gla_out, 16 * 4)
            pool.wait_ge(hgrn_out, 16 * 4)

        O0 = Section("odd_mix")
        O1 = Section("odd_proj")
        O2 = Section("odd_quads")
        O3 = Section("odd_gate")
        kb = mix[:, 0:8704].rearrange("p (i n s t) -> p i n s t", i=KT, n=NCO, s=2)
        qr = mix[:, 8704:17408].rearrange("p (i n s t) -> p i n s t", i=KT, n=NCO, s=2)
        vF = cols(17408, KT, T)
        dx = vF
        xn = cols(21760, KT, T)
        hs = mix[:, 0:8704].rearrange("p (i n v) -> p i n v", i=KT, n=NCO)[:, :, 0:NB, :]
        SC0 = 26112
        ymix = cols(SC0, 2, T)
        t1, t2, e1, e2 = (cols(SC0 + (2 + i) * T, T) for i in range(4))
        gs = cols(SC0 + 6 * T, T)
        omka = mix[:, SC0 + 7 * T:SC0 + 7 * T + KT]
        shT = mix[:, SC0 + 7 * T + 8:SC0 + 7 * T + 88]
        hst = mix[:, SC0:SC0 + 512].rearrange("p (i v) -> p i v", i=KT)
        rb_ = mix[:, SC0 + 512:SC0 + 1536].rearrange("p (g i v) -> p g i v", g=2, i=KT)
        lio = mix[:, SC0 + 1536:SC0 + 1536 + 1024]
        rts = mix[:, SC0 + 2560:SC0 + 3072].rearrange("p (i s t) -> p i s t", i=KT, s=2)
        wc = raw[:, :, D + TH:D + TH + 96].rearrange("p s (i n) -> p s i n", i=4)
        small = nc.alloc_sbuf_tensor_at("odd_small", [P, 8704], F32, offset=xs_byte)
        w1 = small[:, 0:512].rearrange("p (k n) -> p k n", k=KT)
        a1 = small[:, 512:1024].rearrange("p (k n) -> p k n", k=KT)
        w2, a2 = small[0:64, 1024:2048], small[0:64, 2048:3072]
        lw_, la_ = small[0:64, 3072:3072 + T], small[0:64, 3072 + T:3072 + 2 * T]
        quad = nc.alloc_sbuf_tensor_at("odd_quad", [P, 8704], F32, offset=xs_byte)
        vu = quad[:, 0:2048].rearrange("p (c g i v) -> p c g i v", c=2, g=2, i=KT)
        sc = quad[:, 4096:6144].rearrange("p (c g i t) -> p c g i t", c=2, g=2, i=KT)
        aT, xT, xx, bT, pp = (quad[:, 6144 + 512 * i:6144 + 512 * (i + 1)] for i in range(5))
        resetO = tab[:, 0:T]
        s16 = tab[0:HC, 0:T]
        same = tab[:, 544:672]
        lvO = tab[:, 672:832].rearrange("p (l t) -> p l t", l=5)
        scm = tab[:, 832:960].rearrange("p (m t) -> p m t", m=2)
        hsel = tab[:, 960:1088].rearrange("p (k h) -> p k h", k=KT)
        batO = tab[:, 1088:1096]
        chunked = lambda ap: ap.rearrange("p (n t) -> p n t", t=CO)


        def act_mix(act):
            act.wait_ge(added_ok, 9)
            for i in range(2):
                act.wait_ge(mm_ok[i], used["rw_r"][i])
            act.dma_start(tab[:, 0:1096], a["odd_tables"]).then_inc(*O0.dma.loaded("tab"))
            act.dma_start(w1, a["rw_w1"][0].rearrange("(k p) n -> p k n", p=P)).then_inc(*O0.dma.loaded("w1"))
            act.dma_start(a1, a["rw_a1"][0].rearrange("(k p) n -> p k n", p=P)).then_inc(*O0.dma.loaded("a1"))
            act.dma_start(w2, a["rw_w2"][0]).then_inc(*O0.dma.loaded("w2"))
            act.dma_start(a2, a["rw_a2"][0]).then_inc(*O0.dma.loaded("all"))

        def act_mix2(act):
            act.wait_ge(*O0.pe.at(f"mix{KT - 1}"))
            act.activation(lw_.rearrange("p (h t) -> p h t", h=2), ps[0:64, 4:6, 0:TH], ACT.Tanh).then_inc(
                *O0.act.done("lw"))
            act.wait_ge(*O0.pe.at(f"mix{2 * KT - 1}"))
            act.activation(la_.rearrange("p (h t) -> p h t", h=2), ps[0:64, 6:8, 0:TH], ACT.Copy).then_inc(
                *O0.act.done("la"))
            for i in range(KT):
                act.wait_ge(*O0.pe.at(f"w2{i}"))
                b0 = 2 * (i % 2)
                if i >= 2:
                    act.wait_ge(*O0.dve.at(f"a{i - 2}"))
                act.activation(two((t1, t2)[i % 2]), ps[:, b0:b0 + 2, 0:TH], ACT.Sigmoid, bias=col("rw_w0", i)).then_inc(
                    *O0.act.done(f"w{i}"))
                act.wait_ge(*O0.pe.at(f"a2{i}"))
                act.activation(two((e1, e2)[i % 2]), ps[:, 4 + b0:6 + b0, 0:TH], ACT.Sigmoid, bias=col("rw_a0", i)).then_inc(
                    *O0.act.done(f"a{i}"))

        def dve_mix(dve):
            dve.wait_ge(*norm_o.s.dve.at(f"y{KT - 1}"))
            pr = TP - 1
            dve.tensor_tensor(dx[:, :, 1:TP], xn[:, :, 0:pr], xn[:, :, 1:TP], ALU.subtract)
            dve.tensor_scalar(dx[:, :, 0:1], xn[:, :, 0:1], -1.0, None, ALU.mult)
            ends = xn[:, :, TP - 1:TP]
            dve.tensor_copy(shT[:, 0:KT].unsqueeze(2), ends)
            last = vec[:, 1, VCOL["state_shift"][1]:VCOL["state_shift"][1] + 64].rearrange("p (b k) -> p k b", k=KT)
            for k in range(KT):
                x4 = xn[:, k, TP:T].rearrange("p (b t) -> p b t", t=ST)
                d4 = dx[:, k, TP:T].rearrange("p (b t) -> p b t", t=ST)
                dve.tensor_tensor(d4[:, :, 1:ST], x4[:, :, 0:ST - 1], x4[:, :, 1:ST], ALU.subtract)
                dve.tensor_tensor(d4[:, :, 0], last[:, k, :], x4[:, :, 0], ALU.subtract)
                mm = dve.tensor_copy(shT[:, KT:KT + 64].rearrange("p (b k) -> p k b", k=KT)[:, k, :],
                                     x4[:, :, ST - 1])
            mm.then_inc(*O0.dve.done("dx"))
            dve.wait_ge(*O0.dve.at("dx"))
            dve.tensor_scalar(omka, vec[:, 1, VCOL["rw_ka"][1]:VCOL["rw_ka"][1] + KT], -1.0, 1.0, ALU.mult,
                              ALU.add).then_inc(*O0.dve.done("omka"))
            for m, name in ((1, "lw"), (4, "la")):
                for k in range(KT):
                    j = (0 if m == 1 else KT) + k
                    if j >= 2:
                        dve.wait_ge(*O0.pe.at(f"mix{j - 2}"))
                    dve.scalar_tensor_tensor(out=ymix[:, k % 2, :], in0=dx[:, k, :], scalar=col("rw_mu", 8 * m + k),
                                             in1=xn[:, k, :], op0=ALU.mult, op1=ALU.add).then_inc(
                        *O0.dve.done(f"mix{j}"))
            dve.wait_ge(*O0.pe.at("shift"))
            dve.tensor_copy(lioS, ps[0:72, 3, 0:P]).then_inc(*O0.dve.done("shift"))
            for i in range(KT):
                t, u = (t1, t2)[i % 2], (e1, e2)[i % 2]
                dve.wait_ge(*O0.act.at(f"w{i}"))
                dve.tensor_scalar(qr[:, i, :, 0, :], chunked(t), -float(np.exp(-0.5)), None, ALU.mult).then_inc(
                    *O0.dve.done(f"lw{i}"))
                dve.tensor_scalar(t, t, -float(np.exp(-0.5)), None, ALU.mult).then_inc(*O0.dve.done(f"lt{i}"))
                dve.wait_ge(*O0.dve.at(f"lt{i}"))
                dve.tensor_tensor_scan(t, resetO, t, 0.0, ALU.mult, ALU.add).then_inc(*O0.dve.done(f"b{i}"))
                dve.wait_ge(*O0.dve.at(f"b{i}"))
                dve.tensor_copy(qr[:, i, :, 1, :], chunked(t))
                dve.wait_ge(*O0.act.at(f"a{i}"))
                dve.tensor_copy(kb[:, i, :, 0, :], chunked(u)).then_inc(*O0.dve.done(f"a{i}"))

        def pe_mix(pe):
            pe.wait_ge(*O0.dma.at("all"))
            pe.wait_ge(*norm_o.s.act.at("ln"))
            for m, w in enumerate((w1, a1)):
                for k in range(KT):
                    j = m * KT + k
                    pe.wait_ge(*O0.dve.at(f"mix{j}"))
                    for h in range(2):
                        mm = pe.matmul(ps[0:64, 4 + 2 * m + h, 0:TH], w[:, k, :], ymix[:, k % 2, h * TH:(h + 1) * TH],
                                       start=k == 0, stop=k == KT - 1)
                    mm.then_inc(*O0.pe.done(f"mix{j}"))
            for s in range(2):
                pe.wait_ge(bank_free[s], used["rw_r"][s])
            pe.transpose(ps[0:72, 3, 0:P], shT[:, 0:72], ident[:, :]).then_inc(*O0.pe.done("shift"))
            pe.wait_ge(*O0.dve.at("shift"))
            pe.wait_ge(*O0.act.at("la"))
            for i in range(KT):
                b0 = 2 * (i % 2)
                if i >= 2:
                    pe.wait_ge(*O0.act.at(f"a{i - 2}"))
                for w, x, b, name in ((w2, lw_, b0, "w2"), (a2, la_, 4 + b0, "a2")):
                    for h in range(2):
                        mm = pe.matmul(ps[:, b + h, 0:TH], w[:, i * P:(i + 1) * P], x[:, h * TH:(h + 1) * TH],
                                       start=True, stop=True)
                    mm.then_inc(*O0.pe.done(f"{name}{i}"))

        lioS = small[0:72, 4224:4352]

        def pool_shift(pool):
            pool.wait_ge(*O0.dve.at("shift"))
            pool.dma_start(o["shift_prompt"].rearrange("i b (k c) -> (i b k) c", c=P), lioS[0:KT, :]).then_inc(out_sem, 16)
            pool.dma_start(o["shift_sample"].rearrange("i b (k c) -> (i b k) c", c=P), lioS[KT:72, :]).then_inc(
                out_sem, 16)

        mixes = {"rw_r": 0, "rw_k": 2, "rw_g1": 5, "rw_v": 3}
        seq = ["rw_r", "rw_k", "rw_g1", "rw_v"]

        ymixes = [two(ymix[:, 1, :]), raw[:, :, D:D + TH], two(resetO)]

        def mixed(dve, name, k):
            if k >= 3:
                dve.wait_ge(*O1.dve.at(f"{name}l{k - 3}"))
            elif name != seq[0]:
                dve.wait_ge(*O1.dve.at(f"{seq[seq.index(name) - 1]}l{KT - 1}"))
            else:
                dve.wait_ge(*O0.pe.at(f"mix{2 * KT - 1}"))
            dve.scalar_tensor_tensor(out=ymixes[k % 3], in0=two(dx[:, k, :]),
                                     scalar=col("rw_mu", 8 * mixes[name] + k), in1=two(xn[:, k, :]), op0=ALU.mult,
                                     op1=ALU.add).then_inc(*O1.dve.done(f"{name}y{k}"))

        def dve_x(dve, name):
            for k in range(3):
                mixed(dve, name, k)
            for k in range(KT):
                dve.wait_ge(*O1.act.at(f"{name}h{k}"))
                dve.tensor_tensor(two(xl[:, k, :]), ymixes[k % 3], two(xh[:, k, :].bitcast(F32)),
                                  ALU.subtract).then_inc(*O1.dve.done(f"{name}l{k}"))
                if k + 3 < KT:
                    mixed(dve, name, k + 3)

        def act_x(act, name):
            at = seq.index(name)
            if at == 0:
                act.wait_ge(*O0.act.at(f"a{KT - 1}"))
                act.wait_ge(*O0.pe.at(f"a2{KT - 1}"))
                act.wait_ge(out_sem, 16 * 2)
            for k in range(KT):
                if at > 0 and k < KT - 1:
                    act.wait_ge(x_free, (KT - 1) * (at - 1) + k + 1)
                elif at > 0:
                    for s in range(2):
                        act.wait_ge(mm_ok[s], used[name][s])
                act.wait_ge(*O1.dve.at(f"{name}y{k}"))
                act.activation(two(xh[:, k, :]), ymixes[k % 3], ACT.Copy).then_inc(*O1.act.done(f"{name}h{k}"))

        def x_ready(name):
            def ready(pe, k):
                pe.wait_ge(*O1.dve.at(f"{name}l{k}"))
            return ready

        def units_of(name):
            n, units = stages[name]
            return [(i, s, len(units) * i + s, i == n - 1) for i in range(n) for s in range(len(units))]

        def plain(eng_split, name):
            def run(eng):
                for i, s, t, last in units_of(name):
                    eng.wait_ge(mm_ok[s], used[name][s] + i + 1)
                    ahead(eng_split, eng, name, s, i, last)
            return run

        def dve_r(dve):
            for i, s, t, last in units_of("rw_r"):
                if t == KT - 1:
                    dve_x(dve, "rw_k")
                dve.wait_ge(mm_ok[s], used["rw_r"][s] + i + 1)
                ahead(dve_rest, dve, "rw_r", s, i, last)

        def act_r(act):
            for i, s, t, last in units_of("rw_r"):
                if t == KT - 1:
                    act_x(act, "rw_k")
                act.wait_ge(mm_ok[s], used["rw_r"][s] + i + 1)
                ahead(act_head, act, "rw_r", s, i, last)
                act.activation(kb[:, t, 0:8, 1, :], chunked(ps[:, 2 * s, 0:256]), ACT.Copy)
                act.activation(kb[:, t, 8, 1, 0:16], ps[:, 2 * s, 256:272], ACT.Copy)
                act.activation(kb[:, t, 8, 1, 16:32], ps[:, 2 * s + 1, 0:16], ACT.Copy)
                act.activation(kb[:, t, 9:17, 1, :], chunked(ps[:, 2 * s + 1, 16:272]), ACT.Copy).then_inc(
                    bank_free[s], 1)

        def act_k(act):
            for i, s, t, last in units_of("rw_k"):
                if t == KT - 1:
                    act_x(act, "rw_g1")
                act.wait_ge(mm_ok[s], used["rw_k"][s] + i + 1)
                ahead(act_head, act, "rw_k", s, i, last)
                if t == KT - 1:
                    act_g1(act)
                    act_x(act, "rw_v")
                if t > 0:
                    act.wait_ge(*O1.dve.at(f"end{t - 1}"))
                act.activation(two(t1), out2(s), ACT.Copy, scale=col("rw_kk", t))
                act.activation(two(e1), out2(s), ACT.Square, scale=col("rw_kk", t)).then_inc(*O1.act.done(f"sq{t}"))
                act.wait_ge(*O1.dve.at(f"nn{t}"))
                act.activation(e2, e2, ACT.Ln, scale=float(2.0 ** 17)).then_inc(*O1.act.done(f"ln{t}"))
                act.wait_ge(*O1.act.at(f"ln{t}"))
                act.activation(e2, e2, ACT.Exp, scale=-0.5, bias=bias17).then_inc(*O1.act.done(f"rs{t}"))
                act.wait_ge(*O1.dve.at(f"d{t}"))
                act.activation(e1, e1, ACT.Exp).then_inc(*O1.act.done(f"e1{t}"))
                act.wait_ge(*O1.dve.at(f"kn{t}"))
                act.activation(chunked(e2), qr[:, t, :, 1, :], ACT.Exp, scale=-1.0).then_inc(*O1.act.done(f"e2{t}"))
                act.wait_ge(*O1.dve.at(f"kk{t}"))
                act.activation(chunked(e1), qr[:, t, :, 1, :], ACT.Exp).then_inc(*O1.act.done(f"e3{t}"))

        def pe_k(pe):
            for i, s, t, last in units_of("rw_k"):
                unit_products(pe, "rw_k", i, s, x_ready("rw_k") if t == 0 else None, t == KT - 1)
                if t == 0:
                    pe.wait_ge(*O0.act.at(f"a{KT - 1}"))
                else:
                    k_sums(pe, t - 1)
            pe_stage(pe, "rw_g1", x_ready("rw_g1"), freed=True)
            unit_products(pe, "rw_v", 0, 0, x_ready("rw_v"))
            k_sums(pe, KT - 1)
            for i, s, t, last in units_of("rw_v")[1:]:
                unit_products(pe, "rw_v", i, s)

        def k_sums(pe, t):
            pe.wait_ge(*O1.act.at(f"sq{t}"))
            for h in range(2):
                mm = pe.matmul(ps[:, 4 + h, 0:TH], same, e1[:, h * TH:(h + 1) * TH], start=True, stop=True)
            mm.then_inc(*O1.pe.done(f"nn{t}"))
            pe.wait_ge(*O1.dve.at(f"s{t}"))
            for h in range(2):
                mm = pe.matmul(ps[0:HC, 6 + h, 0:TH], hsel[:, t, :], t2s[:, h * TH:(h + 1) * TH], start=t == 0,
                               stop=t == KT - 1)
            mm.then_inc(*O1.pe.done(f"s{t}"))

        t2s = ymix[:, 0, :]

        def dve_k(dve):
            for i, s, t, last in units_of("rw_k"):
                if t == KT - 1:
                    dve_x(dve, "rw_g1")
                dve.wait_ge(mm_ok[s], used["rw_k"][s] + i + 1)
                ahead(dve_rest, dve, "rw_k", s, i, last)
                if t == KT - 1:
                    plain(dve_rest, "rw_g1")(dve)
                    dve_x(dve, "rw_v")
                dve.wait_ge(*O1.pe.at(f"nn{t}"))
                dve.tensor_scalar(two(e2), ps[:, 4:6, 0:TH], 1e-24, None, ALU.max).then_inc(*O1.dve.done(f"nn{t}"))
                dve.tensor_tensor(chunked(e1), qr[:, t, :, 1, :], qr[:, t, :, 0, :], ALU.subtract).then_inc(
                    *O1.dve.done(f"d{t}"))
                dve.tensor_scalar(chunked(t2), kb[:, t, :, 0, :], col("rw_ka", t), omka[:, t:t + 1], ALU.mult,
                                  ALU.add).then_inc(*O1.dve.done(f"f{t}"))
                dve.wait_ge(*O1.dve.at(f"f{t}"))
                dve.tensor_tensor(two(t2), two(t2), out2(s), ALU.mult).then_inc(*O1.dve.done(f"kp{t}"))
                dve.wait_ge(*O1.dve.at(f"kp{t}"))
                dve.wait_ge(*O1.act.at(f"sq{t}"))
                dve.sem_inc(bank_free[s], 1)
                if t > 0:
                    dve.wait_ge(*O1.pe.at(f"s{t - 1}"))
                dve.scalar_tensor_tensor(out=chunked(t2s), in0=chunked(t2), scalar=col("rw_rk", t),
                                         in1=kb[:, t, :, 1, :], op0=ALU.mult, op1=ALU.mult).then_inc(
                    *O1.dve.done(f"s{t}"))
                dve.wait_ge(*O1.act.at(f"rs{t}"))
                dve.tensor_tensor(t1, t1, e2, ALU.mult).then_inc(*O1.dve.done(f"kn{t}"))
                dve.wait_ge(*O1.act.at(f"e1{t}"))
                dve.wait_ge(*O1.dve.at(f"kn{t}"))
                dve.tensor_tensor(qr[:, t, :, 0, :], chunked(t1), chunked(e1), ALU.mult).then_inc(
                    *O1.dve.done(f"kk{t}"))
                dve.tensor_tensor(chunked(t1), chunked(t1), kb[:, t, :, 0, :], ALU.mult).then_inc(
                    *O1.dve.done(f"be{t}"))
                dve.wait_ge(*O1.act.at(f"e3{t}"))
                dve.wait_ge(*O1.dve.at(f"be{t}"))
                dve.tensor_tensor(qr[:, t, :, 1, :], kb[:, t, :, 1, :], chunked(e1), ALU.mult).then_inc(
                    *O1.dve.done(f"r{t}"))
                dve.tensor_copy(wc[:, t // 4, t % 4, 0:16], chunked(e1)[:, 0:16, CO - 1])
                dve.tensor_copy(wc[:, t // 4, t % 4, 16:24], e1[:, TP:T].rearrange("p (b t) -> p b t", t=ST)[:, :, ST - 1])
                dve.tensor_tensor(kb[:, t, :, 0, :], chunked(t2), chunked(e2), ALU.mult)
                dve.wait_ge(*O1.dve.at(f"r{t}"))
                dve.tensor_tensor(kb[:, t, :, 1, :], chunked(t1), chunked(e2), ALU.mult).then_inc(
                    *O1.dve.done(f"end{t}"))
            dve.wait_ge(*O1.pe.at(f"s{KT - 1}"))
            dve.tensor_copy(two(s16), ps[0:HC, 6:8, 0:TH]).then_inc(*O1.dve.done("s16"))

        def act_g1(act):
            for i, s, t, last in units_of("rw_g1"):
                act.wait_ge(mm_ok[s], used["rw_g1"][s] + i + 1)
                ahead(act_head, act, "rw_g1", s, i, last)
                act.activation(two(gs), out2(s), ACT.Sigmoid).then_inc(bank_free[s], 1)

        def dve_v(dve):
            for i, s, t, last in units_of("rw_v"):
                dve.wait_ge(mm_ok[s], used["rw_v"][s] + i + 1)
                ahead(dve_rest, dve, "rw_v", s, i, last)
                if t == 0:
                    dve.wait_ge(*O1.dve.at(f"rw_vl{KT - 1}"))
                dve.tensor_copy(two(vF[:, t, :]), out2(s)).then_inc(bank_free[s], 1)

        odd_parts = [
            dict(scalar=act_mix),
            norm_part(norm_o),
            dict(tensor=pe_mix, scalar=act_mix2, vector=dve_mix, gpsimd=pool_shift),
            dict(tensor=lambda e: pe_stage(e, "rw_r", x_ready("rw_r"), freed=True),
                 scalar=lambda e: (act_x(e, "rw_r"), act_r(e)), vector=lambda e: (dve_x(e, "rw_r"), dve_r(e))),
            dict(tensor=pe_k, scalar=act_k, vector=dve_k),
            dict(scalar=plain(act_head, "rw_v"), vector=dve_v),
        ]

        QUADS = TP // P
        slot_in = [sem("state_in_even"), sem("state_in_odd")]
        slot_out = [sem("state_out_even"), sem("state_out_odd")]
        id32 = mix[:, SC0 + 3072:SC0 + 3072 + CO]
        g2, spread = mix[:, 21760:21760 + D], mix[0:HC, 21760 + D:21760 + 2 * D]
        heads2 = [(g, i) for i in range(KT) for g in range(2)]

        def quad_shape(q):
            return (list(range(4)), P, 2, P) if q < QUADS else ([0], 64, 1, TS)

        def spots(q):
            js, _, ncp, _ = quad_shape(q)
            return [(2 * par + g, cp, g, i) for cp in range(ncp) for i in range(KT) for par in range(min(2, len(js)))
                    for g in range(2)]

        def level_count(q):
            return 5 if q < QUADS else 2

        def blocks(ap, q):
            js, pr, ncp, _ = quad_shape(q)
            return ap[0:pr, 0:256 * ncp].rearrange("p (c t) -> p c t", t=CO)

        def at_block(ap, tile, cp, i):
            c = (cp * KT + i) * CO
            return ap[32 * tile:32 * tile + 32, c:c + CO]

        vus = [vu, mix[:, 21760:23808].rearrange("p (c g i v) -> p c g i v", c=2, g=2, i=KT)]
        scs = [sc, quad[:, 2048:4096].rearrange("p (c g i t) -> p c g i t", c=2, g=2, i=KT)]
        xTs = [xT, mix[:, 23808:24320]]
        kb_by_token = mix[:, 0:8704].rearrange("p (i n c) -> p i n c", i=KT, n=NCO)
        kb_sample = mix[:, 24320:25344].rearrange("p (i g c) -> p i g c", i=KT, g=2)
        read_by = {}

        def key_rows(q, cp, i, g):
            return kb_by_token[:, i, 4 * q + 2 * cp + g, :] if q < QUADS else kb_sample[:, i, g, :]

        def parts_of(q):
            ncp = quad_shape(q)[2]
            parts = [("sc", (cp, g), "dve") for cp in range(ncp) for g in range(2)]
            parts += [("vt", 0, "act"), ("vt", 1, "dve")]
            keys = [("kt", j, "act") for j in range(2 * ncp)]
            for level in range(2, level_count(q) + 1):
                parts.append(("P", level, "act"))
                parts += keys[0:1]
                parts.append(("X", level, "dve"))
                parts += keys[1:2]
                keys = keys[2:]
            if q >= 3:
                parts += [("st", b, "dve" if b % 2 else "act") for b in range(4 * q - 12, 4 * q - 8)]
            if q == QUADS:
                parts.append(("rts", 0, "dve"))
            return [(kind, x, by, k % 2) for k, (kind, x, by) in enumerate(parts)]

        def part_name(q, kind, x):
            return {"sc": lambda: f"sc{q}{x[0]}{x[1]}", "st": lambda: f"st{x}", "rts": lambda: "rts"}.get(
                kind, lambda: f"{kind}{q}{x}")()

        def taken(by, q, kind, x):
            return (O2.act if by == "act" else O2.dve).at(part_name(q, kind, x))

        def pe_prepare(pe, q):
            js, pr, ncp, nt = quad_shape(q)
            if q == 0:
                for s in range(2):
                    pe.wait_ge(bank_free[s], used["rw_o"][s])
                pe.wait_ge(*O1.dve.at("s16"))
            for kind, x, by, bank in parts_of(q):
                if bank in read_by:
                    pe.wait_ge(*read_by[bank]())
                out = ps[:, bank, :]
                if kind == "sc":
                    cp, g = x
                    for par in range(min(2, len(js))):
                        n = 4 * q + 2 * cp + par
                        for i in range(KT):
                            mm = pe.matmul(out[64 * par:64 * par + 64, i * 64:(i + 1) * 64],
                                           kb[64 * g:64 * g + 64, i, n, :, :], qr[64 * g:64 * g + 64, i, n, :, :],
                                           start=True, stop=True)
                elif kind == "vt":
                    for i in range(4):
                        mm = pe.transpose(out[0:nt, i * P:(i + 1) * P], vF[:, 4 * x + i, q * P:q * P + nt], ident[:, :])
                elif kind == "kt":
                    n = 4 * q + 2 * (x // 2)
                    for i in range(4):
                        mm = pe.transpose(out[0:pr, i * P:(i + 1) * P], kb[:, 4 * (x % 2) + i, n:n + (pr // 64), :, :],
                                          ident[:, :])
                elif kind == "P":
                    pe.wait_ge(*O2.dve.at(f"b{q}{x}"))
                    for tile, cp, g, i in spots(q):
                        mm = pe.matmul(at_block(out, tile, cp, i), at_block(bT, tile, cp, i), at_block(xx, tile, cp, i),
                                       start=True, stop=True)
                elif kind == "X":
                    pe.wait_ge(*O2.act.at(f"P{q}{x}"))
                    for tile, cp, g, i in spots(q):
                        mm = pe.matmul(at_block(out, tile, cp, i), at_block(pp, tile, cp, i),
                                       at_block(xTs[q % 2], tile, cp, i), start=True, stop=True)
                elif kind == "st":
                    r = slice(64 * (x % 2), 64 * (x % 2) + 64)
                    pe.wait_ge(slot_in[x % 2], 16 * (x // 2 + 1))
                    for i in range(KT):
                        mm = pe.transpose(out[:, i * NC:(i + 1) * NC], lio[r, i * P:(i + 1) * P], ident[r, r])
                else:
                    pe.wait_ge(*O2.act.at("st6"))
                    pe.wait_ge(*O2.dve.at("st7"))
                    for b in range(NB):
                        for i in range(KT):
                            for g in range(2):
                                r = slice(64 * g, 64 * g + 64)
                                o2 = out[r, i * 64:(i + 1) * 64].rearrange("p (s t) -> p s t", s=2)
                                mm = pe.matmul(o2[:, :, b * ST:(b + 1) * ST], hs[r, i, b, :],
                                               qr[r, i, NCO - 1, :, b * ST:(b + 1) * ST], start=True, stop=True)
                mm.then_inc(*O2.pe.done(part_name(q, kind, x)))
                read_by[bank] = lambda by=by, q=q, kind=kind, x=x: taken(by, q, kind, x)
                yield

        def act_prepare(act, q):
            js, pr, ncp, nt = quad_shape(q)
            for kind, x, by, bank in parts_of(q):
                if by == "act":
                    name = part_name(q, kind, x)
                    act.wait_ge(*O2.pe.at(name))
                    if kind == "vt":
                        for j in js:
                            act.activation(
                                vus[q % 2][64 * (j % 2):64 * (j % 2) + 32, j // 2, :, 0:4, :].rearrange("p g i v -> p i g v"),
                                ps[32 * j:32 * j + 32, bank, :].rearrange("p (i g v) -> p i g v", i=4, g=2),
                                ACT.Copy).then_inc(*O2.act.done(name if j == js[-1] else f"vt{q}_{j}"))
                    elif kind == "kt":
                        half = slice(4 * (x % 2), 4 * (x % 2) + 4)
                        n = 4 * q + 2 * (x // 2)
                        dst = kb_by_token[0:pr, half, n:n + 2, :] if q < QUADS else kb_sample[0:pr, half, :, :]
                        act.activation(dst, ps[0:pr, bank, :].rearrange("p (i g c) -> p i g c", i=4, g=2),
                                       ACT.Copy).then_inc(*O2.act.done(name))
                    elif kind == "P":
                        act.activation(pp[0:pr, 0:256 * ncp], ps[0:pr, bank, 0:256 * ncp], ACT.Copy).then_inc(
                            *O2.act.done(name))
                    else:
                        act.activation(hs[:, :, x, :], ps[:, bank, :].rearrange("p (i v) -> p i v", i=KT),
                                       ACT.Copy).then_inc(*O2.act.done(name))
                yield

        def dve_prepare(dve, q):
            js, pr, ncp, nt = quad_shape(q)
            nb = 8 * ncp
            xTq = xTs[q % 2]

            def halving(level):
                return lvO[0:pr, level - 1, :].unsqueeze(1).to_broadcast([pr, nb, CO])

            if q == 0:
                for k in range(4):
                    r = slice(32 * k, 32 * k + 32)
                    mm = dve.tensor_copy(id32[r, :], ident[r, r])
                mm.then_inc(*O2.dve.done("id32"))
                dve.wait_ge(*O2.dve.at("id32"))
            for kind, x, by, bank in parts_of(q):
                if by == "dve":
                    name = part_name(q, kind, x)
                    dve.wait_ge(*O2.pe.at(name))
                    if kind == "sc":
                        dve.tensor_tensor(scs[q % 2][0:pr, x[0], x[1], :, :],
                                          ps[0:pr, bank, :].rearrange("p (i t) -> p i t", i=KT),
                                          scm[0:pr, q // QUADS, :].unsqueeze(1).to_broadcast([pr, KT, 64]),
                                          ALU.mult).then_inc(*O2.dve.done(name))
                        if x == (ncp - 1, 1):
                            dve.wait_ge(*O2.dve.at(name))
                            for par in range(min(2, len(js))):
                                for g in range(2):
                                    k = 2 * par + g
                                    mm = dve.tensor_copy(
                                        aT[32 * k:32 * k + 32, 0:256 * ncp].rearrange("p (c i t) -> p c i t", c=ncp, i=KT),
                                        scs[q % 2][64 * par + 32:64 * par + 64, 0:ncp, g, :, 0:CO])
                            mm.then_inc(*O2.dve.done(f"aT{q}"))
                            dve.wait_ge(*O2.dve.at(f"aT{q}"))
                            dve.tensor_tensor(blocks(bT, q), blocks(aT, q), halving(1), ALU.mult).then_inc(
                                *O2.dve.done(f"b{q}1"))
                            dve.wait_ge(*O2.dve.at(f"b{q}1"))
                            dve.tensor_tensor(blocks(xTq, q), id32[0:pr].unsqueeze(1).to_broadcast([pr, nb, CO]),
                                              blocks(bT, q), ALU.subtract).then_inc(*O2.dve.done(f"X{q}1"))
                            next_level(dve, q, 2)
                    elif kind == "vt":
                        for j in js:
                            dve.tensor_copy(
                                vus[q % 2][64 * (j % 2):64 * (j % 2) + 32, j // 2, :, 4:8, :].rearrange("p g i v -> p i g v"),
                                ps[32 * j:32 * j + 32, bank, :].rearrange("p (i g v) -> p i g v", i=4, g=2)).then_inc(
                                *O2.dve.done(name if j == js[-1] else f"vt{q}_{j}"))
                    elif kind == "X":
                        dve.tensor_tensor(xTq[0:pr, 0:32 * nb], xTq[0:pr, 0:32 * nb], ps[0:pr, bank, 0:32 * nb],
                                          ALU.subtract).then_inc(*O2.dve.done(name))
                        if x < level_count(q):
                            next_level(dve, q, x + 1)
                    elif kind == "st":
                        dve.tensor_copy(hs[:, :, x, :], ps[:, bank, :].rearrange("p (i v) -> p i v", i=KT)).then_inc(
                            *O2.dve.done(name))
                    else:
                        dve.tensor_copy(rts, ps[:, bank, :].rearrange("p (i s t) -> p i s t", i=KT, s=2)).then_inc(
                            *O2.dve.done(name))
                yield

        def next_level(dve, q, level):
            _, pr, ncp, _ = quad_shape(q)
            dve.wait_ge(*O2.dve.at(f"X{q}{level - 1}"))
            dve.transpose(xx[0:pr, 0:256 * ncp], xTs[q % 2][0:pr, 0:256 * ncp])
            dve.tensor_tensor(blocks(bT, q), blocks(aT, q),
                              lvO[0:pr, level - 1, :].unsqueeze(1).to_broadcast([pr, 8 * ncp, CO]), ALU.mult).then_inc(
                *O2.dve.done(f"b{q}{level}"))

        def go_on(preparation, n):
            for _ in range(n):
                next(preparation, None)

        def pe_chunk(pe, q, j, preparation):
            n, cp, par = 4 * q + j, j // 2, j % 2
            vu, sc, xT = vus[q % 2], scs[q % 2], xTs[q % 2]
            if j == 0:
                pe.wait_ge(*O2.act.at(f"kt{q}{2 * quad_shape(q)[2] - 1}"))
                pe.wait_ge(*O2.dve.at(f"X{q}{level_count(q)}"))
                pe.wait_ge(*O2.dve.at(f"vt{q}1"))
            rb, sample = 64 * par, q == QUADS
            for g in range(2):
                for i in range(KT):
                    mm = pe.matmul(ps[rb + 32 * g:rb + 32 * g + 32, 2 + g, i * NC:(i + 1) * NC],
                                   sc[rb:rb + 32, cp, g, i, 0:CO], vu[rb:rb + 32, cp, g, i, :],
                                   start=i == 0, stop=False, skip_group_check=True)
            mm.then_inc(*O2.pe.done(f"av{n}" if n else "R0"))
            if sample:
                pe.wait_ge(*O2.dve.at("rts"))
            if n > 0:
                pe.wait_ge(*O2.dve.at(f"H{n - 1}"))
                pe.wait_ge(*O2.act.at(f"o{n - 1}"))
            if n > 0:
                pe.wait_ge(*O2.pe.at(f"av{n}"))
                for g in range(2):
                    r = slice(64 * g, 64 * g + 64)
                    for i in range(KT):
                        w = rts[r, i, 0, :] if sample else qr[r, i, n, 0, :]
                        x = ident[r, r] if sample else hst[r, i, :]
                        mm = pe.matmul(ps[rb + 32 * g:rb + 32 * g + 32, 2 + g, i * NC:(i + 1) * NC], w, x, start=False,
                                       stop=True, skip_group_check=True)
                mm.then_inc(*O2.pe.done(f"R{n}"))
                for g in range(2):
                    r = slice(64 * g, 64 * g + 64)
                    for i in range(KT):
                        w = ident[r, r] if sample else hst[r, i, :]
                        x = rts[r, i, 1, :] if sample else qr[r, i, n, 1, :]
                        pe.matmul(ps[r, 6, i * CO:(i + 1) * CO], w, x, start=i == 0, stop=False, skip_group_check=True)
            go_on(preparation, 2)
            pe.wait_ge(*O2.act.at(f"R{n}"))
            pe.wait_ge(*O2.dve.at(f"R{n}"))
            for i in range(KT):
                for g in range(2):
                    rows_g = slice(rb + 32 * g, rb + 32 * g + 32)
                    mm = pe.matmul(ps[rb + 32:rb + 64, 4 + g, i * NC:(i + 1) * NC], at_block(xT, 2 * par + g, cp, i),
                                   rb_[rows_g, g, i, :], start=True, stop=True)
            mm.then_inc(*O2.pe.done(f"U{n}"))
            go_on(preparation, 1)
            pe.wait_ge(*O2.act.at(f"U{n}"))
            pe.wait_ge(*O2.dve.at(f"U{n}"))
            r = slice(rb, rb + 64)
            if not sample:
                for i in range(KT):
                    for g in range(2):
                        mm = pe.matmul(ps[64 * g:64 * g + 64, 7, i * NC:(i + 1) * NC],
                                       key_rows(q, cp, i, g)[r], vu[r, cp, g, i, :], start=True, stop=True)
                mm.then_inc(*O2.pe.done(f"H{n}"))
            for i in range(KT):
                for g in range(2):
                    mm = pe.matmul(ps[64 * g:64 * g + 64, 6, i * CO:(i + 1) * CO], vu[r, cp, g, i, :],
                                   sc[r, cp, g, i, CO:2 * CO], start=n == 0 and i == 0, stop=True,
                                   skip_group_check=True)
            mm.then_inc(*O2.pe.done(f"o{n}"))
            go_on(preparation, 2)

        def act_chunks_odd(act, q, preparation):
            vu = vus[q % 2]
            for j in quad_shape(q)[0]:
                n, rb, cp = 4 * q + j, 64 * (j % 2), j // 2
                act.wait_ge(*O2.pe.at(f"R{n}"))
                act.activation(rb_[rb:rb + 32, 0, :, :], ps[rb:rb + 32, 2, :].rearrange("p (i v) -> p i v", i=KT),
                               ACT.Copy).then_inc(*O2.act.done(f"R{n}"))
                go_on(preparation, 2)
                act.wait_ge(*O2.pe.at(f"U{n}"))
                act.activation(vu[rb + 32:rb + 64, cp, 0, :, :],
                               ps[rb + 32:rb + 64, 4, :].rearrange("p (i v) -> p i v", i=KT), ACT.Copy,
                               scale=-1.0).then_inc(*O2.act.done(f"U{n}"))
                go_on(preparation, 1)
                act.wait_ge(*O2.pe.at(f"o{n}"))
                act.activation(qr[:, :, n, 0, :], ps[:, 6, 0:256].rearrange("p (i t) -> p i t", i=KT),
                               ACT.Copy).then_inc(*O2.act.done(f"o{n}"))
                go_on(preparation, 2)

        def dve_chunks_odd(dve, q, preparation):
            vu = vus[q % 2]
            for j in quad_shape(q)[0]:
                n, rb, cp = 4 * q + j, 64 * (j % 2), j // 2
                dve.wait_ge(*O2.pe.at(f"R{n}"))
                dve.tensor_copy(rb_[rb + 32:rb + 64, 1, :, :],
                                ps[rb + 32:rb + 64, 3, :].rearrange("p (i v) -> p i v", i=KT)).then_inc(
                    *O2.dve.done(f"R{n}"))
                go_on(preparation, 2)
                dve.wait_ge(*O2.pe.at(f"U{n}"))
                dve.tensor_scalar(vu[rb + 32:rb + 64, cp, 1, :, :],
                                  ps[rb + 32:rb + 64, 5, :].rearrange("p (i v) -> p i v", i=KT), -1.0, None,
                                  ALU.mult).then_inc(*O2.dve.done(f"U{n}"))
                go_on(preparation, 1)
                if q == QUADS:
                    continue
                dve.wait_ge(*O2.pe.at(f"H{n}"))
                total = ps[:, 7, :].rearrange("p (i v) -> p i v", i=KT)
                if n > 0:
                    dve.tensor_tensor(hst, hst, total, ALU.add).then_inc(*O2.dve.done(f"h{n}"))
                    dve.wait_ge(*O2.dve.at(f"h{n}"))
                    total = hst
                by4 = lambda ap: ap.rearrange("p (s i) v -> p s i v", s=2)
                dve.tensor_tensor(by4(hst), by4(total), wc[:, :, :, n:n + 1].to_broadcast([P, 2, 4, NC]), ALU.mult).then_inc(
                    *O2.dve.done(f"H{n}"))
                go_on(preparation, 2)

        def pool_states(pool):
            pool.wait_ge(*O1.dve.at("s16"))
            for b in range(NB):
                if b >= 2:
                    pool.wait_ge(*O2.pe.at(f"st{b - 2}"))
                pool.dma_start(lio[64 * (b % 2):64 * (b % 2) + 64, :].rearrange("p (h k) -> p h k", h=HC),
                               a["state_rwkv"][0, b].rearrange("h v k -> v h k")).then_inc(slot_in[b % 2], 16)

        def pe_new_states(pe):
            for k, (g, i) in enumerate(heads2):
                bank = i % 2
                pe.wait_ge(*O2.dve.at(f"vx{k}"))
                if k >= 4 and g == 0:
                    pe.wait_ge(*O2.dve.at(f"ns{i - 2}"))
                pe.matmul(ps[64 * g:64 * g + 64, bank, :], kb_sample[0:64, i, g, :],
                          vux2[k % 2], start=True, stop=True).then_inc(*O2.pe.done(f"ns{k}"))
            for b in range(NB + 1):
                b0 = 2 + 2 * (b % 2)
                if b == 0:
                    pe.wait_ge(*O2.dve.at(f"ns{KT - 1}"))
                elif b >= 2:
                    pe.wait_ge(*O2.act.at(f"so{b - 2}"))
                    pe.wait_ge(*O2.dve.at(f"so{b - 2}"))
                for i in range(KT):
                    src = hs[:, i, b, :] if b < NB else hst[:, i, :]
                    mm = pe.transpose(ps[0:64, b0 + i // 4, (i % 4) * P:(i % 4 + 1) * P], src, ident[:, :])
                mm.then_inc(*O2.pe.done(f"so{b}"))

        vux2 = [quad[0:64, 5120 + 512 * k:5632 + 512 * k] for k in range(2)]

        def dve_new_states(dve):
            dve.wait_ge(*O2.act.at(f"U{4 * QUADS}"))
            dve.wait_ge(*O2.dve.at(f"U{4 * QUADS}"))
            for k, (g, i) in enumerate(heads2):
                if k >= 2:
                    dve.wait_ge(*O2.pe.at(f"ns{k - 2}"))
                dve.tensor_tensor(vux2[k % 2].rearrange("p (b v) -> p b v", b=NB),
                                  vu[0:64, 0, g, i, :].unsqueeze(1).to_broadcast([64, NB, NC]),
                                  batO[0:64, :].unsqueeze(2).to_broadcast([64, NB, NC]), ALU.mult).then_inc(
                    *O2.dve.done(f"vx{k}"))
                if k % 2 == 0 and i > 0:
                    new_state(dve, i - 1)
            new_state(dve, KT - 1)
            dve.wait_ge(*O2.dve.at(f"ns{KT - 1}"))
            for b in range(NB + 1):
                state_rows(dve, O2.dve, b)

        def new_state(dve, i):
            dve.wait_ge(*O2.pe.at(f"ns{2 * i + 1}"))
            h = hs[:, i, :, :]
            dve.tensor_tensor(h, h, ps[:, i % 2, :].rearrange("p (b v) -> p b v", b=NB), ALU.add).then_inc(
                *O2.dve.done(f"na{i}"))
            dve.wait_ge(*O2.dve.at(f"na{i}"))
            dve.tensor_tensor(h, h, wc[:, i // 4, i % 4, 16:24].unsqueeze(2).to_broadcast([P, NB, NC]), ALU.mult).then_inc(
                *O2.dve.done(f"ns{i}"))

        def state_rows(eng, signal, b):
            half = 0 if signal is O2.act else 1
            eng.wait_ge(*O2.pe.at(f"so{b}"))
            if b >= 2:
                eng.wait_ge(slot_out[b % 2], 16 * (b // 2))
            elif half == 0:
                eng.wait_ge(*O2.pe.at(f"st{NB - 2 + b}"))
            dst = lio[64 * (b % 2):64 * (b % 2) + 64, half * 512:half * 512 + 512]
            src = ps[0:64, 2 + 2 * (b % 2) + half, :]
            if half == 0:
                eng.activation(dst, src, ACT.Copy).then_inc(*signal.done(f"so{b}"))
            else:
                eng.tensor_copy(dst, src).then_inc(*signal.done(f"so{b}"))

        def pool_out(pool):
            pool.wait_ge(*O2.pe.at(f"o{4 * QUADS - 1}"))
            pool.dma_start(g2, a["rw_g2"][0]).then_inc(*O3.dma.loaded("g2"))
            pool.dma_start(spread, a["head_spread"]).then_inc(*O3.dma.loaded("all"))
            for b in range(NB + 1):
                pool.wait_ge(*O2.act.at(f"so{b}"))
                pool.wait_ge(*O2.dve.at(f"so{b}"))
                dst = o["rwkv_sample"][0, b] if b < NB else o["rwkv_prompt"][0, 0]
                pool.dma_start(dst.rearrange("h v k -> v h k"),
                               lio[64 * (b % 2):64 * (b % 2) + 64, :].rearrange("p (h k) -> p h k", h=HC)).then_inc(
                    slot_out[b % 2], 16)

        ot, xc, sqo, rso, bo = (cols(2 * D + 2 * T * i, 2, T) for i in range(5))

        gate_w = nc.alloc_sbuf_tensor_at("gate_w_split", [P, 2, D], F32R, offset=mix_byte)
        spread_r = nc.alloc_sbuf_tensor_at("head_spread_r", [P, D], F32R, offset=mix_byte + 4 * 7488)
        gate_x = nc.alloc_sbuf_tensor_at("gate_x_split", [P, 4, T], F32R, offset=mix_byte + 4 * 23808)
        gsh, gsl, s16h, s16l = gate_x[:, 0, :], gate_x[:, 1, :], gate_x[0:HC, 2, :], gate_x[0:HC, 3, :]

        def act_ogate(act):
            act.wait_ge(*O2.pe.at(f"so{NB}"))
            act.wait_ge(*O2.act.at(f"o{4 * QUADS}"))

            def outputs(i):
                if i >= 2:
                    act.wait_ge(*O3.dve.at(f"xc{i - 2}"))
                act.activation(chunked(ot[:, i % 2, :]), qr[:, i, :, 0, :], ACT.Copy).then_inc(*O3.act.done(f"o{i}"))

            outputs(0)
            act.wait_ge(*O3.dma.at("all"))
            act.wait_ge(*O1.dve.at("s16"))
            act.activation(s16h, s16, ACT.Copy)
            act.activation(spread_r[0:HC, :], spread, ACT.Copy)
            act.activation(gsh, gs, ACT.Copy)
            act.activation(gate_w[:, 0, :], g2, ACT.Copy).then_inc(*O3.act.done("heads"))
            for i in range(-1, KT):
                if i + 1 < KT:
                    act.wait_ge(*O3.dve.at(f"xc{i + 1}"))
                    act.activation(sqo[:, (i + 1) % 2, :], xc[:, (i + 1) % 2, :], ACT.Square).then_inc(
                        *O3.act.done(f"sq{i + 1}"))
                    if i + 2 < KT:
                        outputs(i + 2)
                    rs = rso[:, (i + 1) % 2, :]
                    act.wait_ge(*O3.pe.at(f"var{i + 1}"))
                    act.activation(two(rs), ps[:, 6:8, 0:TH], ACT.Ln, bias=eps_gn, scale=1.0 / NC).then_inc(
                        *O3.act.done(f"ln{i + 1}"))
                    act.wait_ge(*O3.act.at(f"ln{i + 1}"))
                    act.activation(rs, rs, ACT.Exp, scale=-0.5).then_inc(*O3.act.done(f"rs{i + 1}"))
                if i >= 0:
                    gated_head(act, i)

        def gated_head(act, k):
            act.wait_ge(*O3.dve.at(f"y{k}"))
            act.activation(xh[:, k, :], bo[:, k % 2, :], ACT.Copy).then_inc(*O3.act.done(f"h{k}"))

        def pe_ogate(pe):
            pe.wait_ge(*O2.act.at(f"so{NB}"))
            pe.wait_ge(*O2.dve.at(f"so{NB}"))

            def mean(i):
                pe.wait_ge(*O3.act.at(f"o{i}"))
                if i > 0:
                    pe.wait_ge(*O3.dve.at(f"xc{i - 1}"))
                for h in range(2):
                    mm = pe.matmul(ps[:, 4 + h, 0:TH], same, ot[:, i % 2, h * TH:(h + 1) * TH], start=True, stop=True)
                mm.then_inc(*O3.pe.done(f"mean{i}"))

            def variance(i):
                pe.wait_ge(*O3.act.at(f"sq{i}"))
                if i > 0:
                    pe.wait_ge(*O3.act.at(f"ln{i - 1}"))
                for h in range(2):
                    mm = pe.matmul(ps[:, 6 + h, 0:TH], same, sqo[:, i % 2, h * TH:(h + 1) * TH], start=True, stop=True)
                mm.then_inc(*O3.pe.done(f"var{i}"))

            mean(0)
            variance(0)
            for i in range(KT):
                if i == 0:
                    pe.wait_ge(*O3.act.at("heads"))
                    pe.wait_ge(*O3.dve.at("rests"))
                else:
                    pe.wait_ge(*O3.dve.at(f"y{i - 1}"))
                tile = slice(i * P, (i + 1) * P)
                for h in range(2):
                    half = slice(h * TH, (h + 1) * TH)
                    pe.matmul(ps[:, h, 0:TH], spread_r[0:HC, tile], s16h[:, half], start=True, stop=False)
                    pe.matmul(ps[:, h, 0:TH], spread_r[0:HC, tile], s16l[:, half], start=False, stop=True)
                for h in range(2):
                    half = slice(h * TH, (h + 1) * TH)
                    pe.matmul(ps[:, 2 + h, 0:TH], gate_w[:, 0, tile], gsh[:, half], start=True, stop=False)
                    pe.matmul(ps[:, 2 + h, 0:TH], gate_w[:, 0, tile], gsl[:, half], start=False, stop=False)
                    mm = pe.matmul(ps[:, 2 + h, 0:TH], gate_w[:, 1, tile], gsh[:, half], start=False, stop=True)
                mm.then_inc(*O3.pe.done(f"g{i}"))
                if i + 1 < KT:
                    mean(i + 1)
                    variance(i + 1)

        def dve_ogate(dve):
            dve.wait_ge(*O3.act.at("heads"))
            dve.tensor_tensor(s16l, s16, s16h.bitcast(F32), ALU.subtract)
            dve.tensor_tensor(gsl, gs, gsh.bitcast(F32), ALU.subtract)
            dve.tensor_tensor(gate_w[:, 1, :], g2, gate_w[:, 0, :].bitcast(F32), ALU.subtract).then_inc(
                *O3.dve.done("rests"))

            def centred(i):
                dve.wait_ge(*O3.pe.at(f"mean{i}"))
                if i >= 2:
                    dve.wait_ge(*O3.dve.at(f"on{i - 2}"))
                    dve.wait_ge(*O3.act.at(f"sq{i - 2}"))
                dve.scalar_tensor_tensor(out=two(xc[:, i % 2, :]), in0=ps[:, 4:6, 0:TH], scalar=-1.0 / NC,
                                         in1=two(ot[:, i % 2, :]), op0=ALU.mult, op1=ALU.add).then_inc(
                    *O3.dve.done(f"xc{i}"))

            centred(0)
            for i in range(KT):
                y, x = bo[:, i % 2, :], xc[:, i % 2, :]
                dve.wait_ge(*O3.pe.at(f"g{i}"))
                if i >= 2:
                    dve.wait_ge(*O3.dve.at(f"l{i - 2}"))
                dve.tensor_tensor(two(y), ps[:, 0:2, 0:TH], two(vF[:, i, :]), ALU.mult).then_inc(
                    *O3.dve.done(f"bo{i}"))
                if i + 1 < KT:
                    centred(i + 1)
                if i > 0:
                    gated_rest(dve, i - 1)
                dve.wait_ge(*O3.act.at(f"rs{i}"))
                dve.scalar_tensor_tensor(out=x, in0=x, scalar=col("rw_lnw", i), in1=rso[:, i % 2, :], op0=ALU.mult,
                                         op1=ALU.mult).then_inc(*O3.dve.done(f"n{i}"))
                dve.wait_ge(*O3.dve.at(f"n{i}"))
                dve.scalar_tensor_tensor(out=y, in0=x, scalar=col("rw_lnb", i), in1=y, op0=ALU.add,
                                         op1=ALU.add).then_inc(*O3.dve.done(f"on{i}"))
                dve.wait_ge(*O3.dve.at(f"on{i}"))
                dve.tensor_tensor(two(y), two(y), ps[:, 2:4, 0:TH], ALU.mult).then_inc(*O3.dve.done(f"y{i}"))
            gated_rest(dve, KT - 1)

        def gated_rest(dve, k):
            dve.wait_ge(*O3.act.at(f"h{k}"))
            dve.tensor_tensor(xl[:, k, :], bo[:, k % 2, :], xh[:, k, :].bitcast(F32), ALU.subtract).then_inc(
                *O3.dve.done(f"l{k}"))

        def o_ready(pe, k):
            if k == 0:
                pe.wait_ge(*O3.dve.at(f"y{KT - 1}"))
            pe.wait_ge(*O3.dve.at(f"l{k}"))

        out_odd = add_stage("rw_o", o_ready, norm_f1)

        def states_out(eng):
            eng.wait_ge(slot_out[0], 16 * (NB // 2 + 1))
            eng.wait_ge(slot_out[1], 16 * (NB // 2))

        odd_late = [dict(gpsimd=pool_states)]

        def all_quads(eng, prepare, chunks):
            go_on(prepare(eng, 0), len(parts_of(0)))
            for q in range(QUADS + 1):
                preparation = prepare(eng, q + 1) if q < QUADS else iter(())
                chunks(eng, q, preparation)
                go_on(preparation, len(parts_of(QUADS - 1)))

        def pe_chunks_odd(pe, q, preparation):
            for j in quad_shape(q)[0]:
                pe_chunk(pe, q, j, preparation)

        odd_late += [dict(tensor=lambda e: all_quads(e, pe_prepare, pe_chunks_odd),
                          scalar=lambda e: all_quads(e, act_prepare, act_chunks_odd),
                          vector=lambda e: all_quads(e, dve_prepare, dve_chunks_odd))]
        odd_late += [
            dict(tensor=pe_new_states, scalar=lambda e: [state_rows(e, O2.act, b) for b in range(NB + 1)],
                 vector=dve_new_states, gpsimd=pool_out),
            dict(tensor=pe_ogate, scalar=act_ogate, vector=dve_ogate),
            dict(tensor=out_odd[0], scalar=lambda e: (out_odd[1](e), states_out(e)), vector=out_odd[2]),
        ]
        OUTS = 2 + 5

        tail_parts = [tail_of(0), tail_of(1)]

        todo = [
            dict(sync=lambda e: [sp_stage(e, n) for n in order[:order.index("rw_r")]]),
            dict(vector=first_counts),
            dict(tensor=pe_embed, scalar=act_embed, vector=dve_embed),
            dict(scalar=lambda e: [act_head(e, "v_a", s, 0) for s in range(2)],
                 vector=lambda e: [dve_rest(e, "v_a", s, 0) for s in range(2)]),
            norm_part(norm0),
            dict(tensor=pe_even_in, scalar=act_even_in, vector=dve_even_in),
            dict(tensor=pe_scores, scalar=act_scores, vector=dve_scores, gpsimd=pool_scores),
            dict(tensor=pe_chunks, scalar=act_chunks, vector=dve_chunks, gpsimd=pool_chunks),
            dict(tensor=pe_gate, scalar=act_gate, vector=dve_gate),
            dict(tensor=out_even[0], scalar=out_even[1], vector=out_even[2]),
            dict(scalar=act_hgrn_out),
        ] + tail_parts[0] + [
            dict(sync=lambda e: [sp_stage(e, n) for n in order[order.index("rw_r"):order.index("rw_o") + 1]]),
        ] + odd_parts + odd_late + [
            dict(sync=lambda e: [sp_stage(e, n) for n in order[order.index("rw_o") + 1:]]),
        ] + tail_parts[1] + [
            norm_part(norm_y), dict(tensor=pe_final, scalar=act_final, gpsimd=pool_final),
        ]
        todo = todo[:stop]
        with nc.Block() as block:
            @block.sync
            def _(sp):
                for part in todo:
                    if "sync" in part:
                        part["sync"](sp)

            @block.tensor
            def _(pe):
                for part in todo:
                    if "tensor" in part:
                        part["tensor"](pe)

            @block.scalar
            def _(act):
                for part in todo:
                    if "scalar" in part:
                        part["scalar"](act)

            @block.vector
            def _(dve):
                for part in todo:
                    if "vector" in part:
                        part["vector"](dve)

            @block.gpsimd
            def _(pool):
                for part in todo:
                    if "gpsimd" in part:
                        part["gpsimd"](pool)


_INS = ["x_prompt", "x_sample", "p_prompt", "p_sample", "state_gla", "state_hgrn", "state_rwkv", "state_shift",
        "norm_mix", "norm_ffn", "norm_ple", "norm_final", "w_in_even", "w_gk2", "b_gk", "gla_norm", "hgrn_gamma",
        "hgrn_norm", "w_out_even", "rw_mu", "rw_wr", "rw_wk", "rw_wv", "rw_wo", "rw_w0", "rw_w1", "rw_w2", "rw_a0",
        "rw_a1", "rw_a2", "rw_g1", "rw_g2", "rw_kk", "rw_ka", "rw_rk", "rw_lnw", "rw_lnb", "w_ffn_gate", "w_ffn_up",
        "w_ffn_down", "w_ple", "w_ple_gate"]
_OUTS = [("y_prompt", (1, TP, D)), ("y_sample", (NB, ST, D)), ("gla_prompt", (1, 1, HA, DKA, DV)),
         ("hgrn_prompt", (1, 1, HB, NBK, DV)), ("rwkv_prompt", (1, 1, HC, NC, NC)), ("shift_prompt", (1, 1, D)),
         ("gla_sample", (1, NB, HA, DKA, DV)), ("hgrn_sample", (1, NB, HB, NBK, DV)),
         ("rwkv_sample", (1, NB, HC, NC, NC)), ("shift_sample", (1, NB, D))]


def _constants():
    return {"ident": np.concatenate([np.eye(P), np.ones((P, P))], 1).astype(np.float32),
            "even_tables": even_tables(), "odd_tables": odd_tables(), "head_spread": head_spread()}


def build(new_core, shapes, stop=99):
    known = None
    for _ in range(2):
        nc, seen = new_core(), {}
        a = {n: nc.dram_tensor(f"in_{n}", s, F32, kind="ExternalInput").ap() for n, s in shapes.items()}
        o = {n: nc.dram_tensor(f"out_{n}", s, F32, kind="ExternalOutput").ap() for n, s in _OUTS}
        trunk(nc, a, o, known, seen, stop)
        known = seen
    return nc


def kernel(**inputs):
    import concourse.bacc as bacc
    from concourse.bass_utils import run_bass_kernel_spmd

    arrays = {n: np.ascontiguousarray(inputs[n]) for n in _INS}
    arrays.update(_constants())
    nc = build(lambda: bacc.Bacc("TRN2", target_bir_lowering=False, num_devices=1),
               {n: x.shape for n, x in arrays.items()})
    r = run_bass_kernel_spmd(nc, [{f"in_{n}": x for n, x in arrays.items()}], core_ids=[0])
    return tuple(r.results[0][f"out_{n}"] for n, _ in _OUTS)
```
